# Optimizing a Trainium2 kernel written in Bass

```python
import jax, jax.numpy as jnp
from jax import lax
import numpy as np

D_MODEL = 1024
BATCH = 1
SEQ = 512
DEPTH = 2
DEC_BATCH = 8
DEC_SEQ = 1
PAST_LEN = 4096
PAGE_SIZE = 128

DN_HEADS = 4
DN_DK = 128
DN_DV = 128
CONV_W = 4
DN_CHUNK = 64
ATT_HEADS = 8
KV_HEADS = 2
HEAD_DIM = 64
IDX_HEADS = 4
IDX_DIM = 64
TOPK_MAX = 256
ROPE_THETA = 500000.0
ROT_FRACTION = 4
Q_BLOCK = 128
MEM_LEN = 256
MEM_HEADS = 4
MEM_HEAD_DIM = 128
N_KEYS = 128
N_EXPERTS = N_KEYS * N_KEYS
PEER_HEADS = 8
PEER_QDIM = 256
PEER_TOPK = 16
PEER_BLOCK = 128
NORM_EPS = 1e-6

DN_QK_W = DN_HEADS * DN_DK
DN_V_W = DN_HEADS * DN_DV
CONV_DIM = 2 * DN_QK_W + DN_V_W
ATT_Q_W = ATT_HEADS * HEAD_DIM
ATT_KV_W = KV_HEADS * HEAD_DIM
IDX_Q_W = IDX_HEADS * IDX_DIM
MEM_W = MEM_HEADS * MEM_HEAD_DIM
IN_SPLITS = (CONV_DIM, DN_V_W, DN_HEADS, DN_HEADS, ATT_Q_W, ATT_KV_W, ATT_KV_W, IDX_Q_W, IDX_DIM, IDX_HEADS, D_MODEL, D_MODEL)
N_IN = CONV_DIM + DN_V_W + 2 * DN_HEADS + ATT_Q_W + 2 * ATT_KV_W + IDX_Q_W + IDX_DIM + IDX_HEADS + 2 * D_MODEL
F32 = jnp.float32

kernel_name = 'hybrid_deltanet_dsa_peer_decoder_step'

def rms_norm(x, g):
    xf = x.astype(F32)
    y = xf * lax.rsqrt(jnp.mean(xf * xf, axis=-1, keepdims=True) + NORM_EPS)
    return (y * g.astype(F32)).astype(x.dtype)

def l2_normalize(x):
    return x * lax.rsqrt(jnp.sum(x * x, axis=-1, keepdims=True) + NORM_EPS)

def rope_partial(x, pos):
    rot = x.shape[-1] // ROT_FRACTION
    half = rot // 2
    inv_freq = ROPE_THETA ** (-jnp.arange(half, dtype=F32) / half)
    ang = pos.astype(F32)[:, None] * inv_freq[None, :]
    cos = jnp.cos(ang)[:, None, :]
    sin = jnp.sin(ang)[:, None, :]
    xr = x[..., :rot].astype(F32)
    x1, x2 = xr[..., :half], xr[..., half:]
    rotated = jnp.concatenate([x1 * cos - x2 * sin, x2 * cos + x1 * sin], axis=-1)
    return jnp.concatenate([rotated.astype(x.dtype), x[..., rot:]], axis=-1)

def split_columns(z):
    offsets = np.cumsum(IN_SPLITS)[:-1].tolist()
    return jnp.split(z, offsets, axis=-1)

def causal_dwconv_silu(xp, w):
    y = lax.conv_general_dilated(xp, w[:, None, :].astype(xp.dtype), window_strides=(1,), padding='VALID',
                                 dimension_numbers=('NWC', 'WIO', 'NWC'), feature_group_count=xp.shape[-1])
    return jax.nn.silu(y)

def dn_features(c, a, b, a_log, dt_bias):
    B, T, _ = c.shape
    cf = c.astype(F32)
    q = l2_normalize(cf[..., :DN_QK_W].reshape(B, T, DN_HEADS, DN_DK)) * (DN_DK ** -0.5)
    k = l2_normalize(cf[..., DN_QK_W:2 * DN_QK_W].reshape(B, T, DN_HEADS, DN_DK))
    v = cf[..., 2 * DN_QK_W:].reshape(B, T, DN_HEADS, DN_DV)
    beta = jax.nn.sigmoid(b.astype(F32))
    g = -jnp.exp(a_log.astype(F32)) * jax.nn.softplus(a.astype(F32) + dt_bias.astype(F32))
    return q, k, v, g, beta

def dn_output(o, z, gain, dtype):
    B, T = o.shape[:2]
    on = o * lax.rsqrt(jnp.mean(o * o, axis=-1, keepdims=True) + NORM_EPS) * gain.astype(F32)
    y = on * jax.nn.silu(z.astype(F32)).reshape(B, T, DN_HEADS, DN_DV)
    return y.reshape(B, T, DN_V_W).astype(dtype)

def gated_delta_chunked(q, k, v, g, beta):
    B, T, H, DK = q.shape
    DV = v.shape[-1]
    C = DN_CHUNK
    NC = T // C

    def chunks(x):
        return jnp.moveaxis(x.reshape((B, NC, C, H) + x.shape[3:]), 3, 1)

    qc, kc, vc, bc = chunks(q), chunks(k), chunks(v), chunks(beta)
    gc = jnp.cumsum(chunks(g), axis=-1)
    tri = jnp.tril(jnp.ones((C, C), bool))
    strict = jnp.tril(jnp.ones((C, C), bool), -1)
    diff = gc[..., :, None] - gc[..., None, :]
    decay = jnp.where(tri, jnp.exp(jnp.where(tri, diff, 0.0)), 0.0)
    kk = jnp.einsum('bhnid,bhnjd->bhnij', kc, kc)
    a_mat = jnp.where(strict, bc[..., :, None] * kk * decay, 0.0) + jnp.eye(C, dtype=F32)
    rhs = jnp.concatenate([vc * bc[..., None], kc * (bc * jnp.exp(gc))[..., None]], axis=-1)
    sol = lax.linalg.triangular_solve(a_mat, rhs, left_side=True, lower=True)
    val, kcd = sol[..., :DV], sol[..., DV:]
    a_qk = jnp.einsum('bhnid,bhnjd->bhnij', qc, kc) * decay
    q_dec = qc * jnp.exp(gc)[..., None]
    g_last = gc[..., -1]
    k_dec = kc * jnp.exp(g_last[..., None] - gc)[..., None]

    def step(S, xs):
        qd, kd, vl, kcd_c, aqk, gl = xs
        v_new = vl - jnp.einsum('bhck,bhkv->bhcv', kcd_c, S)
        o = jnp.einsum('bhck,bhkv->bhcv', qd, S) + jnp.einsum('bhcj,bhjv->bhcv', aqk, v_new)
        S = S * jnp.exp(gl)[..., None, None] + jnp.einsum('bhck,bhcv->bhkv', kd, v_new)
        return S, o

    xs = tuple(jnp.moveaxis(t, 2, 0) for t in (q_dec, k_dec, val, kcd, a_qk, g_last))
    S_fin, o = lax.scan(step, jnp.zeros((B, H, DK, DV), F32), xs)
    o = jnp.transpose(o, (1, 0, 3, 2, 4)).reshape(B, T, H, DV)
    return o, S_fin

def gated_delta_recurrent(q, k, v, g, beta, S0):
    def step(S, xs):
        qt, kt, vt, gt, bt = xs
        S = S * jnp.exp(gt)[..., None, None]
        pred = jnp.einsum('bhk,bhkv->bhv', kt, S)
        S = S + jnp.einsum('bhk,bhv->bhkv', kt, bt[..., None] * (vt - pred))
        return S, jnp.einsum('bhk,bhkv->bhv', qt, S)

    xs = tuple(jnp.moveaxis(t, 1, 0) for t in (q, k, v, g, beta))
    S_fin, o = lax.scan(step, S0, xs)
    return jnp.moveaxis(o, 0, 1), S_fin

def dsa_features(q, k, v, qi, ki, pos):
    B, T, _ = q.shape
    q = rope_partial(q.reshape(B, T, ATT_HEADS, HEAD_DIM), pos)
    k = rope_partial(k.reshape(B, T, KV_HEADS, HEAD_DIM), pos)
    v = v.reshape(B, T, KV_HEADS, HEAD_DIM)
    qi = rope_partial(qi.reshape(B, T, IDX_HEADS, IDX_DIM), pos)
    ki = rope_partial(ki.reshape(B, T, 1, IDX_DIM), pos)[:, :, 0]
    return q, k, v, qi, ki

def index_scores(qi, ki, wi):
    s = jax.nn.relu(jnp.einsum('bqhd,bsd->bqhs', qi, ki).astype(F32) * (IDX_DIM ** -0.5))
    return jnp.einsum('bqh,bqhs->bqs', wi.astype(F32) * (IDX_HEADS ** -0.5), s)

def sparse_attend(q, ks, vs, valid):
    B, Q, H, HD = q.shape
    qg = q.reshape(B, Q, KV_HEADS, H // KV_HEADS, HD)
    s = jnp.einsum('bqngd,bqknd->bqngk', qg, ks).astype(F32) * (HD ** -0.5)
    s = jnp.where(valid[:, :, None, None, :], s, -jnp.inf)
    p = jax.nn.softmax(s, axis=-1).astype(vs.dtype)
    o = jnp.einsum('bqngk,bqknd->bqngd', p, vs)
    return o.reshape(B, Q, H * HD)

def dsa_prompt(q, k, v, qi, ki, wi, topk):
    B, T = q.shape[:2]
    nb = T // Q_BLOCK
    bidx = jnp.arange(B)[:, None, None]
    kpos = jnp.arange(T)

    def blocks(x):
        return jnp.swapaxes(x.reshape((B, nb, Q_BLOCK) + x.shape[2:]), 0, 1)

    def one_block(args):
        qb, qib, wib, t0 = args
        tpos = t0 + jnp.arange(Q_BLOCK)
        visible = kpos[None, :] <= tpos[:, None]
        score = jnp.where(visible[None], index_scores(qib, ki, wib), -jnp.inf)
        _, sel = lax.top_k(score, topk)
        valid = sel <= tpos[None, :, None]
        return sparse_attend(qb, k[bidx, sel], v[bidx, sel], valid)

    out = lax.map(one_block, (blocks(q), blocks(qi), blocks(wi), jnp.arange(nb) * Q_BLOCK))
    return jnp.swapaxes(out, 0, 1).reshape(B, T, ATT_Q_W)

def dsa_sample(q, k_new, v_new, qi, ki_new, wi, cache_k, cache_v, cache_kidx, page_table, layer, topk):
    B, S = q.shape[:2]
    past = page_table.shape[1] * PAGE_SIZE
    slots = jnp.arange(PAGE_SIZE)
    ki_past = cache_kidx[page_table[:, :, None], slots[None, None, :], layer].reshape(B, past, IDX_DIM)
    ki_all = jnp.concatenate([ki_past.astype(ki_new.dtype), ki_new], axis=1)
    qpos = past + jnp.arange(S)
    kpos = jnp.arange(past + S)
    visible = kpos[None, :] <= qpos[:, None]
    score = jnp.where(visible[None], index_scores(qi, ki_all, wi), -jnp.inf)
    _, sel = lax.top_k(score, topk)
    in_past = sel < past
    ps = jnp.minimum(sel, past - 1)
    phys = jnp.take_along_axis(page_table, (ps // PAGE_SIZE).reshape(B, S * topk), axis=1).reshape(B, S, topk)
    slot = ps % PAGE_SIZE
    bidx = jnp.arange(B)[:, None, None]
    ns = jnp.clip(sel - past, 0, S - 1)
    sel_k = jnp.where(in_past[..., None, None], cache_k[phys, slot, layer].astype(k_new.dtype), k_new[bidx, ns])
    sel_v = jnp.where(in_past[..., None, None], cache_v[phys, slot, layer].astype(v_new.dtype), v_new[bidx, ns])
    valid = sel <= qpos[None, :, None]
    return sparse_attend(q, sel_k, sel_v, valid)

def branch_merge(o_dn, o_att, g_dn, g_att, w_dn_up, w_att_up, w_o):
    y = jax.nn.sigmoid(g_dn) * (o_dn @ w_dn_up) + jax.nn.sigmoid(g_att) * (o_att @ w_att_up)
    return y @ w_o

def mem_kv(mem, g, w_mk, w_mv):
    B, M, _ = mem.shape
    m = rms_norm(mem, g)
    return ((m @ w_mk).reshape(B, M, MEM_HEADS, MEM_HEAD_DIM), (m @ w_mv).reshape(B, M, MEM_HEADS, MEM_HEAD_DIM))

def mem_attend(x, mk, mv, g, w_mq, w_mo):
    B, T, _ = x.shape
    q = (rms_norm(x, g) @ w_mq).reshape(B, T, MEM_HEADS, MEM_HEAD_DIM)
    s = jnp.einsum('bthd,bmhd->bhtm', q, mk.astype(q.dtype)).astype(F32) * (MEM_HEAD_DIM ** -0.5)
    p = jax.nn.softmax(s, axis=-1).astype(q.dtype)
    o = jnp.einsum('bhtm,bmhd->bthd', p, mv.astype(q.dtype)).reshape(B, T, MEM_W)
    return o @ w_mo

def peer_block(h, wq, sub_keys, u, v):
    n = h.shape[0]
    q = (h @ wq).reshape(n, PEER_HEADS, 2, PEER_QDIM // 2)
    s = jnp.einsum('nhcd,hckd->nhck', q, sub_keys).astype(F32)
    s_top, i_top = lax.top_k(s, PEER_TOPK)
    cand = (s_top[:, :, 0, :, None] + s_top[:, :, 1, None, :]).reshape(n, PEER_HEADS, PEER_TOPK * PEER_TOPK)
    cidx = (i_top[:, :, 0, :, None] * N_KEYS + i_top[:, :, 1, None, :]).reshape(n, PEER_HEADS, PEER_TOPK * PEER_TOPK)
    best, pos = lax.top_k(cand, PEER_TOPK)
    eidx = jnp.take_along_axis(cidx, pos, axis=-1).reshape(n, PEER_HEADS * PEER_TOPK)
    gate = jax.nn.softmax(best, axis=-1).reshape(n, PEER_HEADS * PEER_TOPK)
    act = jax.nn.gelu(jnp.einsum('nd,ned->ne', h, u[eidx]).astype(F32), approximate=False)
    return jnp.einsum('ne,ned->nd', (gate * act).astype(h.dtype), v[eidx])

def peer_ffn(h, wq, sub_keys, u, v):
    B, T, D = h.shape
    n = B * T
    flat = h.reshape(n, D)
    if n % PEER_BLOCK == 0 and n > PEER_BLOCK:
        out = lax.map(lambda hb: peer_block(hb, wq, sub_keys, u, v), flat.reshape(n // PEER_BLOCK, PEER_BLOCK, D))
        out = out.reshape(n, D)
    else:
        out = peer_block(flat, wq, sub_keys, u, v)
    return out.reshape(B, T, D)

def setup_inputs(seed: int = 0) -> dict:
    key = jax.random.key(seed)
    ks = iter(jax.random.split(key, 48))

    def nrm(shape, scale=1.0):
        return jax.random.normal(next(ks), shape, F32) * scale

    def gain(shape):
        return 1.0 + nrm(shape, 0.01)

    n_pages = PAST_LEN // PAGE_SIZE
    n_used = DEC_BATCH * n_pages
    n_pool = n_used + max(1, n_used // 4)
    perm = jax.random.permutation(next(ks), n_pool)
    page_table = perm[:n_used].reshape(DEC_BATCH, n_pages).astype(jnp.int32)
    dt = jnp.exp(jax.random.uniform(next(ks), (DEPTH, DN_HEADS), F32, np.log(1e-3), np.log(1e-1)))
    return {
        'x_prompt': nrm((BATCH, SEQ, D_MODEL)),
        'x_sample': nrm((DEC_BATCH, DEC_SEQ, D_MODEL)),
        'cache_k': nrm((n_pool, PAGE_SIZE, DEPTH, KV_HEADS, HEAD_DIM)),
        'cache_v': nrm((n_pool, PAGE_SIZE, DEPTH, KV_HEADS, HEAD_DIM)),
        'cache_kidx': nrm((n_pool, PAGE_SIZE, DEPTH, IDX_DIM)),
        'state_conv': nrm((DEPTH, DEC_BATCH, CONV_W - 1, CONV_DIM)),
        'state_delta': nrm((DEPTH, DEC_BATCH, DN_HEADS, DN_DK, DN_DV), 0.1),
        'cache_mem_k': nrm((DEPTH, DEC_BATCH, MEM_LEN, MEM_HEADS, MEM_HEAD_DIM)),
        'cache_mem_v': nrm((DEPTH, DEC_BATCH, MEM_LEN, MEM_HEADS, MEM_HEAD_DIM)),
        'page_table': page_table,
        'mem_prompt': nrm((BATCH, MEM_LEN, D_MODEL)),
        'norm_mix': gain((DEPTH, D_MODEL)),
        'w_in': nrm((DEPTH, D_MODEL, N_IN), D_MODEL ** -0.5),
        'dn_conv_w': nrm((DEPTH, CONV_W, CONV_DIM), CONV_W ** -0.5),
        'dn_a_log': jnp.log(jax.random.uniform(next(ks), (DEPTH, DN_HEADS), F32, 1.0, 16.0)),
        'dn_dt_bias': dt + jnp.log(-jnp.expm1(-dt)),
        'dn_norm': gain((DEPTH, DN_DV)),
        'w_dn_up': nrm((DEPTH, DN_V_W, D_MODEL), DN_V_W ** -0.5),
        'w_att_up': nrm((DEPTH, ATT_Q_W, D_MODEL), ATT_Q_W ** -0.5),
        'w_o': nrm((DEPTH, D_MODEL, D_MODEL), D_MODEL ** -0.5),
        'norm_mem_q': gain((DEPTH, D_MODEL)),
        'norm_mem_kv': gain((DEPTH, D_MODEL)),
        'w_mq': nrm((DEPTH, D_MODEL, MEM_W), D_MODEL ** -0.5),
        'w_mk': nrm((DEPTH, D_MODEL, MEM_W), D_MODEL ** -0.5),
        'w_mv': nrm((DEPTH, D_MODEL, MEM_W), D_MODEL ** -0.5),
        'w_mo': nrm((DEPTH, MEM_W, D_MODEL), MEM_W ** -0.5),
        'norm_ffn': gain((DEPTH, D_MODEL)),
        'peer_wq': nrm((DEPTH, D_MODEL, PEER_HEADS * PEER_QDIM), D_MODEL ** -0.5),
        'peer_keys': nrm((DEPTH, PEER_HEADS, 2, N_KEYS, PEER_QDIM // 2), (PEER_QDIM // 2) ** -0.5),
        'peer_u': nrm((DEPTH, N_EXPERTS, D_MODEL), D_MODEL ** -0.5),
        'peer_v': nrm((DEPTH, N_EXPERTS, D_MODEL), (PEER_HEADS * PEER_TOPK) ** -0.5),
        'norm_final': gain((D_MODEL,)),
    }

def reference(x_prompt, x_sample, cache_k, cache_v, cache_kidx, state_conv, state_delta, cache_mem_k, cache_mem_v,
              page_table, mem_prompt, norm_mix, w_in, dn_conv_w, dn_a_log, dn_dt_bias, dn_norm, w_dn_up, w_att_up,
              w_o, norm_mem_q, norm_mem_kv, w_mq, w_mk, w_mv, w_mo, norm_ffn, peer_wq, peer_keys, peer_u, peer_v,
              norm_final):
    B, T, _ = x_prompt.shape
    S = x_sample.shape[1]
    past = page_table.shape[1] * PAGE_SIZE
    pos_p = jnp.arange(T)
    pos_s = past + jnp.arange(S)
    topk_p = min(TOPK_MAX, T // 4)
    topk_s = min(TOPK_MAX, (past + S) // 4)

    hp, hs = x_prompt, x_sample
    p_k, p_v, p_kidx, p_conv, p_delta, p_mk, p_mv = [], [], [], [], [], [], []
    s_k, s_v, s_kidx, s_conv, s_delta = [], [], [], [], []
    for l in range(DEPTH):
        (conv_in, z, a, b, q, k, v, qi, ki, wi, g_dn, g_att) = split_columns(rms_norm(hp, norm_mix[l]) @ w_in[l])
        cbuf = jnp.concatenate([jnp.zeros((B, CONV_W - 1, CONV_DIM), conv_in.dtype), conv_in], axis=1)
        dq, dk, dv, dg, dbeta = dn_features(causal_dwconv_silu(cbuf, dn_conv_w[l]), a, b, dn_a_log[l], dn_dt_bias[l])
        o, st = gated_delta_chunked(dq, dk, dv, dg, dbeta)
        o_dn = dn_output(o, z, dn_norm[l], hp.dtype)
        aq, ak, av, aqi, aki = dsa_features(q, k, v, qi, ki, pos_p)
        o_att = dsa_prompt(aq, ak, av, aqi, aki, wi, topk_p)
        hp = hp + branch_merge(o_dn, o_att, g_dn, g_att, w_dn_up[l], w_att_up[l], w_o[l])
        mk, mv = mem_kv(mem_prompt, norm_mem_kv[l], w_mk[l], w_mv[l])
        hp = hp + mem_attend(hp, mk, mv, norm_mem_q[l], w_mq[l], w_mo[l])
        hp = hp + peer_ffn(rms_norm(hp, norm_ffn[l]), peer_wq[l], peer_keys[l], peer_u[l], peer_v[l])
        p_k.append(ak)
        p_v.append(av)
        p_kidx.append(aki)
        p_conv.append(cbuf[:, -(CONV_W - 1):])
        p_delta.append(st)
        p_mk.append(mk)
        p_mv.append(mv)

        (conv_in, z, a, b, q, k, v, qi, ki, wi, g_dn, g_att) = split_columns(rms_norm(hs, norm_mix[l]) @ w_in[l])
        cbuf = jnp.concatenate([state_conv[l].astype(conv_in.dtype), conv_in], axis=1)
        dq, dk, dv, dg, dbeta = dn_features(causal_dwconv_silu(cbuf, dn_conv_w[l]), a, b, dn_a_log[l], dn_dt_bias[l])
        o, st = gated_delta_recurrent(dq, dk, dv, dg, dbeta, state_delta[l].astype(F32))
        o_dn = dn_output(o, z, dn_norm[l], hs.dtype)
        aq, ak, av, aqi, aki = dsa_features(q, k, v, qi, ki, pos_s)
        o_att = dsa_sample(aq, ak, av, aqi, aki, wi, cache_k, cache_v, cache_kidx, page_table, l, topk_s)
        hs = hs + branch_merge(o_dn, o_att, g_dn, g_att, w_dn_up[l], w_att_up[l], w_o[l])
        hs = hs + mem_attend(hs, cache_mem_k[l], cache_mem_v[l], norm_mem_q[l], w_mq[l], w_mo[l])
        hs = hs + peer_ffn(rms_norm(hs, norm_ffn[l]), peer_wq[l], peer_keys[l], peer_u[l], peer_v[l])
        s_k.append(ak)
        s_v.append(av)
        s_kidx.append(aki)
        s_conv.append(cbuf[:, -(CONV_W - 1):])
        s_delta.append(st)

    y_prompt = rms_norm(hp, norm_final)
    y_sample = rms_norm(hs, norm_final)
    return (y_prompt, y_sample,
            jnp.stack(p_k, axis=2), jnp.stack(p_v, axis=2), jnp.stack(p_kidx, axis=2),
            jnp.stack(p_conv, axis=0), jnp.stack(p_delta, axis=0),
            jnp.stack(p_mk, axis=0), jnp.stack(p_mv, axis=0),
            jnp.stack(s_k, axis=2), jnp.stack(s_v, axis=2), jnp.stack(s_kidx, axis=2),
            jnp.stack(s_conv, axis=0), jnp.stack(s_delta, axis=0))


_drawn_inputs = setup_inputs


def setup_inputs(seed=0):
    import zlib

    import numpy as np

    out = dict(_drawn_inputs(seed))
    spreads = {}
    factors = {'norm_mix': 3.065,
     'dn_norm': 7.379,
     'norm_mem_q': 8.0,
     'norm_mem_kv': 5.507,
     'norm_ffn': 30.089,
     'norm_final': 32.854}
    for name, (base, spread) in spreads.items():
        noise = np.random.default_rng([zlib.crc32(name.encode()), seed]).standard_normal(out[name].shape)
        drawn = base * np.exp(spread * noise) if base else spread * noise
        out[name] = __import__('jax').numpy.asarray(drawn.astype(out[name].dtype))
    for name, factor in factors.items():
        out[name] = (out[name] * factor).astype(out[name].dtype)
    return out
```

```python
from contextlib import contextmanager, ExitStack


import numpy as np
import concourse.bass as bass
from concourse import mybir

FP32 = mybir.dt.float32
FP32R = mybir.dt.float32r
I32 = mybir.dt.int32
U32 = mybir.dt.uint32
ALU = mybir.AluOpType
ACT = mybir.ActivationFunctionType
AX = mybir.AxisListType
ds = bass.ds

P = 128
D = 1024
KD = D // P
T = 512
B = 8
DEPTH = 2
TT = T // P
NT = TT + 1
TOK = T + B
TOKP = NT * P
PAST, PAGE = 4096, 128
PAGES = PAST // PAGE
H, DK = 4, 128
CONV = 3 * H * DK
CC = CONV // P
CW = 4
AH, KV, HD = 8, 2, 64
IH, ID = 4, 64
ROT = HD // 4
HALF = ROT // 2
TOPK_P = min(256, T // 4)
TOPK_S = min(256, (PAST + 1) // 4)
MEM, MH, MD = 256, 4, 128
MT_ = MEM // P
MW = MH * MD
NK = 128
PH, PTOP = 8, 16
PJ = PH * PTOP
EPS = 1e-6
BIG = 3.0e38
TAKEN = -3.4e38
C_Z = CONV
NAT_W = H * DK + 2 * H + AH * HD + 2 * KV * HD + IH * ID + ID + IH
C_G = C_Z + NAT_W
N_IN = C_G + 2 * D
N_A = H * DK
N_B = N_A + H
N_Q = N_B + H
N_K = N_Q + AH * HD
N_V = N_K + KV * HD
N_QI = N_V + KV * HD
N_KI = N_QI + IH * ID
N_WI = N_KI + ID

ROPE_THETA = 500000.0


def host_constants():
    p = np.arange(P)[:, None]
    f = np.arange(P)[None, :]
    cols = {}
    cols["ident"] = (p == f)
    cols["ones"] = np.ones((P, P))
    cols["triu"] = (p <= f)
    cols["tril"] = (p >= f)
    cols["strict"] = (p > f)
    for s in range(7):
        cols[f"lev{s}"] = ((f >> s) % 2 == 1) & ((p >> s) == (f >> s) - 1)
    cols["iota"] = np.broadcast_to(f, (P, P))
    pos = np.concatenate([np.arange(T), np.full(P, PAST)]).astype(np.float32)
    inv = np.float32(ROPE_THETA) ** (-np.arange(HALF, dtype=np.float32) / np.float32(HALF))
    ang = (pos[:, None] * inv[None, :]).astype(np.float32)
    cols["cos"] = np.cos(ang).reshape(NT, P, HALF).transpose(1, 0, 2).reshape(P, -1)
    cols["sin"] = np.sin(ang).reshape(NT, P, HALF).transpose(1, 0, 2).reshape(P, -1)
    cols["tpos"] = np.arange(T).reshape(TT, P).T
    cols["iota512"] = np.broadcast_to(np.arange(T)[None, :], (P, T))
    cols["slot"] = p
    cols["own"] = (p[:, :1] // IH == f[:, :B])
    where, parts, at = {}, [], 0
    for name, a in cols.items():
        a = np.asarray(a, np.float32)
        where[name] = (at, a.shape[1])
        at += a.shape[1]
        parts.append(a)
    return np.ascontiguousarray(np.concatenate(parts, axis=1)), where


class Core:

    def __init__(self, nc):
        self.nc = nc
        self.used = 0

    def unique(self, name):
        self.used += 1
        return f"{name}_{self.used}"

    def buffer(self, name, shape, dt):
        return self.nc.sbuf_tensor(self.unique(name), list(shape), dt)


@contextmanager
def stage(g, *names):
    nc = g.nc
    with ExitStack() as ctx:
        sems = [ctx.enter_context(nc.semaphore(g.unique(n))) for n in names]
        with nc.Block(no_gpsimd_drain=True) as block:
            yield (block, *sems)
        for s in sems:
            nc.sync.sem_clear(s)
        nc.all_engine_barrier()


def in_order(eng, sem):
    count = [0]

    def step(ins):
        count[0] += 1
        ins.then_inc(sem, 1)
        eng.wait_ge(sem, count[0])
    return step



def norm_transposed(g, src, tiles, gains, dst):
    nc = g.nc
    with ExitStack() as ctx:
        gain = ctx.enter_context(g.buffer("gain", [P, 1, KD], FP32))
        sq = ctx.enter_context(g.buffer("sq", [P, D], FP32))
        ss = ctx.enter_context(g.buffer("ss", [P, 4], FP32))
        xn = ctx.enter_context(g.buffer("xn", [P, D], FP32))
        with stage(g, "gain_in") as (block, gain_in):
            @block.sync
            def _(sp):
                sp.dma_start(gain[:], gains, allow_slow_non_contiguous=True).then_inc(gain_in, 16)
                sp.wait_ge(gain_in, 16)
        with nc.Fori(0, tiles) as i:
            with stage(g, "squared", "rooted", "vec", "turned") as (block, squared, rooted, vec, turned):
                x = src[:, ds(i, 1), :].rearrange("p a n -> p (a n)")

                @block.scalar
                def _(act):
                    nc.scalar.activation(sq[:], x, ACT.Square, accum_out=ss[:, 0:1]).then_inc(squared, 1)
                    act.wait_ge(vec, 1)
                    nc.scalar.activation(ss[:, 2:3], ss[:, 1:2], ACT.Sqrt).then_inc(rooted, 1)

                @block.vector
                def _(dve):
                    step = in_order(dve, vec)
                    dve.wait_ge(squared, 1)
                    step(nc.vector.tensor_scalar(ss[:, 1:2], ss[:, 0:1], 1.0 / D, EPS, ALU.mult, ALU.add))
                    dve.wait_ge(rooted, 1)
                    step(nc.vector.reciprocal(ss[:, 3:4], ss[:, 2:3]))
                    step(nc.vector.tensor_scalar(xn[:], x, ss[:, 3:4], None, ALU.mult))
                    dve.wait_ge(turned, 1)
                    for b in range(2):
                        nc.vector.tensor_tensor(
                            dst[:, 4 * b:4 * b + 4, ds(i * P, P)], g.ps[:, b, :].rearrange("p (k t) -> p k t", k=4),
                            gain[:, 0, 4 * b:4 * b + 4].unsqueeze(2).to_broadcast([P, 4, P]), ALU.mult)

                @block.tensor
                def _(pe):
                    pe.wait_ge(vec, 3)
                    for k in range(KD):
                        last = nc.tensor.transpose(g.ps[:, k // 4, (k % 4) * P:(k % 4 + 1) * P],
                                                   xn[:, k * P:(k + 1) * P], g.ident)
                    last.then_inc(turned, 1)



def linear(g, name, weights, nk, nw, chunks, groups, only=None):
    nc = g.nc
    count = len(groups(0, g.wb[:, 0]))
    body = 2 * count
    if only:
        to_vector = [only == "vector"] * body
    else:
        n_act = body // 2 - (body // 2) % 2
        to_vector = [not (x % 2 == 1 and x // 2 < n_act) for x in range(body)]
    n_v, n_a = sum(to_vector), body - sum(to_vector)
    with stage(g, name + "_w0", name + "_w1", "v_full", "a_full", "v_free", "a_free") as (
            block, w0, w1, v_full, a_full, v_free, a_free):
        w_in = (w0, w1)

        def wbuf(u):
            return g.wb[:, u].rearrange("p k n -> p (k n)")[:, 0:nk * nw].rearrange("p (k n) -> p k n", k=nk)

        @block.sync
        def _(sp):
            for u in range(2):
                sp.dma_start(wbuf(u), weights(u)).then_inc(w_in[u], 16)
            if chunks > 2:
                with sp.Fori(1, chunks // 2) as it:
                    for u in range(2):
                        through = to_vector[:(u + 1) * count]
                        if through[-1]:
                            sp.wait_ge(v_full, (it - 1) * n_v + sum(through))
                        else:
                            sp.wait_ge(a_full, (it - 1) * n_a + len(through) - sum(through))
                        sp.dma_start(wbuf(u), weights(it * 2 + u)).then_inc(w_in[u], 16)

        @block.tensor
        def _(pe):
            with pe.Fori(0, chunks // 2) as it:
                at_v = at_a = 0
                for u in range(2):
                    pe.wait_ge(w_in[u], it * 16 + 16)
                    for n, (parts, _) in enumerate(groups(it * 2 + u, wbuf(u))):
                        if to_vector[u * count + n]:
                            slot, full, free, total, at = at_v % 2, v_full, v_free, n_v, at_v
                            at_v += 1
                        else:
                            slot, full, free, total, at = 2 + at_a % 2, a_full, a_free, n_a, at_a
                            at_a += 1
                        pe.wait_ge(free, it * total + (at + 1))
                        for side, (lhs, rhs, rows, width) in enumerate(parts):
                            for k in range(nk):
                                last = nc.tensor.matmul(g.ps[0:rows, slot + 4 * side, 0:width], lhs(k), rhs(k),
                                                        start=(k == 0), stop=(k == nk - 1))
                        last.then_inc(full, 1)

        def drain(eng, mine, full, free, total, first, kind):
            eng.sem_inc(free, 2)
            with eng.Fori(0, chunks // 2) as it:
                at = 0
                for u in range(2):
                    for n, (parts, evac) in enumerate(groups(it * 2 + u, wbuf(u))):
                        if to_vector[u * count + n] != mine:
                            continue
                        slot = first + at % 2
                        eng.wait_ge(full, it * total + (at + 1))
                        main = g.ps[0:parts[0][2], slot, 0:parts[0][3]]
                        side = g.ps[0:parts[1][2], slot + 4, 0:parts[1][3]] if len(parts) > 1 else None
                        evac(kind, main, side).then_inc(free, 1)
                        at += 1

        if n_v:
            @block.vector
            def _(dve):
                drain(dve, True, v_full, v_free, n_v, 0, "vector")

        if n_a:
            @block.scalar
            def _(act):
                drain(act, False, a_full, a_free, n_a, 2, "scalar")


def copy(g, kind, dst, src):
    if kind == "vector":
        return g.nc.vector.tensor_copy(dst, src)
    return g.nc.scalar.copy(dst, src)


def weight_rows(w, l, k0, nk, c0, nw):
    v = w.rearrange("l (k p) n -> p (l k) n", p=P)
    per = w.shape[1] // P
    return lambda j: v[:, ds(l * per + k0, nk), ds(j * nw + c0, nw)]


def token_major(g, name, weights, lhs, nk, nw, chunks, evac, only=None, tiles=NT):
    def groups(j, w):
        return [([(lambda k, t=t: lhs[:, k, t * P:(t + 1) * P], lambda k: w[:, k, :], P, nw)],
                 lambda kind, main, side, t=t: evac(kind, t, j, main)) for t in range(tiles)]
    linear(g, name, weights, nk, nw, chunks, groups, only)


def channel_major(g, name, weights, rhs, nk, nw, chunks, evac, only=None, side=True, width=T):
    def groups(j, w):
        out = []
        for m in range(nw // P):
            parts = [(lambda k, m=m: w[:, k, m * P:(m + 1) * P], lambda k: rhs[:, k, 0:width], P, width)]
            if side:
                parts.append((lambda k, m=m: w[:, k, m * P:(m + 1) * P], lambda k: rhs[:, k, T:TOK], P, B))
            out.append((parts, lambda kind, main, sd, m=m: evac(kind, j * (nw // P) + m, main, sd)))
        return out
    linear(g, name, weights, nk, nw, chunks, groups, only)



def convolution(g, l, d, conv):
    nc = g.nc
    S0 = CW - 1 + T
    with ExitStack() as ctx:
        cin = ctx.enter_context(g.buffer("cin", [P, CC, S0 + B * CW], FP32))
        past = ctx.enter_context(g.buffer("conv_past", [B * (CW - 1), CONV], FP32))
        taps = ctx.enter_context(g.buffer("taps", [P, CW, CC], FP32))
        sig = ctx.enter_context(g.buffer("sig", [P, CC, TOK], FP32))
        win = cin[:, :, S0:S0 + B * CW].rearrange("p c (b w) -> p c b w", w=CW)
        with stage(g, "past_in", "turned", "zeroed") as (block, past_in, turned, zeroed):
            @block.sync
            def _(sp):
                sp.dma_start(past[:], d["state_conv"].rearrange("l b w c -> (l b w) c")
                             [ds(l * (B * (CW - 1)), B * (CW - 1)), :]).then_inc(past_in, 16)
                sp.dma_start(taps[:].rearrange("p w c -> p (w c)"),
                             d["dn_conv_w"].rearrange("l w (c p) -> p l (w c)", p=P)[:, ds(l, 1), :]
                             .rearrange("p l x -> p (l x)"), allow_slow_non_contiguous=True).then_inc(past_in, 16)

            @block.tensor
            def _(pe):
                pe.wait_ge(past_in, 32)
                for c in range(CC):
                    last = nc.tensor.transpose(g.ps[:, 0, c * 24:(c + 1) * 24], past[:, c * P:(c + 1) * P],
                                               g.ident[0:24, 0:24])
                last.then_inc(turned, 1)

            @block.vector
            def _(dve):
                nc.vector.memset(cin[:, :, 0:CW - 1], 0.0)
                dve.wait_ge(turned, 1)
                ps = g.ps[:, 0, 0:CC * 24].rearrange("p (c b w) -> p c b w", c=CC, w=CW - 1)
                for w in range(CW - 1):
                    nc.vector.tensor_copy(win[:, :, :, w], ps[:, :, :, w])

        def evac(kind, c, main, side):
            copy(g, kind, cin[:, ds(c, 1), CW - 1:S0].rearrange("p a n -> p (a n)"), main)
            return copy(g, kind, win[:, ds(c, 1), :, CW - 1].rearrange("p a b -> p (a b)"), side)
        channel_major(g, "conv", weight_rows(d["w_in"], l, 0, KD, 0, 384), g.ht, KD, 384, 4, evac)

        with stage(g, "stored", "vec", "squashed") as (block, stored, vec, squashed):
            @block.sync
            def _(sp):
                for c in range(CC):
                    sp.dma_start(d["p_conv"].rearrange("l b w (c p) -> p (l b) c w", p=P)[:, ds(l, 1), c, :]
                                 .rearrange("p l w -> p (l w)"), cin[:, c, T:S0],
                                 allow_slow_non_contiguous=True).then_inc(stored, 16)
                    for w in range(CW - 1):
                        sp.dma_start(d["s_conv"].rearrange("l b w (c p) -> p l c w b", p=P)[:, ds(l, 1), c, w, :]
                                     .rearrange("p l b -> p (l b)"), win[:, c, :, w + 1],
                                     allow_slow_non_contiguous=True).then_inc(stored, 16)
                sp.wait_ge(stored, 16 * CC * CW)

            @block.vector
            def _(dve):
                step = in_order(dve, vec)
                for c in range(CC):
                    def srcs(w):
                        return (cin[:, c, w:w + T], win[:, c, :, w])
                    for part, lo, hi in ((0, 0, T), (1, T, TOK)):
                        step(nc.vector.tensor_scalar(conv[:, c, lo:hi], srcs(0)[part], taps[:, 0, c:c + 1], None, ALU.mult))
                        for w in range(1, CW):
                            step(nc.vector.scalar_tensor_tensor(conv[:, c, lo:hi], srcs(w)[part], taps[:, w, c:c + 1],
                                                                conv[:, c, lo:hi], ALU.mult, ALU.add))
                    dve.wait_ge(squashed, c + 1)
                    nc.vector.tensor_tensor(conv[:, c, :], conv[:, c, :], sig[:, c, :], ALU.mult)

            @block.scalar
            def _(act):
                for c in range(CC):
                    act.wait_ge(vec, 2 * CW * (c + 1))
                    nc.scalar.activation(sig[:, c, :], conv[:, c, :], ACT.Sigmoid).then_inc(squashed, 1)



def delta_features(g, l, d, conv, kn, vn, gb):
    nc = g.nc
    gg, beta = gb[:, :, 0:H], gb[:, :, H:2 * H]
    with ExitStack() as ctx:
        sq = ctx.enter_context(g.buffer("sq2", [P, 2, TOK], FP32))
        rt = ctx.enter_context(g.buffer("rt", [P, 2, TOK], FP32))
        par = ctx.enter_context(g.buffer("par", [P, 2, H], FP32))
        ea = ctx.enter_context(g.buffer("ea", [P, H], FP32))
        tmp = ctx.enter_context(g.buffer("tmpab", [P, 4, NT * H], FP32))
        with stage(g, "squared", "summed", "epsed", "rooted", "vec") as (block, squared, summed, epsed, rooted, vec):
            @block.scalar
            def _(act):
                for c in range(2 * H + 1):
                    if c < 2 * H:
                        if c >= 2:
                            act.wait_ge(summed, c - 1)
                        nc.scalar.activation(sq[:, c % 2, :], conv[:, c, :], ACT.Square).then_inc(squared, 1)
                    if c >= 1:
                        act.wait_ge(epsed, c)
                        nc.scalar.activation(rt[:, (c - 1) % 2, :], rt[:, (c - 1) % 2, :], ACT.Sqrt).then_inc(rooted, 1)

            @block.tensor
            def _(pe):
                for c in range(2 * H):
                    pe.wait_ge(squared, c + 1)
                    if c >= 2:
                        pe.wait_ge(epsed, c - 1)
                    nc.tensor.matmul(g.ps[:, c % 2, :], g.ones, sq[:, c % 2, 0:T], start=True, stop=True)
                    nc.tensor.matmul(g.ps[:, 2 + c % 2, 0:B], g.ones, sq[:, c % 2, T:TOK], start=True,
                                     stop=True).then_inc(summed, 1)

            @block.vector
            def _(dve):
                step = in_order(dve, vec)
                for c in range(2 * H):
                    dve.wait_ge(summed, c + 1)
                    nc.vector.tensor_scalar(rt[:, c % 2, 0:T], g.ps[:, c % 2, :], EPS, None, ALU.add)
                    nc.vector.tensor_scalar(rt[:, c % 2, T:TOK], g.ps[:, 2 + c % 2, 0:B], EPS, None,
                                            ALU.add).then_inc(epsed, 1)
                    dve.wait_ge(rooted, c + 1)
                    step(nc.vector.reciprocal(rt[:, c % 2, :], rt[:, c % 2, :]))
                    scale = DK ** -0.5 if c < H else 1.0
                    step(nc.vector.scalar_tensor_tensor(conv[:, c, :], conv[:, c, :], scale, rt[:, c % 2, :],
                                                        ALU.mult, ALU.mult))
        with stage(g, "par_in", "vec", "act_done", "turned", "copied") as (block, par_in, vec, act_done, turned, copied):
            a_in = g.nat[:, :, N_A:N_A + H]
            b_in = g.nat[:, :, N_B:N_B + H]

            def t3(n):
                return tmp[:, n, :].rearrange("p (t h) -> p t h", h=H)

            @block.sync
            def _(sp):
                for n, v in enumerate((d["dn_a_log"], d["dn_dt_bias"])):
                    sp.dma_start(par[:, n, :], v[ds(l, 1), :].to_broadcast([P, H])).then_inc(par_in, 16)

            @block.vector
            def _(dve):
                step = in_order(dve, vec)
                dve.wait_ge(par_in, 32)
                bias = par[:, 1, :].unsqueeze(1).to_broadcast([P, NT, H])
                step(nc.vector.tensor_tensor(t3(0), a_in, bias, ALU.add))
                step(nc.vector.tensor_scalar(tmp[:, 1, :], tmp[:, 0, :], -1.0, None, ALU.mult))
                step(nc.vector.tensor_tensor(tmp[:, 1, :], tmp[:, 0, :], tmp[:, 1, :], ALU.max))
                step(nc.vector.tensor_scalar(tmp[:, 0, :], tmp[:, 0, :], 0.0, None, ALU.max))
                dve.wait_ge(act_done, 2)
                step(nc.vector.tensor_scalar(tmp[:, 1, :], tmp[:, 2, :], 1.0, None, ALU.add))
                dve.wait_ge(act_done, 3)
                step(nc.vector.tensor_tensor(tmp[:, 0, :], tmp[:, 0, :], tmp[:, 3, :], ALU.add))
                step(nc.vector.tensor_scalar(ea[:], ea[:], -1.0, None, ALU.mult))
                step(nc.vector.tensor_tensor(gg, t3(0), ea[:].unsqueeze(1).to_broadcast([P, NT, H]), ALU.mult))
                for n in range(2 * TT):
                    dve.wait_ge(turned, n + 1)
                    dst = (kn, vn)[n // TT]
                    nc.vector.tensor_copy(dst[:, n % TT, :, :].rearrange("p h n -> p (h n)"),
                                          g.ps[:, n % 2, :]).then_inc(copied, 1)

            @block.scalar
            def _(act):
                act.wait_ge(par_in, 32)
                nc.scalar.activation(ea[:], par[:, 0, :], ACT.Exp).then_inc(act_done, 1)
                act.wait_ge(vec, 4)
                nc.scalar.activation(tmp[:, 2, :], tmp[:, 1, :], ACT.Exp, scale=-1.0).then_inc(act_done, 1)
                act.wait_ge(vec, 5)
                nc.scalar.activation(tmp[:, 3, :], tmp[:, 1, :], ACT.Ln).then_inc(act_done, 1)
                nc.scalar.activation(beta, b_in, ACT.Sigmoid).then_inc(act_done, 1)

            @block.tensor
            def _(pe):
                for n in range(2 * TT):
                    if n >= 2:
                        pe.wait_ge(copied, n - 1)
                    for h in range(H):
                        last = nc.tensor.transpose(g.ps[:, n % 2, h * P:(h + 1) * P],
                                                   conv[:, (1 + n // TT) * H + h, (n % TT) * P:(n % TT + 1) * P], g.ident)
                    last.then_inc(turned, 1)


def delta_prompt(g, l, d, conv, kn, vn, gb, o_all):
    nc = g.nc
    W = H * P

    with ExitStack() as ctx:
        def sb(name, shape=(P, H, P)):
            return ctx.enter_context(g.buffer(name, list(shape), FP32))
        qk = sb("qk", (P, 2 * H, P))
        kc = sb("kc")
        S, gbc, d1, e1, e2, low, lowT, lev, M, MT, Pm, aq, r, vnew, vs, t1 = (
            sb(n) for n in ("S", "gbc", "d1", "e1", "e2", "low", "lowT", "lev", "M", "MT", "Pm", "aq", "r", "vnew", "vs", "t1"))
        gc = sb("gc", (P, 2 * H))
        ex = sb("ex", (P, 3, H))
        be = sb("be", (P, H))
        dif = sb("dif", (P, H))

        def bank(n):
            return g.ps[:, n, :].rearrange("p (h n) -> p h n", h=H)

        def over(x):
            return x.unsqueeze(2).to_broadcast([P, H, P])

        def mask(x):
            return x.unsqueeze(1).to_broadcast([P, H, P])

        with stage(g, "zeroed") as (block, zeroed):
            @block.vector
            def _(dve):
                nc.vector.memset(S[:], 0.0)

        with nc.Fori(0, TT) as c:
            gg = gb[:, ds(c, 1), 0:H].rearrange("p a h -> p (a h)")
            beta = gb[:, ds(c, 1), H:2 * H].rearrange("p a h -> p (a h)")

            def tok(tile):
                return qk[:, tile, :]
            vc = vn[:, ds(c, 1), :, :].rearrange("p a h n -> p (a h) n")
            with stage(g, "vec", "grams", "sums", "exps", "level_p", "level_m", "state_read", "solved",
                       "out_ready", "fetched") as (
                           block, vec, grams, sums, exps, level_p, level_m, state_read, solved, out_ready, fetched):
                V = {}

                @block.vector
                def _(dve):
                    count = [0]

                    def step(ins, name=None):
                        count[0] += 1
                        ins.then_inc(vec, 1)
                        dve.wait_ge(vec, count[0])
                        if name:
                            V[name] = count[0]
                    step(nc.vector.tensor_copy(gbc[:], over(gg)), "g_spread")
                    step(nc.vector.tensor_copy(M[:], mask(g.ident)))
                    step(nc.vector.tensor_copy(MT[:], mask(g.ident)), "started")
                    dve.wait_ge(sums, 1)
                    step(nc.vector.tensor_copy(gc[:], g.ps[:, 1, 0:2 * H]))
                    step(nc.vector.tensor_tensor(dif[:], gc[:, H:2 * H], gc[:, 0:H], ALU.subtract), "gc")
                    step(nc.vector.tensor_tensor(d1[:], bank(0), over(gc[:, 0:H]), ALU.subtract))
                    step(nc.vector.tensor_scalar(e1[:], d1[:], 0.0, None, ALU.min))
                    step(nc.vector.tensor_scalar(e2[:], d1[:], -1.0, 0.0, ALU.mult, ALU.min), "diffs")
                    dve.wait_ge(exps, 5)
                    step(nc.vector.tensor_tensor(be[:], beta, ex[:, 0, :], ALU.mult))
                    dve.wait_ge(grams, 1)
                    step(nc.vector.tensor_tensor(low[:], bank(2), e2[:], ALU.mult))
                    step(nc.vector.tensor_tensor(low[:], low[:], over(beta), ALU.mult))
                    step(nc.vector.tensor_tensor(low[:], low[:], mask(g.strict), ALU.mult), "low")
                    step(nc.vector.tensor_tensor(aq[:], bank(3), e1[:], ALU.mult))
                    step(nc.vector.tensor_tensor(aq[:], aq[:], mask(g.triu), ALU.mult), "aq")
                    dve.wait_ge(grams, 2)
                    step(nc.vector.tensor_copy(lowT[:], bank(4)))
                    for s in range(7):
                        step(nc.vector.tensor_tensor(lev[:], lowT[:], mask(g.lev[s]), ALU.mult), f"lev{s}")
                        dve.wait_ge(level_p, s + 1)
                        step(nc.vector.tensor_copy(Pm[:], bank(5)), f"P{s}")
                        dve.wait_ge(level_m, s + 1)
                        step(nc.vector.tensor_tensor(M[:], M[:], bank(6), ALU.subtract))
                        step(nc.vector.tensor_tensor(MT[:], MT[:], bank(7), ALU.subtract), f"M{s}")
                    dve.wait_ge(state_read, 1)
                    step(nc.vector.tensor_tensor(t1[:], bank(0), over(be[:]), ALU.mult))
                    step(nc.vector.tensor_tensor(r[:], vc, over(beta), ALU.mult))
                    step(nc.vector.tensor_tensor(r[:], r[:], t1[:], ALU.subtract), "rhs")
                    dve.wait_ge(solved, 1)
                    step(nc.vector.tensor_copy(vnew[:], bank(2)), "vnew")
                    step(nc.vector.tensor_tensor(vs[:], vnew[:], over(ex[:, 2, :]), ALU.mult), "vs")
                    step(nc.vector.tensor_tensor(t1[:], bank(1), over(ex[:, 0, :]), ALU.mult))
                    step(nc.vector.tensor_tensor(S[:], S[:], over(ex[:, 1, :]), ALU.mult))
                    dve.wait_ge(out_ready, 1)
                    step(nc.vector.tensor_tensor(o_all[:, ds(c, 1), :, :].rearrange("p a h n -> p (a h) n"),
                                                 t1[:], bank(3), ALU.add))
                    step(nc.vector.tensor_tensor(S[:], S[:], bank(4), ALU.add))

                @block.scalar
                def _(act):
                    nc.scalar.copy(qk[:], conv[:, 0:2 * H, ds(c * P, P)])
                    nc.scalar.copy(kc[:], kn[:, ds(c, 1), :, :].rearrange("p a h n -> p (a h) n")).then_inc(fetched, 1)
                    act.wait_ge(vec, V["gc"])
                    nc.scalar.activation(ex[:, 0:2, :].rearrange("p a h -> p (a h)"), gc[:], ACT.Exp).then_inc(exps, 1)
                    nc.scalar.activation(ex[:, 2, :], dif[:], ACT.Exp).then_inc(exps, 1)
                    act.wait_ge(vec, V["diffs"])
                    nc.scalar.activation(e1[:], e1[:], ACT.Exp).then_inc(exps, 1)
                    nc.scalar.activation(e2[:], e2[:], ACT.Exp).then_inc(exps, 2)

                @block.tensor
                def _(pe):
                    def heads(bank_no, lhs, rhs):
                        for h in range(H):
                            last = nc.tensor.matmul(bank(bank_no)[:, h, :], lhs(h), rhs(h), start=True, stop=True)
                        return last
                    pe.wait_ge(vec, V["g_spread"])
                    heads(0, lambda h: gbc[:, h, :], lambda h: g.triu)
                    nc.tensor.matmul(g.ps[:, 1, 0:H], g.triu, gg, start=True, stop=True)
                    nc.tensor.matmul(g.ps[:, 1, H:2 * H], g.ones, gg, start=True, stop=True).then_inc(sums, 1)
                    pe.wait_ge(fetched, 1)
                    heads(2, lambda h: tok(H + h), lambda h: tok(H + h))
                    heads(3, lambda h: tok(H + h), lambda h: tok(h)).then_inc(grams, 1)
                    pe.wait_ge(vec, V["low"])
                    for h in range(H):
                        last = nc.tensor.transpose(bank(4)[:, h, :], low[:, h, :], g.ident)
                    last.then_inc(grams, 1)
                    for s in range(7):
                        pe.wait_ge(vec, V[f"lev{s}"])
                        heads(5, lambda h: lev[:, h, :], lambda h: M[:, h, :]).then_inc(level_p, 1)
                        pe.wait_ge(vec, V[f"P{s}"])
                        heads(6, lambda h: MT[:, h, :], lambda h: Pm[:, h, :])
                        heads(7, lambda h: Pm[:, h, :], lambda h: MT[:, h, :]).then_inc(level_m, 1)
                    heads(0, lambda h: tok(H + h), lambda h: S[:, h, :])
                    heads(1, lambda h: tok(h), lambda h: S[:, h, :]).then_inc(state_read, 1)
                    pe.wait_ge(vec, V["rhs"])
                    heads(2, lambda h: MT[:, h, :], lambda h: r[:, h, :]).then_inc(solved, 1)
                    pe.wait_ge(vec, V["vs"])
                    heads(3, lambda h: aq[:, h, :], lambda h: vnew[:, h, :])
                    heads(4, lambda h: kc[:, h, :], lambda h: vs[:, h, :]).then_inc(out_ready, 1)
        with stage(g, "stored") as (block, stored):
            @block.sync
            def _(sp):
                sp.dma_start(d["p_delta"].rearrange("l b h k v -> k (l b) h v")[:, ds(l, 1), :, :]
                             .rearrange("k a h v -> k (a h) v"), S[:]).then_inc(stored, 16)
                sp.wait_ge(stored, 16)


def delta_sample(g, l, d, conv, gb, o_all):
    nc = g.nc
    N = B * H
    with ExitStack() as ctx:
        def sb(name, *shape):
            return ctx.enter_context(g.buffer(name, shape, FP32))
        S = sb("states", P, N, DK)
        ud = sb("u_blocks", N, N, DK)
        rows = sb("rows", N, 2, P)
        kq = sb("kq", P, N, 2)
        vv = sb("vv", P, N)
        ab = sb("ab", P, B, 2 * H)
        eg = sb("eg", P, B, H)
        bb = sb("bb", P, B, H)
        prod = sb("prod", P, N)
        u = sb("u", P, N)
        t1 = sb("t1s", P, N)
        o = sb("o_s", P, H, B)

        def bh(x):
            return x.rearrange("p (b h) -> p b h", b=B)

        def cols(first):
            return conv[:, first:first + H, T:TOK].rearrange("p h b -> p b h")
        with stage(g, "states_in", "ab_out", "ab_in", "exped", "stored") as (
                block, states_in, ab_out, ab_in, exped, stored):
            @block.sync
            def _(sp):
                sp.dma_start(g.scratch_ab, gb[0:B, TT, :]).then_inc(ab_out, 16)
                for n in range(0, N, 8):
                    sp.dma_start(S[:, n:n + 8, :], d["state_delta"].rearrange("l b h k v -> k (l b h) v")
                                 [:, ds(l * N + n, 8), :]).then_inc(states_in, 16)
                sp.wait_ge(ab_out, 16)
                sp.dma_start(ab[:].rearrange("p b x -> p (b x)"),
                             g.scratch_ab.rearrange("(a b) x -> a (b x)", a=1).to_broadcast([P, B * 2 * H])
                             ).then_inc(ab_in, 16)
                sp.wait_ge(states_in, 4 * 16)
                sp.wait_ge(ab_in, 16)

            @block.scalar
            def _(act):
                act.wait_ge(ab_in, 16)
                nc.scalar.activation(eg[:], ab[:, :, 0:H], ACT.Exp)
                nc.scalar.copy(bb[:], ab[:, :, H:2 * H])

            @block.vector
            def _(dve):
                nc.vector.memset(o_all[:, TT, :, :], 0.0)
                nc.vector.tensor_copy(kq[:].rearrange("p (b h) x -> p b h x", b=B)[:, :, :, 0], cols(H))
                nc.vector.tensor_copy(kq[:].rearrange("p (b h) x -> p b h x", b=B)[:, :, :, 1], cols(0))
                nc.vector.tensor_copy(bh(vv[:]), cols(2 * H))
        with stage(g, "vec", "multiplied", "turned", "outer", "o_turned", "stored") as (
                block, vec, multiplied, turned, outer, o_turned, stored):
            egf = eg[:].rearrange("p b h -> p (b h)")
            bbf = bb[:].rearrange("p b h -> p (b h)")
            dots = g.ps[:, 0, 0:2 * N].rearrange("p (n x) -> p n x", x=2)

            @block.vector
            def _(dve):
                step = in_order(dve, vec)
                step(nc.vector.tensor_tensor(prod[:], kq[:, :, 0], kq[:, :, 1], ALU.mult))
                dve.wait_ge(multiplied, 1)
                step(nc.vector.tensor_tensor(t1[:], dots[:, :, 0], egf, ALU.mult))
                step(nc.vector.tensor_tensor(t1[:], vv[:], t1[:], ALU.subtract))
                step(nc.vector.tensor_tensor(u[:], t1[:], bbf, ALU.mult))
                step(nc.vector.tensor_tensor(t1[:], dots[:, :, 1], egf, ALU.mult))
                step(nc.vector.tensor_tensor(prod[:], u[:], g.ps[:, 1, 0:N], ALU.mult))
                step(nc.vector.tensor_tensor(o[:].rearrange("p h b -> p b h"), bh(t1[:]), bh(prod[:]), ALU.add))
                step(nc.vector.tensor_tensor(S[:], S[:], egf.unsqueeze(2).to_broadcast([P, N, DK]), ALU.mult))
                dve.wait_ge(turned, 1)
                step(nc.vector.tensor_copy(rows[:].rearrange("n a x -> n (a x)"), g.ps[0:N, 2, 0:2 * P]))
                step(nc.vector.tensor_tensor(ud[:], rows[:, 1:2, :].to_broadcast([N, N, DK]),
                                             g.ident[0:N, 0:N].unsqueeze(2).to_broadcast([N, N, DK]), ALU.mult))
                for i in range(N // 4):
                    dve.wait_ge(outer, i + 1)
                    step(nc.vector.tensor_tensor(S[:, 4 * i:4 * i + 4, :], S[:, 4 * i:4 * i + 4, :],
                                                 g.ps[:, 4 + i % 4, :].rearrange("p (n v) -> p n v", n=4), ALU.add))
                dve.wait_ge(o_turned, 1)
                nc.vector.tensor_copy(o_all[0:B, TT, :, :].rearrange("b h v -> b (h v)"), g.ps[0:B, 3, :])

            @block.tensor
            def _(pe):
                for n in range(N):
                    nc.tensor.matmul(dots[:, n, :], S[:, n, :], kq[:, n, :], start=True, stop=True)
                pe.wait_ge(vec, 1)
                nc.tensor.matmul(g.ps[:, 1, 0:N], g.ones, prod[:], start=True, stop=True).then_inc(multiplied, 1)
                pe.wait_ge(vec, 7)
                nc.tensor.transpose(g.ps[0:N, 2, 0:P], kq[:, :, 0], g.ident)
                nc.tensor.transpose(g.ps[0:N, 2, P:2 * P], u[:], g.ident).then_inc(turned, 1)
                for h in range(H):
                    last = nc.tensor.transpose(g.ps[0:B, 3, h * P:(h + 1) * P], o[:, h, :], g.ident)
                last.then_inc(o_turned, 1)
                for i in range(N // 4):
                    pe.wait_ge(vec, 10 if i < 4 else 10 + i - 3)
                    nc.tensor.matmul(g.ps[:, 4 + i % 4, :], rows[:, 0, :],
                                     ud[:, 4 * i:4 * i + 4, :].rearrange("p n v -> p (n v)"),
                                     start=True, stop=True).then_inc(outer, 1)

            @block.sync
            def _(sp):
                sp.wait_ge(vec, 10 + N // 4)
                sp.dma_start(d["s_delta"].rearrange("l b h k v -> k (l b h) v")[:, ds(l * N, N), :], S[:]).then_inc(stored, 16)
                sp.wait_ge(stored, 16)


def turn_tokens(g, src, dst, tiles):
    nc = g.nc
    with stage(g, "turned", "copied") as (block, turned, copied):
        @block.tensor
        def _(pe):
            for t in range(tiles):
                if t >= 2:
                    pe.wait_ge(copied, t - 1)
                for k in range(4):
                    last = nc.tensor.transpose(g.ps[:, t % 2, k * P:(k + 1) * P], src(t, k), g.ident)
                last.then_inc(turned, 1)

        @block.scalar
        def _(act):
            for t in range(tiles):
                act.wait_ge(turned, t + 1)
                nc.scalar.copy(dst[:, :, t * P:(t + 1) * P],
                               g.ps[:, t % 2, :].rearrange("p (k n) -> p k n", k=4)).then_inc(copied, 1)


def delta_output(g, l, d, o_all, ot):
    nc = g.nc
    G = NT * H
    with ExitStack() as ctx:
        def sb(name, *shape):
            return ctx.enter_context(g.buffer(name, shape, FP32))
        sq = sb("sqo", P, NT, H * DK)
        gain = sb("gaino", P, DK)
        ss = sb("sso", P, 4, G)
        of = o_all[:].rearrange("p t h v -> p (t h) v")
        sqf = sq[:].rearrange("p t (h v) -> p (t h) v", h=H)
        with stage(g, "gain_in", "vec", "act_done") as (block, gain_in, vec, act_done):
            @block.sync
            def _(sp):
                sp.dma_start(gain[:], d["dn_norm"][ds(l, 1), :].to_broadcast([P, DK])).then_inc(gain_in, 16)

            @block.vector
            def _(dve):
                step = in_order(dve, vec)
                step(nc.vector.tensor_tensor(sqf, of, of, ALU.mult))
                step(nc.vector.tensor_reduce(ss[:, 0, :], sqf, AX.X, ALU.add))
                step(nc.vector.tensor_scalar(ss[:, 1, :], ss[:, 0, :], 1.0 / DK, EPS, ALU.mult, ALU.add))
                dve.wait_ge(act_done, 2)
                step(nc.vector.reciprocal(ss[:, 3, :], ss[:, 2, :]))
                step(nc.vector.tensor_tensor(of, of, ss[:, 3, :].unsqueeze(2).to_broadcast([P, G, DK]), ALU.mult))
                dve.wait_ge(gain_in, 16)
                step(nc.vector.tensor_tensor(of, of, gain[:].unsqueeze(1).to_broadcast([P, G, DK]), ALU.mult))
                o3 = o_all[:].rearrange("p t h v -> p t (h v)")
                step(nc.vector.tensor_tensor(sq[:], sq[:], g.nat[:, :, 0:H * DK], ALU.mult))
                step(nc.vector.tensor_tensor(o3, o3, sq[:], ALU.mult))

            @block.scalar
            def _(act):
                act.wait_ge(vec, 3)
                nc.scalar.activation(ss[:, 2, :], ss[:, 1, :], ACT.Sqrt).then_inc(act_done, 1)
                nc.scalar.activation(sq[:], g.nat[:, :, 0:H * DK], ACT.Sigmoid).then_inc(act_done, 1)
        turn_tokens(g, lambda t, k: o_all[:, t, k, :], ot, NT)



def rotary(g, l, d):
    nc = g.nc
    with ExitStack() as ctx:
        tmp = ctx.enter_context(g.buffer("rot", [P, 4, NT, AH + KV, HALF], FP32))
        with stage(g, "vec", "stored") as (block, vec, stored):
            @block.vector
            def _(dve):
                step = in_order(dve, vec)
                for first, heads in ((N_Q, AH + KV), (N_QI, IH + 1)):
                    v = g.nat[:, :, first:first + heads * HD].rearrange("p t (h e) -> p t h e", e=HD)
                    x1, x2 = v[:, :, :, 0:HALF], v[:, :, :, HALF:ROT]
                    cos = g.cos.unsqueeze(2).to_broadcast([P, NT, heads, HALF])
                    sin = g.sin.unsqueeze(2).to_broadcast([P, NT, heads, HALF])
                    for t in range(NT):
                        for n, (x, y) in enumerate(((x1, cos), (x2, sin), (x2, cos), (x1, sin))):
                            step(nc.vector.tensor_tensor(tmp[:, n, t, 0:heads, :], x[:, t], y[:, t], ALU.mult))
                        step(nc.vector.tensor_tensor(x1[:, t], tmp[:, 0, t, 0:heads, :], tmp[:, 1, t, 0:heads, :], ALU.subtract))
                        step(nc.vector.tensor_tensor(x2[:, t], tmp[:, 2, t, 0:heads, :], tmp[:, 3, t, 0:heads, :], ALU.add))

            @block.sync
            def _(sp):
                sp.wait_ge(vec, 2 * 6 * NT)
                for dst, c0, w in ((d["p_k"].rearrange("a (t p) l k e -> p (a t) l (k e)", p=P), N_K, KV * HD),
                                   (d["p_v"].rearrange("a (t p) l k e -> p (a t) l (k e)", p=P), N_V, KV * HD),
                                   (d["p_kidx"].rearrange("a (t p) l e -> p (a t) l e", p=P), N_KI, ID)):
                    sp.dma_start(dst[:, :, ds(l, 1), :].rearrange("p t a e -> p t (a e)"),
                                 g.nat[:, 0:TT, c0:c0 + w]).then_inc(stored, 16)
                for dst, c0, w in ((d["s_k"].rearrange("b a l k e -> (b a) l (k e)"), N_K, KV * HD),
                                   (d["s_v"].rearrange("b a l k e -> (b a) l (k e)"), N_V, KV * HD),
                                   (d["s_kidx"].rearrange("b a l e -> (b a) l e"), N_KI, ID)):
                    sp.dma_start(dst[:, ds(l, 1), :].rearrange("b a e -> b (a e)"),
                                 g.nat[0:B, TT, c0:c0 + w]).then_inc(stored, 16)
                sp.wait_ge(stored, 6 * 16)


def sparse_prompt(g, l, d, oat):
    nc = g.nc
    with ExitStack() as ctx:
        def sb(name, *shape):
            return ctx.enter_context(g.buffer(name, shape, FP32))
        kT = sb("kT", HD, KV, T)
        kiT = sb("kiT", ID, T)
        oa = sb("oa", P, TT, AH * HD)
        with stage(g, "turned", "copied") as (block, turned, copied):
            @block.tensor
            def _(pe):
                for n, c0 in enumerate((N_K, N_K + HD, N_KI)):
                    for t in range(TT):
                        last = nc.tensor.transpose(g.ps[0:HD, n, t * P:(t + 1) * P], g.nat[:, t, c0:c0 + HD], g.ident)
                    last.then_inc(turned, 1)

            @block.vector
            def _(dve):
                for n, dst in enumerate((kT[:, 0, :], kT[:, 1, :], kiT[:])):
                    dve.wait_ge(turned, n + 1)
                    nc.vector.tensor_copy(dst, g.ps[0:HD, n, :])
        with ExitStack() as inner:
            def sbi(name, *shape):
                return inner.enter_context(g.buffer(name, shape, FP32))
            qc = sbi("qc", P, AH * HD)
            qic = sbi("qic", P, IH * ID)
            wic = sbi("wic", P, IH)
            qT = sbi("qT", HD, AH, P)
            qiT = sbi("qiT", ID, IH, P)
            rl = sbi("rl", P, IH, T)
            cm = sbi("cm", P, T)
            acc = sbi("acc", P, T)
            work = sbi("work", P, T)
            pen = sbi("pen", P, T)
            m8 = sbi("m8", P, 2, 8)
            pr = sbi("pr", P, 2, T)
            nm = sbi("nm", P, AH)
            sums = sbi("sums", P, AH)
            pT = sbi("pT", P, 2, TT, P)
            with nc.Fori(0, TT) as qt:
                with stage(g, "fetched", "turned", "back", "scored", "relued", "vec", "multiplied", "shifted", "exped",
                           "p_turned", "p_back", "out_ready") as (
                               block, fetched, turned, back, scored, relued, vec, multiplied, shifted, exped,
                               p_turned, p_back, out_ready):
                    @block.scalar
                    def _(act):
                        def cols(c0, w):
                            return g.nat[:, ds(qt, 1), c0:c0 + w].rearrange("p a n -> p (a n)")
                        nc.scalar.copy(qc[:], cols(N_Q, AH * HD))
                        nc.scalar.copy(qic[:], cols(N_QI, IH * ID))
                        nc.scalar.mul(wic[:], cols(N_WI, IH), IH ** -0.5).then_inc(fetched, 1)
                        act.wait_ge(turned, 1)
                        for b in range(2):
                            nc.scalar.copy(qT[:, 4 * b:4 * b + 4, :].rearrange("p h n -> p (h n)"), g.ps[0:HD, b, :])
                        nc.scalar.copy(qiT[:].rearrange("p h n -> p (h n)"), g.ps[0:ID, 2, :]).then_inc(back, 1)
                        for h in range(IH):
                            act.wait_ge(scored, h + 1)
                            nc.scalar.activation(rl[:, h, :], g.ps[:, 4 + h, :], ACT.Relu, scale=ID ** -0.5).then_inc(relued, 1)
                        for h in range(AH):
                            act.wait_ge(shifted, h + 1)
                            nc.scalar.activation(pr[:, h % 2, :], pr[:, h % 2, :], ACT.Exp, bias=nm[:, h:h + 1],
                                                 accum_out=sums[:, h:h + 1]).then_inc(exped, 1)
                            act.wait_ge(p_turned, h + 1)
                            nc.scalar.copy(pT[:, h % 2, :, :].rearrange("p k n -> p (k n)"),
                                           g.ps[:, 4 + h % 2, :]).then_inc(p_back, 1)

                    @block.tensor
                    def _(pe):
                        pe.wait_ge(fetched, 1)
                        for h in range(AH):
                            nc.tensor.transpose(g.ps[0:HD, h // 4, (h % 4) * P:(h % 4 + 1) * P],
                                                qc[:, h * HD:(h + 1) * HD], g.ident)
                        for h in range(IH):
                            last = nc.tensor.transpose(g.ps[0:ID, 2, h * P:(h + 1) * P], qic[:, h * ID:(h + 1) * ID], g.ident)
                        last.then_inc(turned, 1)
                        pe.wait_ge(back, 1)
                        for h in range(IH):
                            nc.tensor.matmul(g.ps[:, 4 + h, :], qiT[:, h, :], kiT[:], start=True, stop=True).then_inc(scored, 1)

                        def scores(h):
                            nc.tensor.matmul(g.ps[:, h % 4, :], qT[:, h, :], kT[:, h // (AH // KV), :],
                                             start=True, stop=True).then_inc(multiplied, 1)
                        for h in range(4):
                            scores(h)
                        pe.wait_ge(relued, IH)
                        for h in range(AH):
                            pe.wait_ge(exped, h + 1)
                            if h >= 2:
                                pe.wait_ge(p_back, h - 1)
                            for k in range(TT):
                                last = nc.tensor.transpose(g.ps[:, 4 + h % 2, k * P:(k + 1) * P],
                                                           pr[:, h % 2, k * P:(k + 1) * P], g.ident)
                            last.then_inc(p_turned, 1)
                            if h + 4 < AH:
                                scores(h + 4)
                            pe.wait_ge(p_back, h + 1)
                            c0 = N_V + (h // (AH // KV)) * HD
                            for k in range(TT):
                                last = nc.tensor.matmul(g.ps[:, 6, h * HD:(h + 1) * HD], pT[:, h % 2, k, :],
                                                        g.nat[:, k, c0:c0 + HD], start=(k == 0), stop=(k == TT - 1))
                            if h == AH - 1:
                                last.then_inc(out_ready, 1)

                    @block.vector
                    def _(dve):
                        step = in_order(dve, vec)
                        step(nc.vector.tensor_scalar(cm[:], g.iota512, g.tpos[:, ds(qt, 1)], None, ALU.is_le))
                        step(nc.vector.tensor_scalar(pen[:], cm[:], -1.0, BIG, ALU.add, ALU.mult))
                        dve.wait_ge(fetched, 1)
                        for h in range(IH):
                            dve.wait_ge(relued, h + 1)
                            if h == 0:
                                step(nc.vector.tensor_scalar(acc[:], rl[:, h, :], wic[:, h:h + 1], 0.0, ALU.mult, ALU.add))
                            else:
                                step(nc.vector.scalar_tensor_tensor(acc[:], rl[:, h, :], wic[:, h:h + 1], acc[:],
                                                                    ALU.mult, ALU.add))
                        step(nc.vector.tensor_tensor(acc[:], acc[:], cm[:], ALU.mult))
                        step(nc.vector.tensor_tensor(work[:], acc[:], pen[:], ALU.add))
                        for r in range(TOPK_P // 8):
                            step(nc.vector.max(m8[:, r % 2, :], work[:]))
                            step(nc.vector.match_replace(work[:], m8[:, r % 2, :], work[:], TAKEN))
                        step(nc.vector.tensor_scalar(work[:], work[:], -3.2e38, None, ALU.is_le))
                        step(nc.vector.tensor_tensor(work[:], work[:], cm[:], ALU.mult))
                        step(nc.vector.tensor_scalar(pen[:], work[:], -1.0, 1.0e30, ALU.add, ALU.mult))
                        for h in range(AH):
                            dve.wait_ge(multiplied, h + 1)
                            if h >= 2:
                                dve.wait_ge(p_turned, h - 1)
                            step(nc.vector.scalar_tensor_tensor(pr[:, h % 2, :], g.ps[:, h % 4, :], HD ** -0.5, pen[:],
                                                                ALU.mult, ALU.add))
                            nc.vector.tensor_reduce(nm[:, h:h + 1], pr[:, h % 2, :], AX.X, ALU.max,
                                                    negate=True).then_inc(shifted, 1)
                        dve.wait_ge(exped, AH)
                        step(nc.vector.reciprocal(sums[:], sums[:]))
                        dve.wait_ge(out_ready, 1)
                        nc.vector.tensor_tensor(
                            oa[:, ds(qt, 1), :].rearrange("p a (h e) -> p (a h) e", e=HD),
                            g.ps[:, 6, :].rearrange("p (h e) -> p h e", e=HD),
                            sums[:].unsqueeze(2).to_broadcast([P, AH, HD]), ALU.mult)
        turn_tokens(g, lambda t, k: oa[:, t, k * P:(k + 1) * P], oat, TT)


def softmax_rows(g, rows, width, s, small, sem_names=("vec", "exped")):
    nc = g.nc
    with stage(g, *sem_names) as (block, vec, exped):
        @block.vector
        def _(dve):
            step = in_order(dve, vec)
            step(nc.vector.tensor_reduce(small[0:rows, 0:1], s[:], AX.X, ALU.max, negate=True))
            dve.wait_ge(exped, 1)
            step(nc.vector.reciprocal(small[0:rows, 2:3], small[0:rows, 1:2]))
            nc.vector.tensor_scalar(s[:], s[:], small[0:rows, 2:3], None, ALU.mult)

        @block.scalar
        def _(act):
            act.wait_ge(vec, 1)
            nc.scalar.activation(s[:], s[:], ACT.Exp, bias=small[0:rows, 0:1],
                                 accum_out=small[0:rows, 1:2]).then_inc(exped, 1)


def sparse_sample(g, l, d, oat):
    nc = g.nc
    GRP = 4
    NG = PAGES // GRP
    HALVES = TOPK_S // P
    KEYS = PAST + 8
    with ExitStack() as ctx:
        def sb(name, *shape, dt=FP32):
            return ctx.enter_context(g.buffer(name, shape, dt))
        qb = sb("qb", P, B * (B + 1) * AH)
        score = sb("score", B, KEYS)
        rows = sb("addresses", P, HALVES, B, dt=I32)
        fresh = sb("fresh", P, HALVES, B)
        small = sb("small", P, 4)

        def diag(buf, w):
            return buf.rearrange("p (b x) -> p b x", x=(B + 1) * w)[:, :, 0:w]

        def q_nat(g4):
            return g.nat[0:B, TT, N_Q:N_Q + AH * HD].rearrange("p (k g e) -> p g k e", k=KV, e=HD)[:, g4]

        with ExitStack() as inner:
            def sbi(name, *shape, dt=FP32):
                return inner.enter_context(g.buffer(name, shape, dt))
            qiz = [sbi(f"qiz{n}", P, B * (B + 1) * IH) for n in range(2)]
            ki = sbi("ki", P, 2, B * GRP, ID)
            kiT = sbi("kiT_s", P, 2, GRP // 2, P)
            relu = sbi("relu", P, 2, GRP * P)
            qi2 = sbi("qi2", B, IH, 2, ID)
            wcol = sbi("wcol", B * IH, 1)
            wsel = sbi("wsel", P, B)
            q4 = sbi("q4", B, 4, KV * HD)
            with stage(g, "vec", "turned", "w_out", "w_in", "cleared") as (block, vec, turned, w_out, w_in, cleared):
                @block.sync
                def _(sp):
                    sp.dma_start(g.scratch_w, g.nat[0:B, TT, N_WI:N_WI + IH]).then_inc(w_out, 16)
                    sp.dma_start(g.scratch_kv, g.nat[0:B, TT, N_K:N_K + 2 * KV * HD]).then_inc(w_out, 16)
                    sp.wait_ge(w_out, 32)
                    sp.dma_start(wcol[:], g.scratch_w.rearrange("b (h a) -> (b h) a", a=1)).then_inc(w_in, 16)

                @block.vector
                def _(dve):
                    step = in_order(dve, vec)
                    for x in range(4):
                        step(nc.vector.tensor_copy(q4[:, x, :].rearrange("b (k e) -> b k e", k=KV), q_nat(x)))
                    step(nc.vector.memset(qb[:], 0.0))
                    for n in range(2):
                        step(nc.vector.memset(qiz[n][:], 0.0))
                        step(nc.vector.tensor_copy(qi2[:, :, n, :], g.nat[0:B, TT, N_QI:N_QI + IH * ID]
                                                   .rearrange("b (h e) -> b h e", h=IH)))
                    step(nc.vector.memset(wsel[:], 0.0))
                    step(nc.vector.memset(relu[:], 0.0))
                    dve.wait_ge(turned, 1)
                    for k in range(KV):
                        nc.vector.tensor_copy(
                            diag(qb, AH)[k * HD:(k + 1) * HD, :, 4 * k:4 * k + 4],
                            g.ps[k * HD:(k + 1) * HD, 0, 0:4 * B].rearrange("p (x b) -> p b x", b=B))
                    for n in range(2):
                        nc.vector.tensor_copy(
                            diag(qiz[n], IH)[n * ID:(n + 1) * ID],
                            g.ps[n * ID:(n + 1) * ID, 1, 0:IH * B].rearrange("p (h b) -> p b h", b=B))
                    dve.wait_ge(w_in, 16)
                    nc.vector.tensor_scalar(wsel[0:B * IH, :], g.own[0:B * IH, :], wcol[:], IH ** -0.5, ALU.mult, ALU.mult)

                @block.tensor
                def _(pe):
                    pe.wait_ge(vec, 9)
                    for x in range(4):
                        nc.tensor.transpose(g.ps[:, 0, x * B:(x + 1) * B], q4[:, x, :], g.ident[0:B, 0:B])
                    for h in range(IH):
                        last = nc.tensor.transpose(g.ps[:, 1, h * B:(h + 1) * B],
                                                   qi2[:, h].rearrange("b a e -> b (a e)"), g.ident[0:B, 0:B])
                    last.then_inc(turned, 1)

            with stage(g, "ki_in0", "ki_in1", "turned", "back", "dotted", "relued", "weighed", "kept") as (
                    block, ki_in0, ki_in1, turned, back, dotted, relued, weighed, kept):
                ki_in = (ki_in0, ki_in1)

                def load(eng, c, u, q):
                    for b in range(q * (B // 2), (q + 1) * (B // 2)):
                        for pg in range(GRP):
                            page = eng.value_load(g.pages[0:1, ds(c * GRP + (b * PAGES + pg), 1)],
                                                  min_val=0, max_val=d["cache_kidx"].shape[0] - 1)
                            eng.dma_start(ki[:, u, b * GRP + pg, :],
                                          d["cache_kidx"][ds(page, 1), :, ds(l, 1), :].rearrange("a s b e -> (a s) (b e)")
                                          ).then_inc(ki_in[u], 16)

                @block.sync
                def _(sp):
                    for u in range(2):
                        for q in range(2):
                            load(sp, u, u, q)
                    with sp.Fori(1, NG // 2) as it:
                        for u in range(2):
                            sp.wait_ge(turned, (it - 1) * (2 * B) + (u + 1) * B)
                            for q in range(2):
                                load(sp, it * 2 + u, u, q)

                @block.tensor
                def _(pe):
                    with pe.Fori(0, NG // 2) as it:
                        for u in range(2):
                            pe.wait_ge(ki_in[u], it * (16 * B * GRP) + 16 * B * GRP)

                            def dots(b):
                                pe.wait_ge(back, it * (2 * B) + (u * B + b + 1))
                                for n in range(2):
                                    last = nc.tensor.matmul(
                                        g.ps[0:B * IH, 4 + 2 * u + n, 0:GRP * P // 2], qiz[n][:, b * B * IH:(b + 1) * B * IH],
                                        kiT[:, b % 2].rearrange("p a s -> p (a s)"), start=(b == 0), stop=(b == B - 1))
                                return last
                            for b in range(B):
                                for a in range(GRP // 2):
                                    pair = ki[:, u, b * GRP + 2 * a:b * GRP + 2 * a + 2, :]
                                    last = nc.tensor.transpose(g.ps[:, b % 2, a * P:(a + 1) * P],
                                                               pair.rearrange("p n e -> p (n e)"), g.ident)
                                last.then_inc(turned, 1)
                                if b >= 1:
                                    last = dots(b - 1)
                            dots(B - 1).then_inc(dotted, 1)
                            pe.wait_ge(relued, it * 2 + (u + 1))
                            nc.tensor.matmul(g.ps[0:B, 2 + u, :], wsel[:], relu[:, u, :], start=True,
                                             stop=True).then_inc(weighed, 1)

                @block.scalar
                def _(act):
                    with act.Fori(0, NG // 2) as it:
                        for n in range(2 * B):
                            act.wait_ge(turned, it * (2 * B) + (n + 1))
                            nc.scalar.copy(kiT[:, n % 2].rearrange("p a s -> p (a s)"),
                                           g.ps[:, n % 2, 0:GRP * P // 2]).then_inc(back, 1)

                @block.vector
                def _(dve):
                    with dve.Fori(0, NG // 2) as it:
                        for u in range(2):
                            dve.wait_ge(dotted, it * 2 + (u + 1))
                            for n in range(2):
                                last = nc.vector.tensor_scalar(
                                    relu[0:B * IH, u, :].rearrange("p (a n s) -> p a n s", n=2, s=P)[:, :, n],
                                    g.ps[0:B * IH, 4 + 2 * u + n, 0:GRP * P // 2].rearrange("p (a s) -> p a s", s=P),
                                    ID ** -0.5, 0.0, ALU.mult, ALU.max)
                            last.then_inc(relued, 1)
                            dve.wait_ge(weighed, it * 2 + (u + 1))
                            nc.vector.tensor_scalar(score[:, ds((it * 2 + u) * (GRP * P), GRP * P)], g.ps[0:B, 2 + u, :],
                                                    0.0, None, ALU.add).then_inc(kept, 1)

        with ExitStack() as inner:
            def sbi(name, *shape, dt=FP32):
                return inner.enter_context(g.buffer(name, shape, dt))
            own = sbi("own", B, IH, ID)
            owns = sbi("owns", B, 4, IH)
            m8 = sbi("m8s", B, 8)
            i8 = sbi("i8", B, 8, dt=U32)
            pos = sbi("pos", B, TOPK_S)
            with stage(g, "vec") as (block, vec):
                @block.vector
                def _(dve):
                    step = in_order(dve, vec)
                    qi = g.nat[0:B, TT, N_QI:N_QI + IH * ID].rearrange("b (h e) -> b h e", h=IH)
                    kx = g.nat[0:B, TT:TT + 1, N_KI:N_KI + ID].to_broadcast([B, IH, ID])
                    step(nc.vector.tensor_tensor(own[:], qi, kx, ALU.mult))
                    step(nc.vector.tensor_reduce(owns[:, 0, :], own[:], AX.X, ALU.add))
                    step(nc.vector.tensor_scalar(owns[:, 1, :], owns[:, 0, :], ID ** -0.5, 0.0, ALU.mult, ALU.max))
                    step(nc.vector.tensor_scalar(owns[:, 2, :], g.nat[0:B, TT, N_WI:N_WI + IH], IH ** -0.5, None, ALU.mult))
                    step(nc.vector.tensor_tensor(owns[:, 3, :], owns[:, 1, :], owns[:, 2, :], ALU.mult))
                    step(nc.vector.tensor_reduce(owns[:, 0, 0:1], owns[:, 3, :], AX.X, ALU.add))
                    step(nc.vector.memset(score[:, PAST:KEYS], -BIG))
                    step(nc.vector.tensor_scalar(score[:, PAST:PAST + 1], owns[:, 0, 0:1], 0.0, None, ALU.add))
                    step(nc.vector.engine_nop())
                    dve.sem_clear(vec)
                    with dve.Fori(0, TOPK_S // 8) as r:
                        step = in_order(dve, vec)
                        step(nc.vector.max(m8[:], score[:]))
                        step(nc.vector.max_index(i8[:], m8[:], score[:]))
                        step(nc.vector.match_replace(score[:], m8[:], score[:], TAKEN))
                        step(nc.vector.tensor_copy(pos[:, ds(r * 8, 8)], i8[:]))
                        dve.sem_clear(vec)
            posT = sbi("posT", P, HALVES * B)
            posi = sbi("posi", P, 3, HALVES * B, dt=I32)
            posf = sbi("posf", P, 3, HALVES * B)
            hot = sbi("hot", P, HALVES, B, PAGES)
            pti = sbi("pti", P, B * PAGES, dt=I32)
            ptf = sbi("ptf", P, B * PAGES)
            with stage(g, "table_in", "turned", "vec") as (block, table_in, turned, vec):
                @block.sync
                def _(sp):
                    sp.dma_start(pti[:], d["page_table"].rearrange("(a b) n -> a (b n)", a=1).to_broadcast([P, B * PAGES])
                                 ).then_inc(table_in, 16)

                @block.tensor
                def _(pe):
                    for x in range(HALVES):
                        last = nc.tensor.transpose(g.ps[:, 0, x * B:(x + 1) * B], pos[:, x * P:(x + 1) * P], g.ident[0:B, 0:B])
                    last.then_inc(turned, 1)

                @block.vector
                def _(dve):
                    step = in_order(dve, vec)
                    dve.wait_ge(table_in, 16)
                    step(nc.vector.tensor_copy(ptf[:], pti[:]))
                    dve.wait_ge(turned, 1)
                    step(nc.vector.tensor_copy(posi[:, 0, :], g.ps[:, 0, 0:HALVES * B]))
                    step(nc.vector.tensor_scalar(fresh[:].rearrange("p x b -> p (x b)"), g.ps[:, 0, 0:HALVES * B],
                                                 float(PAST), None, ALU.is_ge))
                    step(nc.vector.tensor_scalar(posi[:, 1, :], posi[:, 0, :], 7, None, ALU.logical_shift_right))
                    step(nc.vector.tensor_scalar(posi[:, 2, :], posi[:, 0, :], PAGE - 1, None, ALU.bitwise_and))
                    step(nc.vector.tensor_copy(posf[:, 0:2, :], posi[:, 1:3, :]))
                    for x in range(HALVES):
                        step(nc.vector.tensor_tensor(
                            hot[:, x], posf[:, 0, x * B:(x + 1) * B].unsqueeze(2).to_broadcast([P, B, PAGES]),
                            g.iota[:, 0:PAGES].unsqueeze(1).to_broadcast([P, B, PAGES]), ALU.is_equal))
                        step(nc.vector.tensor_tensor(hot[:, x], hot[:, x], ptf[:].rearrange("p (b n) -> p b n", b=B), ALU.mult))
                    step(nc.vector.tensor_reduce(posT[:], hot[:].rearrange("p x b n -> p (x b) n"), AX.X, ALU.add))
                    step(nc.vector.scalar_tensor_tensor(posT[:], posT[:], float(PAGE), posf[:, 1, :], ALU.mult, ALU.add))
                    step(nc.vector.tensor_scalar(posT[:], posT[:], float(DEPTH), g.layer[:], ALU.mult, ALU.add))
                    step(nc.vector.tensor_copy(rows[:].rearrange("p x b -> p (x b)"), posT[:]))
        with ExitStack() as inner:
            def sbi(name, *shape, dt=FP32):
                return inner.enter_context(g.buffer(name, shape, dt))
            ks = sbi("k_sel", P, B, HALVES, KV * HD)
            vs = sbi("v_sel", P, B, HALVES, KV * HD)
            new = sbi("kv_new", P, B, 2, KV * HD)
            tmp = sbi("tmp_sel", P, B, KV * HD)
            old = sbi("old", P, HALVES, B)
            ksT = sbi("k_selT", P, 2, 2 * TOPK_S)
            sc = sbi("sc", B * AH, TOPK_S)
            pT = sbi("pT_s", P, HALVES, B * AH)
            all_rows = 16 * 2 * B * HALVES
            with stage(g, "new_in", "vec") as (block, new_in, vec):
                @block.gpsimd
                def _(pool):
                    for x in range(HALVES):
                        for b in range(B):
                            for dst, src in ((ks, d["cache_k"]), (vs, d["cache_v"])):
                                nc.gpsimd.indirect_dma_start(
                                    dst[:, b, x, :], None, src.rearrange("n s l k e -> (n s l) (k e)"),
                                    bass.IndirectOffsetOnAxis(rows[:, x, b:b + 1], 0)).then_inc(g.gathered, 16)

                @block.sync
                def _(sp):
                    sp.dma_start(new[:].rearrange("p b a e -> p (b a e)"),
                                 g.scratch_kv.rearrange("(a b) x -> a (b x)", a=1).to_broadcast([P, B * 2 * KV * HD])
                                 ).then_inc(new_in, 16)

                @block.vector
                def _(dve):
                    step = in_order(dve, vec)
                    step(nc.vector.tensor_scalar(old[:], fresh[:], -1.0, 1.0, ALU.mult, ALU.add))
                    dve.wait_ge(new_in, 16)
                    dve.wait_ge(g.gathered, l * all_rows + all_rows)
                    for a, buf in enumerate((ks, vs)):
                        for x in range(HALVES):
                            def over(y):
                                return y[:, x, :].unsqueeze(2).to_broadcast([P, B, KV * HD])
                            step(nc.vector.tensor_tensor(tmp[:], new[:, :, a, :], over(fresh), ALU.mult))
                            step(nc.vector.tensor_tensor(buf[:, :, x, :], buf[:, :, x, :], over(old), ALU.mult))
                            step(nc.vector.tensor_tensor(buf[:, :, x, :], buf[:, :, x, :], tmp[:], ALU.add))
            with stage(g, "turned", "back", "multiplied") as (block, turned, back, multiplied):
                @block.tensor
                def _(pe):
                    def dots(n):
                        pe.wait_ge(back, n + 1)
                        for b in (2 * n, 2 * n + 1):
                            last = nc.tensor.matmul(g.ps[0:B * AH, 2, 0:TOPK_S], qb[:, b * B * AH:(b + 1) * B * AH],
                                                    ksT[:, n % 2, (b % 2) * TOPK_S:(b % 2 + 1) * TOPK_S],
                                                    start=(b == 0), stop=(b == B - 1))
                        return last
                    for n in range(B // 2):
                        for i in range(2 * HALVES):
                            last = nc.tensor.transpose(g.ps[:, n % 2, i * P:(i + 1) * P],
                                                       ks[:, 2 * n + i // HALVES, i % HALVES, :], g.ident)
                        last.then_inc(turned, 1)
                        if n >= 1:
                            last = dots(n - 1)
                    dots(B // 2 - 1).then_inc(multiplied, 1)

                @block.scalar
                def _(act):
                    for n in range(B // 2):
                        act.wait_ge(turned, n + 1)
                        nc.scalar.copy(ksT[:, n % 2, :], g.ps[:, n % 2, :]).then_inc(back, 1)
                    act.wait_ge(multiplied, 1)
                    nc.scalar.mul(sc[:], g.ps[0:B * AH, 2, 0:TOPK_S], HD ** -0.5)
            softmax_rows(g, B * AH, TOPK_S, sc, small)
            with stage(g, "turned", "back", "out_ready") as (block, turned, back, out_ready):
                @block.tensor
                def _(pe):
                    for x in range(HALVES):
                        last = nc.tensor.transpose(g.ps[:, 0, x * B * AH:(x + 1) * B * AH], sc[:, x * P:(x + 1) * P],
                                                   g.ident[0:B * AH, 0:B * AH])
                    last.then_inc(turned, 1)
                    pe.wait_ge(back, 1)
                    for b in range(B):
                        for k in range(KV):
                            c = b * AH + k * 4
                            for half in range(2):
                                for x in range(HALVES):
                                    last = nc.tensor.matmul(g.ps[half * HD:(half + 1) * HD, 1, c:c + 4],
                                                            vs[:, b, x, k * HD:(k + 1) * HD], pT[:, x, c:c + 4],
                                                            start=(x == 0), stop=(x == HALVES - 1))
                    last.then_inc(out_ready, 1)

                @block.vector
                def _(dve):
                    dve.wait_ge(turned, 1)
                    nc.vector.tensor_copy(pT[:].rearrange("p x n -> p (x n)"), g.ps[:, 0, 0:HALVES * B * AH]).then_inc(back, 1)
                    dve.wait_ge(out_ready, 1)
                    for half in range(2):
                        nc.vector.tensor_copy(
                            oat[half * HD:(half + 1) * HD, :, T:TOK],
                            g.ps[half * HD:(half + 1) * HD, 1, 0:B * AH].rearrange("p (b k a) -> p a k b", k=4, a=2)[:, half])



def merge(g, l, d, ot, oat):
    nc = g.nc
    with ExitStack() as ctx:
        gate = ctx.enter_context(g.buffer("gate", [P, 2 * KD, TOK], FP32))

        def squash(kind, m, main, side):
            nc.scalar.activation(gate[:, ds(m, 1), 0:T].rearrange("p a n -> p (a n)"), main, ACT.Sigmoid)
            return nc.scalar.activation(gate[:, ds(m, 1), T:TOK].rearrange("p a n -> p (a n)"), side, ACT.Sigmoid)
        channel_major(g, "gates", weight_rows(d["w_in"], l, 0, KD, C_G, 512), g.ht, KD, 512, 4, squash, only="scalar")
        for w, src, first in ((d["w_dn_up"], ot, 0), (d["w_att_up"], oat, KD)):
            def scale(kind, m, main, side):
                v = gate[:, ds(m + first, 1), :].rearrange("p a n -> p (a n)")
                nc.vector.tensor_tensor(v[:, 0:T], v[:, 0:T], main, ALU.mult)
                return nc.vector.tensor_tensor(v[:, T:TOK], v[:, T:TOK], side, ALU.mult)
            channel_major(g, "up", weight_rows(w, l, 0, H, 0, 512), src, H, 512, 2, scale, only="vector")
        with stage(g, "added") as (block, added):
            @block.vector
            def _(dve):
                nc.vector.memset(g.ht[:, :, TOK:TOKP], 0.0)
                nc.vector.tensor_tensor(g.ht[:, :, 0:TOK], gate[:, 0:KD, :], gate[:, KD:2 * KD, :], ALU.add)
    token_major(g, "w_o", weight_rows(d["w_o"], l, 0, KD, 0, 512), g.ht, KD, 512, 2,
                lambda kind, t, j, ps: add_to_x(g, t, j, ps), only="vector")


def add_to_x(g, t, j, ps, w=512):
    x = g.x[:, t, ds(j * w, w)]
    return g.nc.vector.tensor_tensor(x, x, ps, ALU.add)



def memory(g, l, d):
    nc = g.nc
    N = B * MH
    with ExitStack() as ctx:
        def sb(name, *shape, dt=FP32):
            return ctx.enter_context(g.buffer(name, shape, dt))
        mk = sb("mk", P, MT_, MW)
        mv = sb("mv", P, MT_, MW)
        with ExitStack() as inner:
            mem = inner.enter_context(g.buffer("mem", [P, MT_, D], FP32))
            mt = inner.enter_context(g.buffer("memT", [P, KD, MEM], FP32))
            with stage(g, "mem_in") as (block, mem_in):
                @block.sync
                def _(sp):
                    sp.dma_start(mem[:], d["mem_prompt"][0].rearrange("(t p) n -> p t n", p=P)).then_inc(mem_in, 16)
                    sp.wait_ge(mem_in, 16)
            norm_transposed(g, mem, MT_, d["norm_mem_kv"].rearrange("l (k p) -> p l k", p=P)[:, ds(l, 1), :], mt)
            for w, dst in ((d["w_mk"], mk), (d["w_mv"], mv)):
                token_major(g, "mkv", weight_rows(w, l, 0, KD, 0, 256), mt, KD, 256, 2,
                            lambda kind, t, j, ps: copy(g, kind, dst[:, t, ds(j * 256, 256)], ps), tiles=MT_)
            with stage(g, "stored") as (block, stored):
                @block.sync
                def _(sp):
                    for out, src in ((d["p_mem_k"], mk), (d["p_mem_v"], mv)):
                        sp.dma_start(out.rearrange("l b (t p) h e -> p (l b) t (h e)", p=P)[:, ds(l, 1), :, :]
                                     .rearrange("p a t n -> p (a t) n"), src[:]).then_inc(stored, 16)
                    sp.wait_ge(stored, 32)
        norm_transposed(g, g.x, NT, d["norm_mem_q"].rearrange("l (k p) -> p l k", p=P)[:, ds(l, 1), :], g.ht)
        qT = sb("mqT", P, MH, TOK)
        om = sb("om", P, TT, MW)
        omT = sb("omT", P, MH, TOKP)
        mkT = sb("mkT", P, MH, MEM)

        def evac(kind, m, main, side):
            copy(g, kind, qT[:, ds(m, 1), 0:T].rearrange("p a n -> p (a n)"), main)
            return copy(g, kind, qT[:, ds(m, 1), T:TOK].rearrange("p a n -> p (a n)"), side)
        channel_major(g, "mq", weight_rows(d["w_mq"], l, 0, KD, 0, 256), g.ht, KD, 256, 2, evac)
        with stage(g, "turned", "copied") as (block, turned, copied):
            @block.tensor
            def _(pe):
                for h in range(MH):
                    for t in range(MT_):
                        last = nc.tensor.transpose(g.ps[:, h, t * P:(t + 1) * P], mk[:, t, h * MD:(h + 1) * MD], g.ident)
                last.then_inc(turned, 1)

            @block.scalar
            def _(act):
                act.wait_ge(turned, 1)
                nc.scalar.copy(mkT[:], g.ps[:, 0:MH, 0:MEM])
        with ExitStack() as inner:
            def sbi(name, *shape, dt=FP32):
                return inner.enter_context(g.buffer(name, shape, dt))
            pr = sbi("mpr", P, 2, MEM)
            nm = sbi("mnm", P, TT * MH)
            sums = sbi("msums", P, TT * MH)
            pT = sbi("mpT", P, 2, MT_, P)
            with stage(g, "multiplied", "maxed", "exped", "turned", "back", "ready", "rows_out", "inverted",
                       "scaled") as (block, multiplied, maxed, exped, turned, back, ready, rows_out, inverted, scaled):
                NI = TT * MH
                scale = MD ** -0.5

                @block.tensor
                def _(pe):
                    def scores(i):
                        t, h = i // MH, i % MH
                        nc.tensor.matmul(g.ps[:, i % 2, 0:MEM], qT[:, h, t * P:(t + 1) * P], mkT[:, h, :],
                                         start=True, stop=True).then_inc(multiplied, 1)
                    for i in range(2):
                        scores(i)
                    for i in range(NI):
                        pe.wait_ge(exped, i + 1)
                        if i + 2 < NI:
                            scores(i + 2)
                        if i >= 2:
                            pe.wait_ge(back, i - 1)
                        for k in range(MT_):
                            last = nc.tensor.transpose(g.ps[:, 2 + i % 2, k * P:(k + 1) * P], pr[:, i % 2, k * P:(k + 1) * P], g.ident)
                        last.then_inc(turned, 1)
                        pe.wait_ge(back, i + 1)
                        if i >= 2:
                            pe.wait_ge(rows_out, i - 1)
                        for k in range(MT_):
                            last = nc.tensor.matmul(g.ps[:, 4 + i % 2, 0:MD], pT[:, i % 2, k, :],
                                                    mv[:, k, (i % MH) * MD:(i % MH + 1) * MD],
                                                    start=(k == 0), stop=(k == MT_ - 1))
                        last.then_inc(ready, 1)

                @block.vector
                def _(dve):
                    def finish(i):
                        dve.wait_ge(exped, i + 1)
                        nc.vector.reciprocal(sums[:, i:i + 1], sums[:, i:i + 1]).then_inc(inverted, 1)
                        dve.wait_ge(ready, i + 1)
                        dve.wait_ge(inverted, i + 1)
                        nc.vector.tensor_scalar(om[:, i // MH, (i % MH) * MD:(i % MH + 1) * MD], g.ps[:, 4 + i % 2, 0:MD],
                                                sums[:, i:i + 1], None, ALU.mult).then_inc(rows_out, 1)
                    for i in range(NI):
                        dve.wait_ge(multiplied, i + 1)
                        nc.vector.tensor_reduce(nm[:, i:i + 1], g.ps[:, i % 2, 0:MEM], AX.X, ALU.max,
                                                negate=True).then_inc(maxed, 1)
                        if i >= 1:
                            finish(i - 1)
                    finish(NI - 1)

                @block.scalar
                def _(act):
                    for i in range(NI):
                        act.wait_ge(maxed, i + 1)
                        if i >= 2:
                            act.wait_ge(turned, i - 1)
                        nc.scalar.mul(nm[:, i:i + 1], nm[:, i:i + 1], scale).then_inc(scaled, 1)
                        act.wait_ge(scaled, i + 1)
                        nc.scalar.activation(pr[:, i % 2, :], g.ps[:, i % 2, 0:MEM], ACT.Exp, bias=nm[:, i:i + 1], scale=scale,
                                             accum_out=sums[:, i:i + 1]).then_inc(exped, 1)
                        act.wait_ge(turned, i + 1)
                        nc.scalar.copy(pT[:, i % 2, :, :].rearrange("p k n -> p (k n)"), g.ps[:, 2 + i % 2, 0:MEM]).then_inc(back, 1)
        turn_tokens(g, lambda t, k: om[:, t, k * P:(k + 1) * P], omT, TT)
        memory_sample(g, l, d, qT, omT)
        token_major(g, "w_mo", weight_rows(d["w_mo"], l, 0, MH, 0, 512), omT, MH, 512, 2,
                    lambda kind, t, j, ps: add_to_x(g, t, j, ps), only="vector")


def memory_sample(g, l, d, qT, omT):
    nc = g.nc
    N = B * MH
    with ExitStack() as ctx:
        def sb(name, *shape, dt=FP32):
            return ctx.enter_context(g.buffer(name, shape, dt))
        kin = sb("mem_k", P, 2, MT_, MW)
        kT = sb("mem_kT", P, 2, MH, MEM)
        qz = sb("qz", P, N * (N + 1))
        sc = sb("msc", N, MEM)
        small = sb("msmall", P, 4)
        pT = sb("mspT", P, MT_, N)
        tk = d["cache_mem_k"].rearrange("l b (t p) h e -> p (l b) t (h e)", p=P)
        tv = d["cache_mem_v"].rearrange("l b (t p) h e -> p (l b) t (h e)", p=P)
        with stage(g, "vec") as (block, vec):
            @block.vector
            def _(dve):
                step = in_order(dve, vec)
                step(nc.vector.memset(qz[:], 0.0))
                step(nc.vector.tensor_copy(
                    qz[:].rearrange("p (b h x) -> p b h x", b=B, h=MH)[:, :, :, 0],
                    qT[:, :, T:TOK].rearrange("p h b -> p b h")))
                nc.vector.memset(omT[:, :, TOK:TOKP], 0.0)
        with stage(g, "k_in0", "k_in1", "turned", "back", "multiplied") as (block, k_in0, k_in1, turned, back, multiplied):
            k_in = (k_in0, k_in1)

            @block.sync
            def _(sp):
                for b in range(B):
                    if b >= 2:
                        sp.wait_ge(turned, (b - 1) * MT_)
                    sp.dma_start(kin[:, b % 2], tk[:, ds(l * B + b, 1), :, :].rearrange("p a t n -> p (a t) n")
                                 ).then_inc(k_in[b % 2], 16)

            @block.tensor
            def _(pe):
                def dots(b):
                    pe.wait_ge(back, (b + 1) * MT_)
                    for h in range(MH):
                        n = b * MH + h
                        last = nc.tensor.matmul(g.ps[0:N, 4, 0:MEM], qz[:, n * N:(n + 1) * N], kT[:, b % 2, h, :],
                                                start=(n == 0), stop=(n == N - 1))
                    return last
                for b in range(B):
                    pe.wait_ge(k_in[b % 2], 16 * (b // 2 + 1))
                    for t in range(MT_):
                        for h in range(MH):
                            last = nc.tensor.transpose(g.ps[:, 2 * (b % 2) + t, h * P:(h + 1) * P],
                                                       kin[:, b % 2, t, h * MD:(h + 1) * MD], g.ident)
                        last.then_inc(turned, 1)
                    if b >= 1:
                        dots(b - 1)
                dots(B - 1).then_inc(multiplied, 1)

            @block.scalar
            def _(act):
                for b in range(B):
                    for t in range(MT_):
                        act.wait_ge(turned, b * MT_ + t + 1)
                        nc.scalar.copy(kT[:, b % 2, :, t * P:(t + 1) * P],
                                       g.ps[:, 2 * (b % 2) + t, :].rearrange("p (h m) -> p h m", h=MH)).then_inc(back, 1)
                act.wait_ge(multiplied, 1)
                nc.scalar.mul(sc[:], g.ps[0:N, 4, 0:MEM], MD ** -0.5)
        softmax_rows(g, N, MEM, sc, small)
        with stage(g, "k_in0", "k_in1", "turned", "back", "ready") as (block, k_in0, k_in1, turned, back, ready):
            k_in = (k_in0, k_in1)

            @block.sync
            def _(sp):
                for b in range(B):
                    if b >= 2:
                        sp.wait_ge(ready, b - 1)
                    sp.dma_start(kin[:, b % 2], tv[:, ds(l * B + b, 1), :, :].rearrange("p a t n -> p (a t) n")
                                 ).then_inc(k_in[b % 2], 16)

            @block.tensor
            def _(pe):
                for t in range(MT_):
                    last = nc.tensor.transpose(g.ps[:, 0, t * N:(t + 1) * N], sc[:, t * P:(t + 1) * P], g.ident[0:N, 0:N])
                last.then_inc(turned, 1)
                pe.wait_ge(back, 1)
                for b in range(B):
                    pe.wait_ge(k_in[b % 2], 16 * (b // 2 + 1))
                    for h in range(MH):
                        n = b * MH + h
                        for t in range(MT_):
                            last = nc.tensor.matmul(g.ps[:, 1, n:n + 1], kin[:, b % 2, t, h * MD:(h + 1) * MD], pT[:, t, n:n + 1],
                                                    start=(t == 0), stop=(t == MT_ - 1))
                    last.then_inc(ready, 1)

            @block.vector
            def _(dve):
                dve.wait_ge(turned, 1)
                nc.vector.tensor_copy(pT[:].rearrange("p t n -> p (t n)"), g.ps[:, 0, 0:MT_ * N]).then_inc(back, 1)
                dve.wait_ge(ready, B)
                nc.vector.tensor_copy(omT[:, :, T:TOK], g.ps[:, 1, 0:N].rearrange("p (b h) -> p h b", b=B))



def peer_route(g, l, d, rT):
    nc = g.nc
    HC = 2 * PH
    PAIRS = PTOP * PTOP
    with ExitStack() as ctx:
        def sb(name, *shape, dt=FP32):
            return ctx.enter_context(g.buffer(name, shape, dt))
        qT = sb("pqT", P, HC, TOKP)
        keysT = sb("keysT", P, HC, NK)

        def evac(kind, m, main, side):
            copy(g, kind, qT[:, ds(m, 1), 0:T].rearrange("p a n -> p (a n)"), main)
            return copy(g, kind, qT[:, ds(m, 1), T:TOK].rearrange("p a n -> p (a n)"), side)
        channel_major(g, "pq", weight_rows(d["peer_wq"], l, 0, KD, 0, 512), g.ht, KD, 512, 4, evac)
        q = sb("pq", P, HC, P)
        s = sb("ps", P, HC, NK)
        top = sb("top", P, HC, PTOP)
        topi = sb("topi", P, HC, PTOP, dt=U32)
        topf = sb("topf", P, HC, PTOP)
        cand = sb("cand", P, PH, PAIRS)
        best = sb("best", P, PH, PTOP)
        at = sb("at", P, 3, PJ, dt=U32)
        atf = sb("atf", P, 2, PJ)
        route = sb("route", P, 3, PJ)
        small = sb("gsmall", P, 2, PH)
        with stage(g, "keys_in", "turned", "back") as (block, keys_in, turned, back):
            @block.sync
            def _(sp):
                for x in range(0, HC, 8):
                    sp.dma_start(s[:, x:x + 8, :], d["peer_keys"].rearrange("l h c k e -> k (l h c) e")
                                 [:, ds(l * HC + x, 8), :]).then_inc(keys_in, 16)

            @block.tensor
            def _(pe):
                pe.wait_ge(keys_in, 16 * HC // 8)
                for x in range(HC):
                    last = nc.tensor.transpose(g.ps[:, x // 4, (x % 4) * P:(x % 4 + 1) * P], s[:, x, :], g.ident)
                    if x % 4 == 3:
                        last.then_inc(turned, 1)

            @block.scalar
            def _(act):
                for b in range(HC // 4):
                    act.wait_ge(turned, b + 1)
                    nc.scalar.copy(keysT[:, 4 * b:4 * b + 4, :].rearrange("p x k -> p (x k)"), g.ps[:, b, :])

            @block.vector
            def _(dve):
                nc.vector.memset(qT[:, :, TOK:TOKP], 0.0)
        with nc.Fori(0, NT) as t:
            with stage(g, "fetched", "scored", "back", "vec", "exped", "turned") as (
                    block, fetched, scored, back, vec, exped, turned):
                V = {}

                @block.vector
                def _(dve):
                    count = [0]

                    def step(ins, name=None):
                        count[0] += 1
                        ins.then_inc(vec, 1)
                        dve.wait_ge(vec, count[0])
                        if name:
                            V[name] = count[0]

                    def best16(values, out, index):
                        for r in range(2):
                            step(nc.vector.max(out[:, 8 * r:8 * r + 8], values))
                            step(nc.vector.max_index(index[:, 8 * r:8 * r + 8], out[:, 8 * r:8 * r + 8], values))
                            if r == 0:
                                step(nc.vector.match_replace(values, out[:, 0:8], values, TAKEN))
                    for x in range(HC):
                        if x % 4 == 0:
                            dve.wait_ge(back, x // 4 + 1)
                        best16(s[:, x, :], top[:, x, :], topi[:, x, :])
                    step(nc.vector.tensor_copy(topf[:], topi[:]))
                    halves = top[:].rearrange("p (h c) k -> p h c k", c=2)
                    step(nc.vector.tensor_tensor(
                        cand[:].rearrange("p h (a b) -> p h a b", a=PTOP),
                        halves[:, :, 0, :].unsqueeze(3).to_broadcast([P, PH, PTOP, PTOP]),
                        halves[:, :, 1, :].unsqueeze(2).to_broadcast([P, PH, PTOP, PTOP]), ALU.add))
                    posi = at[:, 0, :].rearrange("p (h k) -> p h k", h=PH)
                    for h in range(PH):
                        best16(cand[:, h, :], best[:, h, :], posi[:, h, :])
                    step(nc.vector.tensor_copy(small[:, 0, :], best[:, :, 0]))
                    step(nc.vector.tensor_tensor(best[:], best[:], small[:, 0, :].unsqueeze(2).to_broadcast([P, PH, PTOP]),
                                                 ALU.subtract), "shifted")
                    step(nc.vector.tensor_scalar(at[:, 1, :], at[:, 0, :], 4, None, ALU.logical_shift_right))
                    step(nc.vector.tensor_scalar(at[:, 2, :], at[:, 0, :], PTOP - 1, None, ALU.bitwise_and))
                    step(nc.vector.tensor_copy(atf[:], at[:, 1:3, :]))
                    fhalves = topf[:].rearrange("p (h c) k -> p h c k", c=2)
                    c4 = cand[:].rearrange("p h (k a) -> p h k a", a=PTOP)
                    for c in range(2):
                        step(nc.vector.tensor_tensor(
                            cand[:].rearrange("p h (k a) -> p (h k) a", a=PTOP),
                            atf[:, c, :].unsqueeze(2).to_broadcast([P, PJ, PTOP]),
                            g.iota[:, 0:PTOP].unsqueeze(1).to_broadcast([P, PJ, PTOP]), ALU.is_equal))
                        step(nc.vector.tensor_tensor(c4, c4, fhalves[:, :, c, :].unsqueeze(2).to_broadcast([P, PH, PTOP, PTOP]),
                                                     ALU.mult))
                        step(nc.vector.tensor_reduce(route[:, c, :], cand[:].rearrange("p h (k a) -> p (h k) a", a=PTOP),
                                                     AX.X, ALU.add))
                    dve.wait_ge(exped, 1)
                    step(nc.vector.tensor_reduce(small[:, 0, :], best[:], AX.X, ALU.add))
                    step(nc.vector.reciprocal(small[:, 1, :], small[:, 0, :]))
                    step(nc.vector.tensor_tensor(route[:, 2, :].rearrange("p (h k) -> p h k", h=PH), best[:],
                                                 small[:, 1, :].unsqueeze(2).to_broadcast([P, PH, PTOP]), ALU.mult), "routed")

                @block.scalar
                def _(act):
                    nc.scalar.copy(q[:], qT[:, :, ds(t * P, P)]).then_inc(fetched, 1)
                    for b in range(HC // 4):
                        act.wait_ge(scored, b + 1)
                        nc.scalar.copy(s[:, 4 * b:4 * b + 4, :].rearrange("p x k -> p (x k)"), g.ps[:, b, :]).then_inc(back, 1)
                    act.wait_ge(vec, V["shifted"])
                    nc.scalar.activation(best[:], best[:], ACT.Exp).then_inc(exped, 1)
                    act.wait_ge(turned, 1)
                    nc.scalar.copy(rT[:, :, ds(t * P, P)], g.ps[:, 4, 0:3 * P].rearrange("p (a n) -> p a n", a=3))

                @block.tensor
                def _(pe):
                    pe.wait_ge(fetched, 1)
                    for x in range(HC):
                        last = nc.tensor.matmul(g.ps[:, x // 4, (x % 4) * P:(x % 4 + 1) * P], q[:, x, :], keysT[:, x, :],
                                                start=True, stop=True)
                        if x % 4 == 3:
                            last.then_inc(scored, 1)
                    pe.wait_ge(vec, V["routed"])
                    for a in range(3):
                        last = nc.tensor.transpose(g.ps[:, 4, a * P:(a + 1) * P], route[:, a, :], g.ident)
                    last.then_inc(turned, 1)


GB = 104
NB = TOK // GB
QUADS = GB // 4


def peer_gates(g, rT):
    nc = g.nc
    with ExitStack() as ctx:
        out = ctx.enter_context(g.buffer("gates", [P, 2, NK, GB], FP32))
        hot = ctx.enter_context(g.buffer("hot2", [P, 2, 4, 2, NK], FP32))
        with stage(g, "hot_ready", "multiplied", "emptied", "stored0", "stored1") as (
                block, hot_ready, multiplied, emptied, stored0, stored1):
            stored = (stored0, stored1)

            @block.vector
            def _(dve):
                dve.sem_inc(multiplied, 2)
                for blk in range(NB):
                    with dve.Fori(0, QUADS // 2) as it:
                        for u in range(2):
                            dve.wait_ge(multiplied, it * 2 + (blk * QUADS + u + 1))
                            for x in range(4):
                                def at(a):
                                    return rT[:, a, ds(it * 8 + (blk * GB + 4 * u + x), 1)]
                                nc.vector.tensor_scalar(hot[:, u, x, 0, :], g.iota, at(0), at(2), ALU.is_equal, ALU.mult)
                                last = nc.vector.tensor_scalar(hot[:, u, x, 1, :], g.iota, at(1), None, ALU.is_equal)
                            last.then_inc(hot_ready, 1)

            @block.tensor
            def _(pe):
                pe.sem_inc(emptied, 2)
                for blk in range(NB):
                    with pe.Fori(0, QUADS // 2) as it:
                        for u in range(2):
                            pe.wait_ge(hot_ready, it * 2 + (blk * QUADS + u + 1))
                            pe.wait_ge(emptied, it * 2 + (blk * QUADS + u + 1))
                            for x in range(4):
                                last = nc.tensor.matmul(g.ps[:, u, x * P:(x + 1) * P], hot[:, u, x, 1, :], hot[:, u, x, 0, :],
                                                        start=True, stop=True)
                            last.then_inc(multiplied, 1)

            @block.scalar
            def _(act):
                for blk in range(NB):
                    if blk >= 2:
                        act.wait_ge(stored[blk % 2], 16 * (blk // 2))
                    with act.Fori(0, QUADS // 2) as it:
                        for u in range(2):
                            act.wait_ge(multiplied, it * 2 + (blk * QUADS + u + 3))
                            nc.scalar.copy(out[:, blk % 2, :, ds(it * 8 + 4 * u, 4)],
                                           g.ps[:, u, :].rearrange("p (x k) -> p k x", x=4)).then_inc(emptied, 1)

            @block.sync
            def _(sp):
                for blk in range(NB):
                    sp.wait_ge(emptied, (blk + 1) * QUADS + 2)
                    sp.dma_start(g.gates[:, :, blk * GB:(blk + 1) * GB], out[:, blk % 2]).then_inc(stored[blk % 2], 16)
                sp.wait_ge(stored0, 16 * ((NB + 1) // 2))
                sp.wait_ge(stored1, 16 * (NB // 2))


def peer_experts(g, l, d):
    nc = g.nc
    GT = 2
    NG = NK // GT
    HALF_TOK = TOK // 2
    COMBOS = [(t, n) for t in range(NT) for n in range(2)]
    PART = [COMBOS[0:5], COMBOS[5:10]]
    NCB = len(COMBOS)
    uview = d["peer_u"].rearrange("l (i p) n -> p (l i) n", p=P)
    vview = d["peer_v"].rearrange("l (i p) n -> p (l i) n", p=P)
    with ExitStack() as ctx:
        def sb(name, *shape, dt=FP32):
            return ctx.enter_context(g.buffer(name, shape, dt))
        flat = g.wb[:].rearrange("p a k n -> p (a k n)")
        raw = flat.rearrange("p (w a i n) -> p w a i n", w=2, a=2, i=GT)
        ub, vb = raw[:, 0], raw[:, 1]
        ht = [sb(f"ht{x}", P, KD, TOK, dt=FP32R) for x in "hl"]
        v2 = [sb(f"v{x}", P, 2, GT, D, dt=FP32R) for x in "hl"]
        u2 = [sb(f"u{x}", P, KD, P, dt=FP32R) for x in "hl"]
        z2 = [sb(f"z{x}", P, 2, GT, TOKP, dt=FP32R) for x in "hl"]
        gt = sb("gt", P, 2, GT, TOK)
        act_out = sb("act_out", P, 2, TOK)
        TERMS = ((0, 0), (0, 1), (1, 0))

        def value(x):
            return x.bitcast(FP32)

        with stage(g, "high", "vec") as (block, high, vec):
            @block.scalar
            def _(act):
                for k in range(KD):
                    nc.scalar.copy(ht[0][:, k, :], g.ht[:, k, 0:TOK]).then_inc(high, 1)

            @block.vector
            def _(dve):
                for k in range(KD):
                    dve.wait_ge(high, k + 1)
                    nc.vector.tensor_tensor(ht[1][:, k, :], g.ht[:, k, 0:TOK], value(ht[0][:, k, :]), ALU.subtract)
                for x in range(2):
                    nc.vector.memset(value(z2[x][:, :, :, TOK:TOKP]), 0.0)

        with stage(g, "u_in0", "u_in1", "v_in0", "v_in1", "g_in0", "g_in1", "turned", "a_full", "out_full",
                   "u_high", "v_high", "gelued", "z_high", "u_low", "v_low", "gated", "z_low", "out_free") as (
                       block, u_in0, u_in1, v_in0, v_in1, g_in0, g_in1, turned, a_full, out_full,
                       u_high, v_high, gelued, z_high, u_low, v_low, gated, z_low, out_free):
            u_in, v_in, g_in = (u_in0, u_in1), (v_in0, v_in1), (g_in0, g_in1)

            def pairs(eng, emit):
                emit(0, "first")
                with eng.Fori(1, NG // 2 - 1) as it:
                    emit(it, "")
                emit(NG // 2 - 1, "last")

            @block.sync
            def _(sp):
                def emit(it, place):
                    for u in range(2):
                        G = it * 2 + u
                        before = None if place == "first" else (it - 1) * (2 * GT) + (u + 1) * GT
                        if before is not None:
                            sp.wait_ge(turned, before)
                        sp.dma_start(ub[:, u], uview[:, ds(l * NK + G * GT, GT), :]).then_inc(u_in[u], 16)
                        if before is not None:
                            sp.wait_ge(gated, before)
                        sp.dma_start(gt[:, u], g.gates[:, ds(G * GT, GT), :]).then_inc(g_in[u], 16)
                        if before is not None:
                            sp.wait_ge(v_low, before)
                        sp.dma_start(vb[:, u], vview[:, ds(l * NK + G * GT, GT), :]).then_inc(v_in[u], 16)
                pairs(sp, emit)

            def combo_bank(w, c):
                return 4 + (w * NCB + c) % 4

            @block.tensor
            def _(pe):
                pe.sem_inc(out_free, 4)

                def outputs(it, w, part):
                    for t, n in part:
                        c = COMBOS.index((t, n))
                        pe.wait_ge(out_free, it * (2 * NCB) + (w * NCB + c + 1))
                        for m, (i, (x, y)) in enumerate((i, xy) for i in range(GT) for xy in TERMS):
                            last = nc.tensor.matmul(g.ps[:, combo_bank(w, c), :], z2[x][:, w, i, t * P:(t + 1) * P],
                                                    v2[y][:, w, i, n * 512:(n + 1) * 512],
                                                    start=(m == 0), stop=(m == 3 * GT - 1))
                        last.then_inc(out_full, 1)

                def turn(it, n):
                    u, i = n // GT, n % GT
                    if i == 0:
                        pe.wait_ge(u_in[u], it * 16 + 16)
                    for k in range(KD):
                        last = nc.tensor.transpose(g.ps[:, k // 4, (k % 4) * P:(k % 4 + 1) * P],
                                                   ub[:, u, i, k * P:(k + 1) * P], g.ident)
                    last.then_inc(turned, 1)

                def emit(it, place):
                    if place == "first":
                        turn(it, 0)
                    for n in range(2 * GT):
                        u, i = n // GT, n % GT
                        done = it * (2 * GT) + n
                        if not (place == "first" and n == 0):
                            pe.wait_ge(gelued, done)
                        pe.wait_ge(u_low, done + 1)
                        for hf in range(2):
                            for m, (k, (x, y)) in enumerate((k, xy) for k in range(KD) for xy in TERMS):
                                last = nc.tensor.matmul(g.ps[:, 2 + hf, 0:HALF_TOK], u2[x][:, k, :],
                                                        ht[y][:, k, hf * HALF_TOK:(hf + 1) * HALF_TOK],
                                                        start=(m == 0), stop=(m == 3 * KD - 1))
                        last.then_inc(a_full, 1)
                        if n + 1 < 2 * GT:
                            turn(it, n + 1)
                        elif place != "last":
                            turn(it + 1, 0)
                        if not (place == "first" and u == 0):
                            if i == 0:
                                pe.wait_ge(z_low, it * (2 * GT) + (u * GT + 2))
                                pe.wait_ge(v_low, it * (2 * GT) + u * GT)
                            outputs(it if u == 1 else it - 1, 1 - u, PART[i])
                pairs(pe, emit)
                pe.wait_ge(z_low, NG * GT + 2)
                pe.wait_ge(v_low, NG * GT)
                outputs(NG // 2 - 1, 1, COMBOS)

            turned_tile = g.ps[:, 0:2, :].rearrange("p a n -> p (a n)")

            @block.scalar
            def _(act):
                def split(it, n):
                    act.wait_ge(turned, it * (2 * GT) + (n + 1))
                    nc.scalar.copy(u2[0][:].rearrange("p k e -> p (k e)"), turned_tile).then_inc(u_high, 1)

                def emit(it, place):
                    if place == "first":
                        split(it, 0)
                    for n in range(2 * GT):
                        this = it * (2 * GT) + (n + 1)
                        act.wait_ge(a_full, this)
                        act.wait_ge(z_low, this)
                        nc.scalar.activation(act_out[:, n % 2, :].rearrange("p (a t) -> p a t", a=2),
                                             g.ps[:, 2:4, 0:HALF_TOK], ACT.Gelu).then_inc(gelued, 1)
                        act.wait_ge(gated, this)
                        nc.scalar.copy(z2[0][:, n // GT, n % GT, 0:TOK], act_out[:, n % 2, :]).then_inc(z_high, 1)
                        if n + 1 < 2 * GT:
                            split(it, n + 1)
                        elif place != "last":
                            split(it + 1, 0)
                        u, i = n // GT, n % GT
                        if i == 0:
                            act.wait_ge(v_in[u], it * 16 + 16)
                        nc.scalar.copy(v2[0][:, u, i, :], vb[:, u, i, :]).then_inc(v_high, 1)
                pairs(act, emit)

            @block.vector
            def _(dve):
                dve.sem_inc(z_low, 2)

                def outputs(it, w, part):
                    for t, n in part:
                        c = COMBOS.index((t, n))
                        rows = P if t < TT else B
                        dve.wait_ge(out_full, it * (2 * NCB) + (w * NCB + c + 1))
                        x = g.x[0:rows, t, n * 512:(n + 1) * 512]
                        nc.vector.tensor_tensor(x, x, g.ps[0:rows, combo_bank(w, c), :], ALU.add).then_inc(out_free, 1)

                def split(it, n):
                    dve.wait_ge(u_high, it * (2 * GT) + (n + 1))
                    nc.vector.tensor_tensor(u2[1][:].rearrange("p k e -> p (k e)"), turned_tile,
                                            value(u2[0][:].rearrange("p k e -> p (k e)")),
                                            ALU.subtract).then_inc(u_low, 1)

                def emit(it, place):
                    if place == "first":
                        split(it, 0)
                    for n in range(2 * GT):
                        u, i = n // GT, n % GT
                        this = it * (2 * GT) + (n + 1)
                        if i == 0:
                            dve.wait_ge(g_in[u], it * 16 + 16)
                        dve.wait_ge(gelued, this)
                        a = act_out[:, n % 2, :]
                        nc.vector.tensor_tensor(a, a, gt[:, u, i, :], ALU.mult).then_inc(gated, 1)
                        dve.wait_ge(z_high, this)
                        nc.vector.tensor_tensor(z2[1][:, u, i, 0:TOK], a, value(z2[0][:, u, i, 0:TOK]),
                                                ALU.subtract).then_inc(z_low, 1)
                        if n + 1 < 2 * GT:
                            split(it, n + 1)
                        elif place != "last":
                            split(it + 1, 0)
                        dve.wait_ge(v_high, this)
                        nc.vector.tensor_tensor(v2[1][:, u, i, :], vb[:, u, i, :], value(v2[0][:, u, i, :]),
                                                ALU.subtract).then_inc(v_low, 1)
                        if not (place == "first" and u == 0):
                            outputs(it if u == 1 else it - 1, 1 - u, PART[i])
                pairs(dve, emit)
                outputs(NG // 2 - 1, 1, COMBOS)


def peer(g, l, d):
    norm_transposed(g, g.x, NT, d["norm_ffn"].rearrange("l (k p) -> p l k", p=P)[:, ds(l, 1), :], g.ht)
    with ExitStack() as ctx:
        rT = ctx.enter_context(g.buffer("routeT", [P, 3, TOKP], FP32))
        peer_route(g, l, d, rT)
        peer_gates(g, rT)
    peer_experts(g, l, d)


def layer(g, l, d):
    nc = g.nc
    mixer(g, l, d)
    memory(g, l, d)
    peer(g, l, d)
    with stage(g, "counted") as (block, counted):
        @block.vector
        def _(dve):
            nc.vector.tensor_scalar(g.layer[:], g.layer[:], 1.0, None, ALU.add)


def final(g, d):
    nc = g.nc
    with ExitStack() as ctx:
        gain = ctx.enter_context(g.buffer("fgain", [P, D], FP32))
        y = ctx.enter_context(g.buffer("y", [P, NT, D], FP32))
        ss = ctx.enter_context(g.buffer("fss", [P, 4, NT], FP32))
        with stage(g, "gain_in", "squared", "vec", "rooted", "stored") as (block, gain_in, squared, vec, rooted, stored):
            @block.sync
            def _(sp):
                sp.dma_start(gain[:], d["norm_final"].rearrange("(a n) -> a n", a=1).to_broadcast([P, D])).then_inc(gain_in, 16)
                sp.wait_ge(vec, 2 + 2 * NT)
                sp.dma_start(d["y_prompt"][0].rearrange("(t p) n -> p t n", p=P), y[:, 0:TT, :]).then_inc(stored, 16)
                sp.dma_start(d["y_sample"][:, 0, :], y[0:B, TT, :]).then_inc(stored, 16)
                sp.wait_ge(stored, 32)

            @block.scalar
            def _(act):
                for t in range(NT):
                    nc.scalar.activation(y[:, t, :], g.x[:, t, :], ACT.Square, accum_out=ss[:, 0, t:t + 1]).then_inc(squared, 1)
                act.wait_ge(vec, 1)
                nc.scalar.activation(ss[:, 2, :], ss[:, 1, :], ACT.Sqrt).then_inc(rooted, 1)

            @block.vector
            def _(dve):
                step = in_order(dve, vec)
                dve.wait_ge(squared, NT)
                step(nc.vector.tensor_scalar(ss[:, 1, :], ss[:, 0, :], 1.0 / D, EPS, ALU.mult, ALU.add))
                dve.wait_ge(rooted, 1)
                step(nc.vector.reciprocal(ss[:, 3, :], ss[:, 2, :]))
                dve.wait_ge(gain_in, 16)
                for t in range(NT):
                    step(nc.vector.tensor_scalar(y[:, t, :], g.x[:, t, :], ss[:, 3, t:t + 1], None, ALU.mult))
                    step(nc.vector.tensor_tensor(y[:, t, :], y[:, t, :], gain[:], ALU.mult))


def mixer(g, l, d):
    nc = g.nc
    norm_transposed(g, g.x, NT, d["norm_mix"].rearrange("l (k p) -> p l k", p=P)[:, ds(l, 1), :], g.ht)
    with ExitStack() as ctx:
        def sb(name, shape, dt=FP32):
            return ctx.enter_context(g.buffer(name, shape, dt))
        g.nat = sb("nat", [P, NT, NAT_W])
        o_all = sb("o_all", [P, NT, H, DK])
        wn = NAT_W // 4
        token_major(g, "nat", weight_rows(d["w_in"], l, 0, KD, C_Z, wn), g.ht, KD, wn, 4,
                    lambda kind, t, j, ps: copy(g, kind, g.nat[:, t, ds(j * wn, wn)], ps))
        with ExitStack() as inner:
            def sbi(name, shape, dt=FP32):
                return inner.enter_context(g.buffer(name, shape, dt))
            conv = sbi("conv", [P, CC, TOK])
            convolution(g, l, d, conv)
            kn = sbi("kn", [P, TT, H, DK])
            vn = sbi("vn", [P, TT, H, DK])
            gb = sbi("gb", [P, NT, 2 * H])
            delta_features(g, l, d, conv, kn, vn, gb)
            delta_prompt(g, l, d, conv, kn, vn, gb, o_all)
            delta_sample(g, l, d, conv, gb, o_all)
        ot = sb("ot", [P, H, TOKP])
        delta_output(g, l, d, o_all, ot)
        rotary(g, l, d)
        oat = sb("oat", [P, 4, TOKP])
        sparse_prompt(g, l, d, oat)
        sparse_sample(g, l, d, oat)
        merge(g, l, d, ot, oat)
def program(nc, d, where):
    with ExitStack() as ctx:
        g = Core(nc)

        def sb(name, shape, dt=FP32):
            return ctx.enter_context(g.buffer(name, shape, dt))
        n_const = sum(w for _, w in where.values())
        consts = sb("tables", [P, n_const])

        def const(name):
            at, w = where[name]
            return consts[:, at:at + w]
        g.ident, g.ones, g.triu, g.strict = const("ident"), const("ones"), const("triu"), const("strict")
        g.iota, g.iota512, g.tpos, g.slot = const("iota"), const("iota512"), const("tpos"), const("slot")
        g.own = const("own")
        g.lev = [const(f"lev{s}") for s in range(7)]
        g.cos = const("cos").rearrange("p (t h) -> p t h", h=HALF)
        g.sin = const("sin").rearrange("p (t h) -> p t h", h=HALF)
        g.layer = sb("layer", [P, 1])
        g.pages = sb("pages", [1, B * PAGES], I32)
        g.x = sb("x", [P, NT, D])
        g.ht = sb("ht", [P, KD, TOKP])
        g.wb = sb("wb", [P, 2, KD, 512])
        g.scratch_ab = nc.dram_tensor("scratch_ab", [B, 2 * H], FP32, kind="Internal").ap()
        g.scratch_w = nc.dram_tensor("scratch_w", [B, IH], FP32, kind="Internal").ap()
        g.scratch_kv = nc.dram_tensor("scratch_kv", [B, 2 * KV * HD], FP32, kind="Internal").ap()
        g.gates = nc.dram_tensor("gates", [P, NK, TOK], FP32, kind="Internal").ap()
        g.gathered = ctx.enter_context(nc.semaphore("gathered"))
        g.ps = ctx.enter_context(nc.psum_tensor("ps", [P, 8, 512], FP32))
        with stage(g, "loaded", "cleared") as (block, loaded, cleared):
            @block.sync
            def _(sp):
                sp.dma_start(consts[:], d["consts"]).then_inc(loaded, 16)
                sp.dma_start(g.pages[:], d["page_table"].rearrange("(a b) n -> a (b n)", a=1)).then_inc(loaded, 16)
                sp.dma_start(g.x[:, 0:TT, :], d["x_prompt"][0].rearrange("(t p) n -> p t n", p=P)).then_inc(loaded, 16)
                sp.wait_ge(cleared, 1)
                sp.dma_start(g.x[0:B, TT, :], d["x_sample"][:, 0, :]).then_inc(loaded, 16)
                sp.wait_ge(loaded, 64)

            @block.vector
            def _(dve):
                nc.vector.memset(g.layer[:], 0.0)
                nc.vector.memset(g.x[:, TT, :], 0.0).then_inc(cleared, 1)
        with nc.Fori(0, DEPTH) as l:
            layer(g, l, d)
        final(g, d)



_INS = ['x_prompt', 'x_sample', 'cache_k', 'cache_v', 'cache_kidx', 'state_conv', 'state_delta', 'cache_mem_k',
        'cache_mem_v', 'page_table', 'mem_prompt', 'norm_mix', 'w_in', 'dn_conv_w', 'dn_a_log', 'dn_dt_bias', 'dn_norm',
        'w_dn_up', 'w_att_up', 'w_o', 'norm_mem_q', 'norm_mem_kv', 'w_mq', 'w_mk', 'w_mv', 'w_mo', 'norm_ffn',
        'peer_wq', 'peer_keys', 'peer_u', 'peer_v', 'norm_final']
_OUTS = [('y_prompt', (1, T, D)), ('y_sample', (B, 1, D)),
         ('p_k', (1, T, DEPTH, KV, HD)), ('p_v', (1, T, DEPTH, KV, HD)), ('p_kidx', (1, T, DEPTH, ID)),
         ('p_conv', (DEPTH, 1, CW - 1, CONV)), ('p_delta', (DEPTH, 1, H, DK, DK)),
         ('p_mem_k', (DEPTH, 1, MEM, MH, MD)), ('p_mem_v', (DEPTH, 1, MEM, MH, MD)),
         ('s_k', (B, 1, DEPTH, KV, HD)), ('s_v', (B, 1, DEPTH, KV, HD)), ('s_kidx', (B, 1, DEPTH, ID)),
         ('s_conv', (DEPTH, B, CW - 1, CONV)), ('s_delta', (DEPTH, B, H, DK, DK))]


def kernel(**inputs):
    import concourse.bacc as _bacc
    from concourse.bass_utils import run_bass_kernel_spmd as _run

    nc = _bacc.Bacc("TRN2", target_bir_lowering=False, num_devices=1)
    arrays = {name: np.ascontiguousarray(inputs[name]) for name in _INS}
    arrays["consts"], where = host_constants()
    aps = {}
    for name, a in arrays.items():
        aps[name] = nc.dram_tensor(name, a.shape, mybir.dt.from_np(a.dtype), kind="ExternalInput").ap()
    for name, shape in _OUTS:
        aps[name] = nc.dram_tensor(name, shape, FP32, kind="ExternalOutput").ap()
    program(nc, aps, where)
    r = _run(nc, [arrays], core_ids=[0])
    return tuple(r.results[0][name] for name, _ in _OUTS)
```

```python
from contextlib import contextmanager, ExitStack


import numpy as np
import concourse.bass as bass
from concourse import mybir

FP32 = mybir.dt.float32
FP32R = mybir.dt.float32r
I32 = mybir.dt.int32
U32 = mybir.dt.uint32
ALU = mybir.AluOpType
ACT = mybir.ActivationFunctionType
AX = mybir.AxisListType
ds = bass.ds

P = 128
D = 1024
KD = D // P
T = 512
B = 8
DEPTH = 2
TT = T // P
NT = TT + 1
TOK = T + B
TOKP = NT * P
PAST, PAGE = 4096, 128
PAGES = PAST // PAGE
H, DK = 4, 128
CONV = 3 * H * DK
CC = CONV // P
CW = 4
AH, KV, HD = 8, 2, 64
IH, ID = 4, 64
ROT = HD // 4
HALF = ROT // 2
TOPK_P = min(256, T // 4)
TOPK_S = min(256, (PAST + 1) // 4)
SEGS = 4
SEG = PAST // SEGS
MEM, MH, MD = 256, 4, 128
MT_ = MEM // P
MW = MH * MD
NK = 128
PH, PTOP = 8, 16
PJ = PH * PTOP
EPS = 1e-6
BIG = 3.0e38
TAKEN = -3.4e38
C_Z = CONV
NAT_W = H * DK + 2 * H + AH * HD + 2 * KV * HD + IH * ID + ID + IH
C_G = C_Z + NAT_W
N_IN = C_G + 2 * D
N_A = H * DK
N_B = N_A + H
N_Q = N_B + H
N_K = N_Q + AH * HD
N_V = N_K + KV * HD
N_QI = N_V + KV * HD
N_KI = N_QI + IH * ID
N_WI = N_KI + ID

ROPE_THETA = 500000.0


def host_constants():
    p = np.arange(P)[:, None]
    f = np.arange(P)[None, :]
    cols = {}
    cols["ident"] = (p == f)
    cols["ones"] = np.ones((P, P))
    cols["triu"] = (p <= f)
    cols["tril"] = (p >= f)
    cols["strict"] = (p > f)
    for s in range(7):
        cols[f"lev{s}"] = ((f >> s) % 2 == 1) & ((p >> s) == (f >> s) - 1)
    cols["iota"] = np.broadcast_to(f, (P, P))
    pos = np.concatenate([np.arange(T), np.full(P, PAST)]).astype(np.float32)
    inv = np.float32(ROPE_THETA) ** (-np.arange(HALF, dtype=np.float32) / np.float32(HALF))
    ang = (pos[:, None] * inv[None, :]).astype(np.float32)
    cols["cos"] = np.cos(ang).reshape(NT, P, HALF).transpose(1, 0, 2).reshape(P, -1)
    cols["sin"] = np.sin(ang).reshape(NT, P, HALF).transpose(1, 0, 2).reshape(P, -1)
    cols["tpos"] = np.arange(T).reshape(TT, P).T
    cols["iota512"] = np.broadcast_to(np.arange(T)[None, :], (P, T))
    cols["slot"] = p
    cols["own"] = (p[:, :1] // IH == f[:, :B])
    cols["lists"] = np.broadcast_to(np.arange(B) * SEGS * TOPK_S, (P, B))
    where, parts, at = {}, [], 0
    for name, a in cols.items():
        a = np.asarray(a, np.float32)
        where[name] = (at, a.shape[1])
        at += a.shape[1]
        parts.append(a)
    return np.ascontiguousarray(np.concatenate(parts, axis=1)), where


class Core:

    def __init__(self, nc):
        self.nc = nc
        self.used = 0

    def unique(self, name):
        self.used += 1
        return f"{name}_{self.used}"

    def buffer(self, name, shape, dt):
        return self.nc.sbuf_tensor(self.unique(name), list(shape), dt)


@contextmanager
def stage(g, *names):
    nc = g.nc
    with ExitStack() as ctx:
        sems = [ctx.enter_context(nc.semaphore(g.unique(n))) for n in names]
        with nc.Block(no_gpsimd_drain=True) as block:
            yield (block, *sems)
        for s in sems:
            nc.sync.sem_clear(s)
        nc.all_engine_barrier()


def in_order(eng, sem):
    count = [0]

    def step(ins):
        count[0] += 1
        ins.then_inc(sem, 1)
        eng.wait_ge(sem, count[0])
    return step



def norm_transposed(g, src, tiles, gains, dst):
    nc = g.nc
    with ExitStack() as ctx:
        gain = ctx.enter_context(g.buffer("gain", [P, 1, KD], FP32))
        ss = ctx.enter_context(g.buffer("ss", [P, 4, tiles], FP32))
        idle = g.wb[:].rearrange("p a k n -> p (a k n)")
        xn = idle[:, 0:2 * D].rearrange("p (u n) -> p u n", u=2)
        sq = idle[:, 2 * D:(2 + tiles) * D].rearrange("p (t n) -> p t n", t=tiles)
        with stage(g, "gain_in", "squared", "rooted", "vec", "scaled", "turned", "placed") as (
                block, gain_in, squared, rooted, vec, scaled, turned, placed):
            @block.sync
            def _(sp):
                sp.dma_start(gain[:], gains, allow_slow_non_contiguous=True).then_inc(gain_in, 16)

            @block.scalar
            def _(act):
                for t in range(tiles):
                    nc.scalar.activation(sq[:, t, :], src[:, t, :], ACT.Square, accum_out=ss[:, 0, t:t + 1]).then_inc(squared, 1)
                act.wait_ge(vec, 1)
                nc.scalar.activation(ss[:, 2, :], ss[:, 1, :], ACT.Sqrt).then_inc(rooted, 1)
                act.wait_ge(vec, 2)
                for t in range(tiles):
                    if t >= 2:
                        act.wait_ge(turned, t - 1)
                    nc.scalar.mul(xn[:, t % 2, :], src[:, t, :], ss[:, 3, t:t + 1]).then_inc(scaled, 1)

            @block.vector
            def _(dve):
                step = in_order(dve, vec)
                dve.wait_ge(squared, tiles)
                step(nc.vector.tensor_scalar(ss[:, 1, :], ss[:, 0, :], 1.0 / D, EPS, ALU.mult, ALU.add))
                dve.wait_ge(rooted, 1)
                step(nc.vector.reciprocal(ss[:, 3, :], ss[:, 2, :]))
                dve.wait_ge(gain_in, 16)
                for t in range(tiles):
                    dve.wait_ge(turned, t + 1)
                    for b in range(2):
                        last = nc.vector.tensor_tensor(
                            dst[:, 4 * b:4 * b + 4, t * P:(t + 1) * P],
                            g.ps[:, 2 * (t % 2) + b, :].rearrange("p (k t) -> p k t", k=4),
                            gain[:, 0, 4 * b:4 * b + 4].unsqueeze(2).to_broadcast([P, 4, P]), ALU.mult)
                    last.then_inc(placed, 1)

            @block.tensor
            def _(pe):
                for t in range(tiles):
                    pe.wait_ge(scaled, t + 1)
                    if t >= 2:
                        pe.wait_ge(placed, t - 1)
                    for k in range(KD):
                        last = nc.tensor.transpose(g.ps[:, 2 * (t % 2) + k // 4, (k % 4) * P:(k % 4 + 1) * P],
                                                   xn[:, t % 2, k * P:(k + 1) * P], g.ident)
                    last.then_inc(turned, 1)



def linear(g, name, weights, nk, nw, chunks, groups, only=None, beside=None):
    nc = g.nc
    count = len(groups(0, g.wb[:, 0]))
    body = 2 * count
    if only:
        to_vector = [only == "vector"] * body
    else:
        n_act = body // 2 - (body // 2) % 2
        to_vector = [not (x % 2 == 1 and x // 2 < n_act) for x in range(body)]
    n_v, n_a = sum(to_vector), body - sum(to_vector)
    with stage(g, name + "_w0", name + "_w1", "v_full", "a_full", "v_free", "a_free", "aside") as (
            block, w0, w1, v_full, a_full, v_free, a_free, aside):
        w_in = (w0, w1)

        def wbuf(u):
            return g.wb[:, u].rearrange("p k n -> p (k n)")[:, 0:nk * nw].rearrange("p (k n) -> p k n", k=nk)

        @block.sync
        def _(sp):
            for u in range(2):
                sp.dma_start(wbuf(u), weights(u)).then_inc(w_in[u], 16)
            if chunks > 2:
                with sp.Fori(1, chunks // 2) as it:
                    for u in range(2):
                        through = to_vector[:(u + 1) * count]
                        if through[-1]:
                            sp.wait_ge(v_full, (it - 1) * n_v + sum(through))
                        else:
                            sp.wait_ge(a_full, (it - 1) * n_a + len(through) - sum(through))
                        sp.dma_start(wbuf(u), weights(it * 2 + u)).then_inc(w_in[u], 16)

        @block.tensor
        def _(pe):
            with pe.Fori(0, chunks // 2) as it:
                at_v = at_a = 0
                for u in range(2):
                    pe.wait_ge(w_in[u], it * 16 + 16)
                    for n, (parts, _) in enumerate(groups(it * 2 + u, wbuf(u))):
                        if to_vector[u * count + n]:
                            slot, full, free, total, at = at_v % 2, v_full, v_free, n_v, at_v
                            at_v += 1
                        else:
                            slot, full, free, total, at = 2 + at_a % 2, a_full, a_free, n_a, at_a
                            at_a += 1
                        pe.wait_ge(free, it * total + (at + 1))
                        for side, (lhs, rhs, rows, width) in enumerate(parts):
                            for k in range(nk):
                                last = nc.tensor.matmul(g.ps[0:rows, slot + 4 * side, 0:width], lhs(k), rhs(k),
                                                        start=(k == 0), stop=(k == nk - 1))
                        last.then_inc(full, 1)

        def drain(eng, mine, full, free, total, first, kind):
            eng.sem_inc(free, 2)
            with eng.Fori(0, chunks // 2) as it:
                at = 0
                for u in range(2):
                    for n, (parts, evac) in enumerate(groups(it * 2 + u, wbuf(u))):
                        if to_vector[u * count + n] != mine:
                            continue
                        slot = first + at % 2
                        eng.wait_ge(full, it * total + (at + 1))
                        main = g.ps[0:parts[0][2], slot, 0:parts[0][3]]
                        side = g.ps[0:parts[1][2], slot + 4, 0:parts[1][3]] if len(parts) > 1 else None
                        evac(kind, main, side).then_inc(free, 1)
                        at += 1

        if n_v:
            @block.vector
            def _(dve):
                drain(dve, True, v_full, v_free, n_v, 0, "vector")
        elif beside:
            @block.vector
            def _(dve):
                beside(dve, aside)

        if n_a:
            @block.scalar
            def _(act):
                drain(act, False, a_full, a_free, n_a, 2, "scalar")


def copy(g, kind, dst, src):
    if kind == "vector":
        return g.nc.vector.tensor_copy(dst, src)
    return g.nc.scalar.copy(dst, src)


def weight_rows(w, l, k0, nk, c0, nw):
    v = w.rearrange("l (k p) n -> p (l k) n", p=P)
    per = w.shape[1] // P
    return lambda j: v[:, ds(l * per + k0, nk), ds(j * nw + c0, nw)]


def token_major(g, name, weights, lhs, nk, nw, chunks, evac, only=None, tiles=NT):
    def groups(j, w):
        return [([(lambda k, t=t: lhs[:, k, t * P:(t + 1) * P], lambda k: w[:, k, :], P, nw)],
                 lambda kind, main, side, t=t: evac(kind, t, j, main)) for t in range(tiles)]
    linear(g, name, weights, nk, nw, chunks, groups, only)


def channel_major(g, name, weights, rhs, nk, nw, chunks, evac, only=None, side=True, width=T, beside=None):
    def groups(j, w):
        out = []
        for m in range(nw // P):
            parts = [(lambda k, m=m: w[:, k, m * P:(m + 1) * P], lambda k: rhs[:, k, 0:width], P, width)]
            if side:
                parts.append((lambda k, m=m: w[:, k, m * P:(m + 1) * P], lambda k: rhs[:, k, T:TOK], P, B))
            out.append((parts, lambda kind, main, sd, m=m: evac(kind, j * (nw // P) + m, main, sd)))
        return out
    linear(g, name, weights, nk, nw, chunks, groups, only, beside)



def convolution(g, l, d, conv, beside):
    nc = g.nc
    S0 = CW - 1 + T
    with ExitStack() as ctx:
        cin = ctx.enter_context(g.buffer("cin", [P, CC, S0 + B * CW], FP32))
        past = ctx.enter_context(g.buffer("conv_past", [B * (CW - 1), CONV], FP32))
        taps = ctx.enter_context(g.buffer("taps", [P, CW, CC], FP32))
        sig = ctx.enter_context(g.buffer("sig", [P, 2, TOK], FP32))
        win = cin[:, :, S0:S0 + B * CW].rearrange("p c (b w) -> p c b w", w=CW)
        with stage(g, "past_in", "turned", "zeroed") as (block, past_in, turned, zeroed):
            @block.sync
            def _(sp):
                sp.dma_start(past[:], d["state_conv"].rearrange("l b w c -> (l b w) c")
                             [ds(l * (B * (CW - 1)), B * (CW - 1)), :]).then_inc(past_in, 16)
                sp.dma_start(taps[:].rearrange("p w c -> p (w c)"),
                             d["dn_conv_w"].rearrange("l w (c p) -> p l (w c)", p=P)[:, ds(l, 1), :]
                             .rearrange("p l x -> p (l x)"), allow_slow_non_contiguous=True).then_inc(past_in, 16)

            @block.tensor
            def _(pe):
                pe.wait_ge(past_in, 32)
                for c in range(CC):
                    last = nc.tensor.transpose(g.ps[:, 0, c * 24:(c + 1) * 24], past[:, c * P:(c + 1) * P],
                                               g.ident[0:24, 0:24])
                last.then_inc(turned, 1)

            @block.vector
            def _(dve):
                nc.vector.memset(cin[:, :, 0:CW - 1], 0.0)
                dve.wait_ge(turned, 1)
                ps = g.ps[:, 0, 0:CC * 24].rearrange("p (c b w) -> p c b w", c=CC, w=CW - 1)
                for w in range(CW - 1):
                    nc.vector.tensor_copy(win[:, :, :, w], ps[:, :, :, w])

        def evac(kind, c, main, side):
            copy(g, kind, cin[:, ds(c, 1), CW - 1:S0].rearrange("p a n -> p (a n)"), main)
            return copy(g, kind, win[:, ds(c, 1), :, CW - 1].rearrange("p a b -> p (a b)"), side)
        channel_major(g, "conv", weight_rows(d["w_in"], l, 0, KD, 0, 384), g.ht, KD, 384, 4, evac,
                      only="scalar", beside=beside)

        with stage(g, "stored", "vec", "squashed", "gated") as (block, stored, vec, squashed, gated):
            @block.sync
            def _(sp):
                for c in range(CC):
                    sp.dma_start(d["p_conv"].rearrange("l b w (c p) -> p (l b) c w", p=P)[:, ds(l, 1), c, :]
                                 .rearrange("p l w -> p (l w)"), cin[:, c, T:S0],
                                 allow_slow_non_contiguous=True).then_inc(stored, 16)
                    for w in range(CW - 1):
                        sp.dma_start(d["s_conv"].rearrange("l b w (c p) -> p l c w b", p=P)[:, ds(l, 1), c, w, :]
                                     .rearrange("p l b -> p (l b)"), win[:, c, :, w + 1],
                                     allow_slow_non_contiguous=True).then_inc(stored, 16)
                sp.wait_ge(stored, 16 * CC * CW)

            @block.vector
            def _(dve):
                step = in_order(dve, vec)

                def gate(c):
                    dve.wait_ge(squashed, c + 1)
                    nc.vector.tensor_tensor(conv[:, c, :], conv[:, c, :], sig[:, c % 2, :], ALU.mult).then_inc(gated, 1)
                for c in range(CC):
                    def srcs(w):
                        return (cin[:, c, w:w + T], win[:, c, :, w])
                    for part, lo, hi in ((0, 0, T), (1, T, TOK)):
                        step(nc.vector.tensor_scalar(conv[:, c, lo:hi], srcs(0)[part], taps[:, 0, c:c + 1], None, ALU.mult))
                        for w in range(1, CW):
                            step(nc.vector.scalar_tensor_tensor(conv[:, c, lo:hi], srcs(w)[part], taps[:, w, c:c + 1],
                                                                conv[:, c, lo:hi], ALU.mult, ALU.add))
                    if c >= 1:
                        gate(c - 1)
                gate(CC - 1)

            @block.scalar
            def _(act):
                for c in range(CC):
                    act.wait_ge(vec, 2 * CW * (c + 1))
                    if c >= 2:
                        act.wait_ge(gated, c - 1)
                    nc.scalar.activation(sig[:, c % 2, :], conv[:, c, :], ACT.Sigmoid).then_inc(squashed, 1)



def delta_features(g, l, d, conv, kn, vn, gb):
    nc = g.nc
    gg, beta = gb[:, :, 0:H], gb[:, :, H:2 * H]
    with ExitStack() as ctx:
        sq = ctx.enter_context(g.buffer("sq2", [P, 2, TOK], FP32))
        rt = ctx.enter_context(g.buffer("rt", [P, 2, TOK], FP32))
        par = ctx.enter_context(g.buffer("par", [P, 2, H], FP32))
        ea = ctx.enter_context(g.buffer("ea", [P, H], FP32))
        tmp = ctx.enter_context(g.buffer("tmpab", [P, 4, NT * H], FP32))
        with stage(g, "squared", "summed", "epsed", "rooted", "vec") as (block, squared, summed, epsed, rooted, vec):
            @block.scalar
            def _(act):
                for c in range(2 * H + 1):
                    if c < 2 * H:
                        if c >= 2:
                            act.wait_ge(summed, c - 1)
                        nc.scalar.activation(sq[:, c % 2, :], conv[:, c, :], ACT.Square).then_inc(squared, 1)
                    if c >= 1:
                        act.wait_ge(epsed, c)
                        nc.scalar.activation(rt[:, (c - 1) % 2, :], rt[:, (c - 1) % 2, :], ACT.Sqrt).then_inc(rooted, 1)

            @block.tensor
            def _(pe):
                for c in range(2 * H):
                    pe.wait_ge(squared, c + 1)
                    if c >= 2:
                        pe.wait_ge(epsed, c - 1)
                    nc.tensor.matmul(g.ps[:, c % 2, :], g.ones, sq[:, c % 2, 0:T], start=True, stop=True)
                    nc.tensor.matmul(g.ps[:, 2 + c % 2, 0:B], g.ones, sq[:, c % 2, T:TOK], start=True,
                                     stop=True).then_inc(summed, 1)

            @block.vector
            def _(dve):
                step = in_order(dve, vec)
                for c in range(2 * H):
                    dve.wait_ge(summed, c + 1)
                    nc.vector.tensor_scalar(rt[:, c % 2, 0:T], g.ps[:, c % 2, :], EPS, None, ALU.add)
                    nc.vector.tensor_scalar(rt[:, c % 2, T:TOK], g.ps[:, 2 + c % 2, 0:B], EPS, None,
                                            ALU.add).then_inc(epsed, 1)
                    dve.wait_ge(rooted, c + 1)
                    step(nc.vector.reciprocal(rt[:, c % 2, :], rt[:, c % 2, :]))
                    scale = DK ** -0.5 if c < H else 1.0
                    step(nc.vector.scalar_tensor_tensor(conv[:, c, :], conv[:, c, :], scale, rt[:, c % 2, :],
                                                        ALU.mult, ALU.mult))
        with stage(g, "par_in", "vec", "act_done", "turned", "copied") as (block, par_in, vec, act_done, turned, copied):
            a_in = g.nat[:, :, N_A:N_A + H]
            b_in = g.nat[:, :, N_B:N_B + H]

            def t3(n):
                return tmp[:, n, :].rearrange("p (t h) -> p t h", h=H)

            @block.sync
            def _(sp):
                for n, v in enumerate((d["dn_a_log"], d["dn_dt_bias"])):
                    sp.dma_start(par[:, n, :], v[ds(l, 1), :].to_broadcast([P, H])).then_inc(par_in, 16)

            @block.vector
            def _(dve):
                step = in_order(dve, vec)
                dve.wait_ge(par_in, 32)
                bias = par[:, 1, :].unsqueeze(1).to_broadcast([P, NT, H])
                step(nc.vector.tensor_tensor(t3(0), a_in, bias, ALU.add))
                step(nc.vector.tensor_scalar(tmp[:, 1, :], tmp[:, 0, :], -1.0, None, ALU.mult))
                step(nc.vector.tensor_tensor(tmp[:, 1, :], tmp[:, 0, :], tmp[:, 1, :], ALU.max))
                step(nc.vector.tensor_scalar(tmp[:, 0, :], tmp[:, 0, :], 0.0, None, ALU.max))
                dve.wait_ge(act_done, 2)
                step(nc.vector.tensor_scalar(tmp[:, 1, :], tmp[:, 2, :], 1.0, None, ALU.add))
                dve.wait_ge(act_done, 3)
                step(nc.vector.tensor_tensor(tmp[:, 0, :], tmp[:, 0, :], tmp[:, 3, :], ALU.add))
                step(nc.vector.tensor_scalar(ea[:], ea[:], -1.0, None, ALU.mult))
                step(nc.vector.tensor_tensor(gg, t3(0), ea[:].unsqueeze(1).to_broadcast([P, NT, H]), ALU.mult))
                for n in range(2 * TT):
                    dve.wait_ge(turned, n + 1)
                    dst = (kn, vn)[n // TT]
                    nc.vector.tensor_copy(dst[:, n % TT, :, :].rearrange("p h n -> p (h n)"),
                                          g.ps[:, n % 2, :]).then_inc(copied, 1)

            @block.scalar
            def _(act):
                act.wait_ge(par_in, 32)
                nc.scalar.activation(ea[:], par[:, 0, :], ACT.Exp).then_inc(act_done, 1)
                act.wait_ge(vec, 4)
                nc.scalar.activation(tmp[:, 2, :], tmp[:, 1, :], ACT.Exp, scale=-1.0).then_inc(act_done, 1)
                act.wait_ge(vec, 5)
                nc.scalar.activation(tmp[:, 3, :], tmp[:, 1, :], ACT.Ln).then_inc(act_done, 1)
                nc.scalar.activation(beta, b_in, ACT.Sigmoid).then_inc(act_done, 1)

            @block.tensor
            def _(pe):
                for n in range(2 * TT):
                    if n >= 2:
                        pe.wait_ge(copied, n - 1)
                    for h in range(H):
                        last = nc.tensor.transpose(g.ps[:, n % 2, h * P:(h + 1) * P],
                                                   conv[:, (1 + n // TT) * H + h, (n % TT) * P:(n % TT + 1) * P], g.ident)
                    last.then_inc(turned, 1)


def delta_prompt(g, l, d, conv, kn, vn, gb, o_all):
    nc = g.nc
    LEVELS = 7
    HALF_H = (slice(0, H // 2), slice(H // 2, H))
    P_BANK, M_BANK, MT_BANK = (5, 2), (6, 3), (7, 4)

    with ExitStack() as ctx:
        def sb(name, shape=(P, H, P)):
            return ctx.enter_context(g.buffer(name, list(shape), FP32))
        qk = sb("qk", (P, 2 * H, P))
        kc = sb("kc")
        S, gbc, d1, e1, e2, low, lowT, lev, M, MT, Pm, aq, r, vnew, vs, t1 = (
            sb(n) for n in ("S", "gbc", "d1", "e1", "e2", "low", "lowT", "lev", "M", "MT", "Pm", "aq", "r", "vnew", "vs", "t1"))
        gc = sb("gc", (P, 2 * H))
        ex = sb("ex", (P, 3, H))
        be = sb("be", (P, H))
        dif = sb("dif", (P, H))

        def bank(n):
            return g.ps[:, n, :].rearrange("p (h n) -> p h n", h=H)

        def over(x):
            return x.unsqueeze(2).to_broadcast([P, H, P])

        def mask(x):
            return x.unsqueeze(1).to_broadcast([P, H, P])

        with stage(g, "zeroed") as (block, zeroed):
            @block.vector
            def _(dve):
                nc.vector.memset(S[:], 0.0)

        with nc.Fori(0, TT) as c:
            gg = gb[:, ds(c, 1), 0:H].rearrange("p a h -> p (a h)")
            beta = gb[:, ds(c, 1), H:2 * H].rearrange("p a h -> p (a h)")

            def tok(tile):
                return qk[:, tile, :]
            vc = vn[:, ds(c, 1), :, :].rearrange("p a h n -> p (a h) n")
            with stage(g, "vec", "grams", "sums", "exps", "level_p", "level_m", "state_read", "solved",
                       "out_ready", "fetched") as (
                           block, vec, grams, sums, exps, level_p, level_m, state_read, solved, out_ready, fetched):
                V = {}

                @block.vector
                def _(dve):
                    count = [0]

                    def step(ins, name=None):
                        count[0] += 1
                        ins.then_inc(vec, 1)
                        dve.wait_ge(vec, count[0])
                        if name:
                            V[name] = count[0]

                    def put(ins, name=None):
                        count[0] += 1
                        ins.then_inc(vec, 1)
                        if name:
                            V[name] = count[0]
                    step(nc.vector.tensor_copy(gbc[:], over(gg)), "g_spread")
                    step(nc.vector.tensor_copy(M[:], mask(g.ident)))
                    step(nc.vector.tensor_copy(MT[:], mask(g.ident)), "started")
                    dve.wait_ge(sums, 1)
                    step(nc.vector.tensor_copy(gc[:], g.ps[:, 1, 0:2 * H]))
                    step(nc.vector.tensor_tensor(dif[:], gc[:, H:2 * H], gc[:, 0:H], ALU.subtract), "gc")
                    step(nc.vector.tensor_tensor(d1[:], bank(0), over(gc[:, 0:H]), ALU.subtract))
                    step(nc.vector.tensor_scalar(e1[:], d1[:], 0.0, None, ALU.min))
                    step(nc.vector.tensor_scalar(e2[:], d1[:], -1.0, 0.0, ALU.mult, ALU.min), "diffs")
                    dve.wait_ge(exps, 5)
                    step(nc.vector.tensor_tensor(be[:], beta, ex[:, 0, :], ALU.mult))
                    dve.wait_ge(grams, 1)
                    step(nc.vector.tensor_tensor(low[:], bank(2), e2[:], ALU.mult))
                    step(nc.vector.tensor_tensor(low[:], low[:], over(beta), ALU.mult))
                    step(nc.vector.tensor_tensor(low[:], low[:], mask(g.strict), ALU.mult), "low")
                    step(nc.vector.tensor_tensor(aq[:], bank(3), e1[:], ALU.mult))
                    step(nc.vector.tensor_tensor(aq[:], aq[:], mask(g.triu), ALU.mult), "aq")
                    dve.wait_ge(grams, 2)
                    step(nc.vector.tensor_copy(lowT[:], bank(4)))

                    def joins(s, a):
                        put(nc.vector.tensor_tensor(lev[:, HALF_H[a]], lowT[:, HALF_H[a]],
                                                    g.lev[s].unsqueeze(1).to_broadcast([P, H // 2, P]), ALU.mult),
                            f"lev{s}{a}")
                    for a in range(2):
                        joins(0, a)
                    for s in range(LEVELS):
                        for a in range(2):
                            dve.wait_ge(level_p, 2 * s + a + 1)
                            put(nc.vector.tensor_copy(Pm[:, HALF_H[a]], bank(P_BANK[a])[:, HALF_H[a]]), f"P{s}{a}")
                        for a in range(2):
                            dve.wait_ge(level_m, 2 * s + a + 1)
                            for buf, banks in ((M, M_BANK), (MT, MT_BANK)):
                                half = buf[:, HALF_H[a]]
                                put(nc.vector.tensor_tensor(half, half, bank(banks[a])[:, HALF_H[a]], ALU.subtract))
                            if s + 1 < LEVELS:
                                joins(s + 1, a)
                    dve.wait_ge(state_read, 1)
                    step(nc.vector.tensor_tensor(t1[:], bank(0), over(be[:]), ALU.mult))
                    step(nc.vector.tensor_tensor(r[:], vc, over(beta), ALU.mult))
                    step(nc.vector.tensor_tensor(r[:], r[:], t1[:], ALU.subtract), "rhs")
                    dve.wait_ge(solved, 1)
                    step(nc.vector.tensor_copy(vnew[:], bank(2)), "vnew")
                    step(nc.vector.tensor_tensor(vs[:], vnew[:], over(ex[:, 2, :]), ALU.mult), "vs")
                    step(nc.vector.tensor_tensor(t1[:], bank(1), over(ex[:, 0, :]), ALU.mult))
                    step(nc.vector.tensor_tensor(S[:], S[:], over(ex[:, 1, :]), ALU.mult))
                    dve.wait_ge(out_ready, 1)
                    step(nc.vector.tensor_tensor(o_all[:, ds(c, 1), :, :].rearrange("p a h n -> p (a h) n"),
                                                 t1[:], bank(3), ALU.add))
                    step(nc.vector.tensor_tensor(S[:], S[:], bank(4), ALU.add))

                @block.scalar
                def _(act):
                    nc.scalar.copy(qk[:], conv[:, 0:2 * H, ds(c * P, P)])
                    nc.scalar.copy(kc[:], kn[:, ds(c, 1), :, :].rearrange("p a h n -> p (a h) n")).then_inc(fetched, 1)
                    act.wait_ge(vec, V["gc"])
                    nc.scalar.activation(ex[:, 0:2, :].rearrange("p a h -> p (a h)"), gc[:], ACT.Exp).then_inc(exps, 1)
                    nc.scalar.activation(ex[:, 2, :], dif[:], ACT.Exp).then_inc(exps, 1)
                    act.wait_ge(vec, V["diffs"])
                    nc.scalar.activation(e1[:], e1[:], ACT.Exp).then_inc(exps, 1)
                    nc.scalar.activation(e2[:], e2[:], ACT.Exp).then_inc(exps, 2)

                @block.tensor
                def _(pe):
                    def heads(bank_no, lhs, rhs, which=slice(0, H)):
                        for h in range(which.start, which.stop):
                            last = nc.tensor.matmul(bank(bank_no)[:, h, :], lhs(h), rhs(h), start=True, stop=True)
                        return last
                    pe.wait_ge(vec, V["g_spread"])
                    heads(0, lambda h: gbc[:, h, :], lambda h: g.triu)
                    nc.tensor.matmul(g.ps[:, 1, 0:H], g.triu, gg, start=True, stop=True)
                    nc.tensor.matmul(g.ps[:, 1, H:2 * H], g.ones, gg, start=True, stop=True).then_inc(sums, 1)
                    pe.wait_ge(fetched, 1)
                    heads(2, lambda h: tok(H + h), lambda h: tok(H + h))
                    heads(3, lambda h: tok(H + h), lambda h: tok(h)).then_inc(grams, 1)
                    pe.wait_ge(vec, V["low"])
                    for h in range(H):
                        last = nc.tensor.transpose(bank(4)[:, h, :], low[:, h, :], g.ident)
                    last.then_inc(grams, 1)
                    for s in range(LEVELS):
                        for a in range(2):
                            pe.wait_ge(vec, V[f"lev{s}{a}"])
                            heads(P_BANK[a], lambda h: lev[:, h, :], lambda h: M[:, h, :], HALF_H[a]).then_inc(level_p, 1)
                        for a in range(2):
                            pe.wait_ge(vec, V[f"P{s}{a}"])
                            heads(M_BANK[a], lambda h: MT[:, h, :], lambda h: Pm[:, h, :], HALF_H[a])
                            heads(MT_BANK[a], lambda h: Pm[:, h, :], lambda h: MT[:, h, :], HALF_H[a]).then_inc(level_m, 1)
                    heads(0, lambda h: tok(H + h), lambda h: S[:, h, :])
                    heads(1, lambda h: tok(h), lambda h: S[:, h, :]).then_inc(state_read, 1)
                    pe.wait_ge(vec, V["rhs"])
                    heads(2, lambda h: MT[:, h, :], lambda h: r[:, h, :]).then_inc(solved, 1)
                    pe.wait_ge(vec, V["vs"])
                    heads(3, lambda h: aq[:, h, :], lambda h: vnew[:, h, :])
                    heads(4, lambda h: kc[:, h, :], lambda h: vs[:, h, :]).then_inc(out_ready, 1)
        with stage(g, "stored") as (block, stored):
            @block.sync
            def _(sp):
                sp.dma_start(d["p_delta"].rearrange("l b h k v -> k (l b) h v")[:, ds(l, 1), :, :]
                             .rearrange("k a h v -> k (a h) v"), S[:]).then_inc(stored, 16)
                sp.wait_ge(stored, 16)


def delta_sample(g, l, d, conv, gb, o_all):
    nc = g.nc
    N = B * H
    with ExitStack() as ctx:
        def sb(name, *shape):
            return ctx.enter_context(g.buffer(name, shape, FP32))
        S = sb("states", P, N, DK)
        ud = sb("u_blocks", N, N, DK)
        rows = sb("rows", N, 2, P)
        kq = sb("kq", P, N, 2)
        vv = sb("vv", P, N)
        ab = sb("ab", P, B, 2 * H)
        eg = sb("eg", P, B, H)
        bb = sb("bb", P, B, H)
        prod = sb("prod", P, N)
        u = sb("u", P, N)
        t1 = sb("t1s", P, N)
        o = sb("o_s", P, H, B)

        def bh(x):
            return x.rearrange("p (b h) -> p b h", b=B)

        def cols(first):
            return conv[:, first:first + H, T:TOK].rearrange("p h b -> p b h")
        with stage(g, "states_in", "ab_out", "ab_in", "exped", "stored") as (
                block, states_in, ab_out, ab_in, exped, stored):
            @block.sync
            def _(sp):
                sp.dma_start(g.scratch_ab, gb[0:B, TT, :]).then_inc(ab_out, 16)
                for n in range(0, N, 8):
                    sp.dma_start(S[:, n:n + 8, :], d["state_delta"].rearrange("l b h k v -> k (l b h) v")
                                 [:, ds(l * N + n, 8), :]).then_inc(states_in, 16)
                sp.wait_ge(ab_out, 16)
                sp.dma_start(ab[:].rearrange("p b x -> p (b x)"),
                             g.scratch_ab.rearrange("(a b) x -> a (b x)", a=1).to_broadcast([P, B * 2 * H])
                             ).then_inc(ab_in, 16)
                sp.wait_ge(states_in, 4 * 16)
                sp.wait_ge(ab_in, 16)

            @block.scalar
            def _(act):
                act.wait_ge(ab_in, 16)
                nc.scalar.activation(eg[:], ab[:, :, 0:H], ACT.Exp)
                nc.scalar.copy(bb[:], ab[:, :, H:2 * H])

            @block.vector
            def _(dve):
                nc.vector.memset(o_all[:, TT, :, :], 0.0)
                nc.vector.tensor_copy(kq[:].rearrange("p (b h) x -> p b h x", b=B)[:, :, :, 0], cols(H))
                nc.vector.tensor_copy(kq[:].rearrange("p (b h) x -> p b h x", b=B)[:, :, :, 1], cols(0))
                nc.vector.tensor_copy(bh(vv[:]), cols(2 * H))
        with stage(g, "vec", "multiplied", "turned", "outer", "o_turned", "stored") as (
                block, vec, multiplied, turned, outer, o_turned, stored):
            egf = eg[:].rearrange("p b h -> p (b h)")
            bbf = bb[:].rearrange("p b h -> p (b h)")
            dots = g.ps[:, 0, 0:2 * N].rearrange("p (n x) -> p n x", x=2)

            @block.vector
            def _(dve):
                step = in_order(dve, vec)
                step(nc.vector.tensor_tensor(prod[:], kq[:, :, 0], kq[:, :, 1], ALU.mult))
                dve.wait_ge(multiplied, 1)
                step(nc.vector.tensor_tensor(t1[:], dots[:, :, 0], egf, ALU.mult))
                step(nc.vector.tensor_tensor(t1[:], vv[:], t1[:], ALU.subtract))
                step(nc.vector.tensor_tensor(u[:], t1[:], bbf, ALU.mult))
                step(nc.vector.tensor_tensor(t1[:], dots[:, :, 1], egf, ALU.mult))
                step(nc.vector.tensor_tensor(prod[:], u[:], g.ps[:, 1, 0:N], ALU.mult))
                step(nc.vector.tensor_tensor(o[:].rearrange("p h b -> p b h"), bh(t1[:]), bh(prod[:]), ALU.add))
                step(nc.vector.tensor_tensor(S[:], S[:], egf.unsqueeze(2).to_broadcast([P, N, DK]), ALU.mult))
                dve.wait_ge(turned, 1)
                step(nc.vector.tensor_copy(rows[:].rearrange("n a x -> n (a x)"), g.ps[0:N, 2, 0:2 * P]))
                step(nc.vector.tensor_tensor(ud[:], rows[:, 1:2, :].to_broadcast([N, N, DK]),
                                             g.ident[0:N, 0:N].unsqueeze(2).to_broadcast([N, N, DK]), ALU.mult))
                for i in range(N // 4):
                    dve.wait_ge(outer, i + 1)
                    step(nc.vector.tensor_tensor(S[:, 4 * i:4 * i + 4, :], S[:, 4 * i:4 * i + 4, :],
                                                 g.ps[:, 4 + i % 4, :].rearrange("p (n v) -> p n v", n=4), ALU.add))
                dve.wait_ge(o_turned, 1)
                nc.vector.tensor_copy(o_all[0:B, TT, :, :].rearrange("b h v -> b (h v)"), g.ps[0:B, 3, :])

            @block.tensor
            def _(pe):
                for n in range(N):
                    nc.tensor.matmul(dots[:, n, :], S[:, n, :], kq[:, n, :], start=True, stop=True)
                pe.wait_ge(vec, 1)
                nc.tensor.matmul(g.ps[:, 1, 0:N], g.ones, prod[:], start=True, stop=True).then_inc(multiplied, 1)
                pe.wait_ge(vec, 7)
                nc.tensor.transpose(g.ps[0:N, 2, 0:P], kq[:, :, 0], g.ident)
                nc.tensor.transpose(g.ps[0:N, 2, P:2 * P], u[:], g.ident).then_inc(turned, 1)
                for h in range(H):
                    last = nc.tensor.transpose(g.ps[0:B, 3, h * P:(h + 1) * P], o[:, h, :], g.ident)
                last.then_inc(o_turned, 1)
                for i in range(N // 4):
                    pe.wait_ge(vec, 10 if i < 4 else 10 + i - 3)
                    nc.tensor.matmul(g.ps[:, 4 + i % 4, :], rows[:, 0, :],
                                     ud[:, 4 * i:4 * i + 4, :].rearrange("p n v -> p (n v)"),
                                     start=True, stop=True).then_inc(outer, 1)

            @block.sync
            def _(sp):
                sp.wait_ge(vec, 10 + N // 4)
                sp.dma_start(d["s_delta"].rearrange("l b h k v -> k (l b h) v")[:, ds(l * N, N), :], S[:]).then_inc(stored, 16)
                sp.wait_ge(stored, 16)


def turn_tokens(g, src, dst, tiles):
    nc = g.nc
    with stage(g, "turned", "copied") as (block, turned, copied):
        @block.tensor
        def _(pe):
            for t in range(tiles):
                if t >= 2:
                    pe.wait_ge(copied, t - 1)
                for k in range(4):
                    last = nc.tensor.transpose(g.ps[:, t % 2, k * P:(k + 1) * P], src(t, k), g.ident)
                last.then_inc(turned, 1)

        @block.scalar
        def _(act):
            for t in range(tiles):
                act.wait_ge(turned, t + 1)
                nc.scalar.copy(dst[:, :, t * P:(t + 1) * P],
                               g.ps[:, t % 2, :].rearrange("p (k n) -> p k n", k=4)).then_inc(copied, 1)


def delta_output(g, l, d, o_all, ot):
    nc = g.nc
    G = NT * H
    with ExitStack() as ctx:
        def sb(name, *shape):
            return ctx.enter_context(g.buffer(name, shape, FP32))
        sq = sb("sqo", P, NT, H * DK)
        gain = sb("gaino", P, DK)
        ss = sb("sso", P, 4, G)
        of = o_all[:].rearrange("p t h v -> p (t h) v")
        sqf = sq[:].rearrange("p t (h v) -> p (t h) v", h=H)
        with stage(g, "gain_in", "vec", "act_done") as (block, gain_in, vec, act_done):
            @block.sync
            def _(sp):
                sp.dma_start(gain[:], d["dn_norm"][ds(l, 1), :].to_broadcast([P, DK])).then_inc(gain_in, 16)

            @block.vector
            def _(dve):
                step = in_order(dve, vec)
                step(nc.vector.tensor_tensor(sqf, of, of, ALU.mult))
                step(nc.vector.tensor_reduce(ss[:, 0, :], sqf, AX.X, ALU.add))
                step(nc.vector.tensor_scalar(ss[:, 1, :], ss[:, 0, :], 1.0 / DK, EPS, ALU.mult, ALU.add))
                dve.wait_ge(act_done, 2)
                step(nc.vector.reciprocal(ss[:, 3, :], ss[:, 2, :]))
                step(nc.vector.tensor_tensor(of, of, ss[:, 3, :].unsqueeze(2).to_broadcast([P, G, DK]), ALU.mult))
                dve.wait_ge(gain_in, 16)
                step(nc.vector.tensor_tensor(of, of, gain[:].unsqueeze(1).to_broadcast([P, G, DK]), ALU.mult))
                o3 = o_all[:].rearrange("p t h v -> p t (h v)")
                step(nc.vector.tensor_tensor(sq[:], sq[:], g.nat[:, :, 0:H * DK], ALU.mult))
                step(nc.vector.tensor_tensor(o3, o3, sq[:], ALU.mult))

            @block.scalar
            def _(act):
                act.wait_ge(vec, 3)
                nc.scalar.activation(ss[:, 2, :], ss[:, 1, :], ACT.Sqrt).then_inc(act_done, 1)
                nc.scalar.activation(sq[:], g.nat[:, :, 0:H * DK], ACT.Sigmoid).then_inc(act_done, 1)
        turn_tokens(g, lambda t, k: o_all[:, t, k, :], ot, NT)



def rotary(g, l, d):
    nc = g.nc
    with ExitStack() as ctx:
        tmp = ctx.enter_context(g.buffer("rot", [P, 4, NT, AH + KV, HALF], FP32))
        with stage(g, "vec", "stored") as (block, vec, stored):
            @block.vector
            def _(dve):
                step = in_order(dve, vec)
                for first, heads in ((N_Q, AH + KV), (N_QI, IH + 1)):
                    v = g.nat[:, :, first:first + heads * HD].rearrange("p t (h e) -> p t h e", e=HD)
                    x1, x2 = v[:, :, :, 0:HALF], v[:, :, :, HALF:ROT]
                    cos = g.cos.unsqueeze(2).to_broadcast([P, NT, heads, HALF])
                    sin = g.sin.unsqueeze(2).to_broadcast([P, NT, heads, HALF])
                    for t in range(NT):
                        for n, (x, y) in enumerate(((x1, cos), (x2, sin), (x2, cos), (x1, sin))):
                            step(nc.vector.tensor_tensor(tmp[:, n, t, 0:heads, :], x[:, t], y[:, t], ALU.mult))
                        step(nc.vector.tensor_tensor(x1[:, t], tmp[:, 0, t, 0:heads, :], tmp[:, 1, t, 0:heads, :], ALU.subtract))
                        step(nc.vector.tensor_tensor(x2[:, t], tmp[:, 2, t, 0:heads, :], tmp[:, 3, t, 0:heads, :], ALU.add))

            @block.sync
            def _(sp):
                sp.wait_ge(vec, 2 * 6 * NT)
                for dst, c0, w in ((d["p_k"].rearrange("a (t p) l k e -> p (a t) l (k e)", p=P), N_K, KV * HD),
                                   (d["p_v"].rearrange("a (t p) l k e -> p (a t) l (k e)", p=P), N_V, KV * HD),
                                   (d["p_kidx"].rearrange("a (t p) l e -> p (a t) l e", p=P), N_KI, ID)):
                    sp.dma_start(dst[:, :, ds(l, 1), :].rearrange("p t a e -> p t (a e)"),
                                 g.nat[:, 0:TT, c0:c0 + w]).then_inc(stored, 16)
                for dst, c0, w in ((d["s_k"].rearrange("b a l k e -> (b a) l (k e)"), N_K, KV * HD),
                                   (d["s_v"].rearrange("b a l k e -> (b a) l (k e)"), N_V, KV * HD),
                                   (d["s_kidx"].rearrange("b a l e -> (b a) l e"), N_KI, ID)):
                    sp.dma_start(dst[:, ds(l, 1), :].rearrange("b a e -> b (a e)"),
                                 g.nat[0:B, TT, c0:c0 + w]).then_inc(stored, 16)
                sp.wait_ge(stored, 6 * 16)


def sparse_prompt(g, l, d, oat):
    nc = g.nc
    with ExitStack() as ctx:
        def sb(name, *shape):
            return ctx.enter_context(g.buffer(name, shape, FP32))
        kT = sb("kT", HD, KV, T)
        kiT = sb("kiT", ID, T)
        oa = sb("oa", P, TT, AH * HD)
        with stage(g, "turned", "copied") as (block, turned, copied):
            @block.tensor
            def _(pe):
                for n, c0 in enumerate((N_K, N_K + HD, N_KI)):
                    for t in range(TT):
                        last = nc.tensor.transpose(g.ps[0:HD, n, t * P:(t + 1) * P], g.nat[:, t, c0:c0 + HD], g.ident)
                    last.then_inc(turned, 1)

            @block.vector
            def _(dve):
                for n, dst in enumerate((kT[:, 0, :], kT[:, 1, :], kiT[:])):
                    dve.wait_ge(turned, n + 1)
                    nc.vector.tensor_copy(dst, g.ps[0:HD, n, :])
        with ExitStack() as inner:
            def sbi(name, *shape):
                return inner.enter_context(g.buffer(name, shape, FP32))
            qc = sbi("qc", P, AH * HD)
            qic = sbi("qic", P, IH * ID)
            wic = sbi("wic", P, IH)
            qT = sbi("qT", HD, AH, P)
            qiT = sbi("qiT", ID, IH, P)
            rl = sbi("rl", P, IH, T)
            cm = sbi("cm", P, T)
            acc = sbi("acc", P, T)
            work = sbi("work", P, T)
            pen = sbi("pen", P, T)
            m8 = sbi("m8", P, 2, 8)
            pr = sbi("pr", P, 2, T)
            nm = sbi("nm", P, AH)
            sums = sbi("sums", P, AH)
            pT = sbi("pT", P, 2, TT, P)
            with nc.Fori(0, TT) as qt:
                with stage(g, "fetched", "turned", "back", "scored", "relued", "vec", "multiplied", "shifted", "exped",
                           "p_turned", "p_back", "out_ready") as (
                               block, fetched, turned, back, scored, relued, vec, multiplied, shifted, exped,
                               p_turned, p_back, out_ready):
                    @block.scalar
                    def _(act):
                        def cols(c0, w):
                            return g.nat[:, ds(qt, 1), c0:c0 + w].rearrange("p a n -> p (a n)")
                        nc.scalar.copy(qc[:], cols(N_Q, AH * HD))
                        nc.scalar.copy(qic[:], cols(N_QI, IH * ID))
                        nc.scalar.mul(wic[:], cols(N_WI, IH), IH ** -0.5).then_inc(fetched, 1)
                        act.wait_ge(turned, 1)
                        for b in range(2):
                            nc.scalar.copy(qT[:, 4 * b:4 * b + 4, :].rearrange("p h n -> p (h n)"), g.ps[0:HD, b, :])
                        nc.scalar.copy(qiT[:].rearrange("p h n -> p (h n)"), g.ps[0:ID, 2, :]).then_inc(back, 1)
                        for h in range(IH):
                            act.wait_ge(scored, h + 1)
                            nc.scalar.activation(rl[:, h, :], g.ps[:, 4 + h, :], ACT.Relu, scale=ID ** -0.5).then_inc(relued, 1)
                        for h in range(AH):
                            act.wait_ge(shifted, h + 1)
                            nc.scalar.activation(pr[:, h % 2, :], pr[:, h % 2, :], ACT.Exp, bias=nm[:, h:h + 1],
                                                 accum_out=sums[:, h:h + 1]).then_inc(exped, 1)
                            act.wait_ge(p_turned, h + 1)
                            nc.scalar.copy(pT[:, h % 2, :, :].rearrange("p k n -> p (k n)"),
                                           g.ps[:, 4 + h % 2, :]).then_inc(p_back, 1)

                    @block.tensor
                    def _(pe):
                        pe.wait_ge(fetched, 1)
                        for h in range(AH):
                            nc.tensor.transpose(g.ps[0:HD, h // 4, (h % 4) * P:(h % 4 + 1) * P],
                                                qc[:, h * HD:(h + 1) * HD], g.ident)
                        for h in range(IH):
                            last = nc.tensor.transpose(g.ps[0:ID, 2, h * P:(h + 1) * P], qic[:, h * ID:(h + 1) * ID], g.ident)
                        last.then_inc(turned, 1)
                        pe.wait_ge(back, 1)
                        for h in range(IH):
                            nc.tensor.matmul(g.ps[:, 4 + h, :], qiT[:, h, :], kiT[:], start=True, stop=True).then_inc(scored, 1)

                        def scores(h):
                            nc.tensor.matmul(g.ps[:, h % 4, :], qT[:, h, :], kT[:, h // (AH // KV), :],
                                             start=True, stop=True).then_inc(multiplied, 1)
                        for h in range(4):
                            scores(h)
                        pe.wait_ge(relued, IH)
                        for h in range(AH):
                            pe.wait_ge(exped, h + 1)
                            if h >= 2:
                                pe.wait_ge(p_back, h - 1)
                            for k in range(TT):
                                last = nc.tensor.transpose(g.ps[:, 4 + h % 2, k * P:(k + 1) * P],
                                                           pr[:, h % 2, k * P:(k + 1) * P], g.ident)
                            last.then_inc(p_turned, 1)
                            if h + 4 < AH:
                                scores(h + 4)
                            pe.wait_ge(p_back, h + 1)
                            c0 = N_V + (h // (AH // KV)) * HD
                            for k in range(TT):
                                last = nc.tensor.matmul(g.ps[:, 6, h * HD:(h + 1) * HD], pT[:, h % 2, k, :],
                                                        g.nat[:, k, c0:c0 + HD], start=(k == 0), stop=(k == TT - 1))
                            if h == AH - 1:
                                last.then_inc(out_ready, 1)

                    @block.vector
                    def _(dve):
                        step = in_order(dve, vec)
                        step(nc.vector.tensor_scalar(cm[:], g.iota512, g.tpos[:, ds(qt, 1)], None, ALU.is_le))
                        step(nc.vector.tensor_scalar(pen[:], cm[:], -1.0, BIG, ALU.add, ALU.mult))
                        dve.wait_ge(fetched, 1)
                        for h in range(IH):
                            dve.wait_ge(relued, h + 1)
                            if h == 0:
                                step(nc.vector.tensor_scalar(acc[:], rl[:, h, :], wic[:, h:h + 1], 0.0, ALU.mult, ALU.add))
                            else:
                                step(nc.vector.scalar_tensor_tensor(acc[:], rl[:, h, :], wic[:, h:h + 1], acc[:],
                                                                    ALU.mult, ALU.add))
                        step(nc.vector.tensor_tensor(acc[:], acc[:], cm[:], ALU.mult))
                        step(nc.vector.tensor_tensor(work[:], acc[:], pen[:], ALU.add))
                        for r in range(TOPK_P // 8):
                            step(nc.vector.max(m8[:, r % 2, :], work[:]))
                            step(nc.vector.match_replace(work[:], m8[:, r % 2, :], work[:], TAKEN))
                        step(nc.vector.tensor_scalar(work[:], work[:], -3.2e38, None, ALU.is_le))
                        step(nc.vector.tensor_tensor(work[:], work[:], cm[:], ALU.mult))
                        step(nc.vector.tensor_scalar(pen[:], work[:], -1.0, 1.0e30, ALU.add, ALU.mult))
                        for h in range(AH):
                            dve.wait_ge(multiplied, h + 1)
                            if h >= 2:
                                dve.wait_ge(p_turned, h - 1)
                            step(nc.vector.scalar_tensor_tensor(pr[:, h % 2, :], g.ps[:, h % 4, :], HD ** -0.5, pen[:],
                                                                ALU.mult, ALU.add))
                            nc.vector.tensor_reduce(nm[:, h:h + 1], pr[:, h % 2, :], AX.X, ALU.max,
                                                    negate=True).then_inc(shifted, 1)
                        dve.wait_ge(exped, AH)
                        step(nc.vector.reciprocal(sums[:], sums[:]))
                        dve.wait_ge(out_ready, 1)
                        nc.vector.tensor_tensor(
                            oa[:, ds(qt, 1), :].rearrange("p a (h e) -> p (a h) e", e=HD),
                            g.ps[:, 6, :].rearrange("p (h e) -> p h e", e=HD),
                            sums[:].unsqueeze(2).to_broadcast([P, AH, HD]), ALU.mult)
        turn_tokens(g, lambda t, k: oa[:, t, k * P:(k + 1) * P], oat, TT)


def softmax_rows(g, rows, width, s, small, sem_names=("vec", "exped")):
    nc = g.nc
    with stage(g, *sem_names) as (block, vec, exped):
        @block.vector
        def _(dve):
            step = in_order(dve, vec)
            step(nc.vector.tensor_reduce(small[0:rows, 0:1], s[:], AX.X, ALU.max, negate=True))
            dve.wait_ge(exped, 1)
            step(nc.vector.reciprocal(small[0:rows, 2:3], small[0:rows, 1:2]))
            nc.vector.tensor_scalar(s[:], s[:], small[0:rows, 2:3], None, ALU.mult)

        @block.scalar
        def _(act):
            act.wait_ge(vec, 1)
            nc.scalar.activation(s[:], s[:], ACT.Exp, bias=small[0:rows, 0:1],
                                 accum_out=small[0:rows, 1:2]).then_inc(exped, 1)


def diag(buf, w):
    return buf.rearrange("p (b x) -> p b x", x=(B + 1) * w)[:, :, 0:w]


def best_in_order(g, dve, vec, values, m, i, out, index):
    nc = g.nc
    w = m.shape[-1]
    with dve.Fori(0, TOPK_S // w) as r:
        step = in_order(dve, vec)
        for x in range(0, w, 8):
            step(nc.vector.max(m[:, x:x + 8], values))
            step(nc.vector.max_index(i[:, x:x + 8], m[:, x:x + 8], values))
            step(nc.vector.match_replace(values, m[:, x:x + 8], values, TAKEN))
        if out is not None:
            step(nc.vector.tensor_copy(out[:, ds(r * w, w)], m))
        step(nc.vector.tensor_copy(index[:, ds(r * w, w)], i))
        dve.sem_clear(vec)


def sample_scores(g, l, d, seg):
    nc = g.nc
    GRP = 4
    NG = PAGES // GRP
    KEYS = PAST + 8
    with ExitStack() as ctx:
        def sb(name, *shape, dt=FP32):
            return ctx.enter_context(g.buffer(name, shape, dt))
        score = sb("score", B, KEYS)

        with ExitStack() as inner:
            def sbi(name, *shape, dt=FP32):
                return inner.enter_context(g.buffer(name, shape, dt))
            qiz = [sbi(f"qiz{n}", P, B * (B + 1) * IH) for n in range(2)]
            ki = sbi("ki", P, 2, B * GRP, ID)
            kiT = sbi("kiT_s", P, 2, GRP // 2, P)
            relu = sbi("relu", P, 2, GRP * P)
            qi2 = sbi("qi2", B, IH, 2, ID)
            wcol = sbi("wcol", B * IH, 1)
            wsel = sbi("wsel", P, B)
            with stage(g, "vec", "turned", "w_out", "w_in", "cleared") as (block, vec, turned, w_out, w_in, cleared):
                @block.sync
                def _(sp):
                    sp.dma_start(g.scratch_w, g.nat[0:B, TT, N_WI:N_WI + IH]).then_inc(w_out, 16)
                    sp.wait_ge(w_out, 16)
                    sp.dma_start(wcol[:], g.scratch_w.rearrange("b (h a) -> (b h) a", a=1)).then_inc(w_in, 16)

                @block.vector
                def _(dve):
                    step = in_order(dve, vec)
                    for n in range(2):
                        step(nc.vector.memset(qiz[n][:], 0.0))
                        step(nc.vector.tensor_copy(qi2[:, :, n, :], g.nat[0:B, TT, N_QI:N_QI + IH * ID]
                                                   .rearrange("b (h e) -> b h e", h=IH)))
                    step(nc.vector.memset(wsel[:], 0.0))
                    step(nc.vector.memset(relu[:], 0.0))
                    step(nc.vector.memset(seg[:], -BIG))
                    dve.wait_ge(turned, 1)
                    for n in range(2):
                        nc.vector.tensor_copy(
                            diag(qiz[n], IH)[n * ID:(n + 1) * ID],
                            g.ps[n * ID:(n + 1) * ID, 1, 0:IH * B].rearrange("p (h b) -> p b h", b=B))
                    dve.wait_ge(w_in, 16)
                    nc.vector.tensor_scalar(wsel[0:B * IH, :], g.own[0:B * IH, :], wcol[:], IH ** -0.5, ALU.mult, ALU.mult)

                @block.tensor
                def _(pe):
                    pe.wait_ge(vec, 4)
                    for h in range(IH):
                        last = nc.tensor.transpose(g.ps[:, 1, h * B:(h + 1) * B],
                                                   qi2[:, h].rearrange("b a e -> b (a e)"), g.ident[0:B, 0:B])
                    last.then_inc(turned, 1)

            with stage(g, "ki_in0", "ki_in1", "turned", "back", "dotted", "relued", "weighed", "kept") as (
                    block, ki_in0, ki_in1, turned, back, dotted, relued, weighed, kept):
                ki_in = (ki_in0, ki_in1)

                def load(eng, c, u, q):
                    for b in (range(0, 5), range(5, B))[q]:
                        for pg in range(GRP):
                            page = eng.value_load(g.pages[0:1, ds(c * GRP + (b * PAGES + pg), 1)],
                                                  min_val=0, max_val=d["cache_kidx"].shape[0] - 1)
                            eng.dma_start(ki[:, u, b * GRP + pg, :],
                                          d["cache_kidx"][ds(page, 1), :, ds(l, 1), :].rearrange("a s b e -> (a s) (b e)")
                                          ).then_inc(ki_in[u], 16)

                @block.sync
                def _(sp):
                    for u in range(2):
                        load(sp, u, u, 0)
                    with sp.Fori(1, NG // 2) as it:
                        for u in range(2):
                            sp.wait_ge(turned, (it - 1) * (2 * B) + (u + 1) * B)
                            load(sp, it * 2 + u, u, 0)

                @block.tensor
                def _(pe):
                    with pe.Fori(0, NG // 2) as it:
                        for u in range(2):
                            pe.wait_ge(ki_in[u], it * (16 * B * GRP) + 16 * B * GRP)

                            def dots(b):
                                pe.wait_ge(back, it * (2 * B) + (u * B + b + 1))
                                for n in range(2):
                                    last = nc.tensor.matmul(
                                        g.ps[0:B * IH, 4 + 2 * u + n, 0:GRP * P // 2], qiz[n][:, b * B * IH:(b + 1) * B * IH],
                                        kiT[:, b % 2].rearrange("p a s -> p (a s)"), start=(b == 0), stop=(b == B - 1))
                                return last
                            for b in range(B):
                                for a in range(GRP // 2):
                                    pair = ki[:, u, b * GRP + 2 * a:b * GRP + 2 * a + 2, :]
                                    last = nc.tensor.transpose(g.ps[:, b % 2, a * P:(a + 1) * P],
                                                               pair.rearrange("p n e -> p (n e)"), g.ident)
                                last.then_inc(turned, 1)
                                if b >= 1:
                                    last = dots(b - 1)
                            dots(B - 1).then_inc(dotted, 1)
                            pe.wait_ge(relued, it * 2 + (u + 1))
                            nc.tensor.matmul(g.ps[0:B, 2 + u, :], wsel[:], relu[:, u, :], start=True,
                                             stop=True).then_inc(weighed, 1)

                @block.scalar
                def _(act):
                    def turn_back(it, u):
                        for n in range(u * B, (u + 1) * B):
                            act.wait_ge(turned, it * (2 * B) + (n + 1))
                            nc.scalar.copy(kiT[:, n % 2].rearrange("p a s -> p (a s)"),
                                           g.ps[:, n % 2, 0:GRP * P // 2]).then_inc(back, 1)

                    for u in range(2):
                        load(act, u, u, 1)
                    with act.Fori(0, NG // 2 - 1) as it:
                        for u in range(2):
                            turn_back(it, u)
                            load(act, it * 2 + (u + 2), u, 1)
                    for u in range(2):
                        turn_back(NG // 2 - 1, u)

                @block.vector
                def _(dve):
                    with dve.Fori(0, NG // 2) as it:
                        for u in range(2):
                            dve.wait_ge(dotted, it * 2 + (u + 1))
                            for n in range(2):
                                last = nc.vector.tensor_scalar(
                                    relu[0:B * IH, u, :].rearrange("p (a n s) -> p a n s", n=2, s=P)[:, :, n],
                                    g.ps[0:B * IH, 4 + 2 * u + n, 0:GRP * P // 2].rearrange("p (a s) -> p a s", s=P),
                                    ID ** -0.5, 0.0, ALU.mult, ALU.max)
                            last.then_inc(relued, 1)
                            dve.wait_ge(weighed, it * 2 + (u + 1))
                            nc.vector.tensor_scalar(score[:, ds((it * 2 + u) * (GRP * P), GRP * P)], g.ps[0:B, 2 + u, :],
                                                    0.0, None, ALU.add).then_inc(kept, 1)

        with ExitStack() as inner:
            def sbi(name, *shape, dt=FP32):
                return inner.enter_context(g.buffer(name, shape, dt))
            own = sbi("own", B, IH, ID)
            owns = sbi("owns", B, 4, IH)
            with stage(g, "vec", "spread") as (block, vec, spread):
                @block.vector
                def _(dve):
                    step = in_order(dve, vec)
                    qi = g.nat[0:B, TT, N_QI:N_QI + IH * ID].rearrange("b (h e) -> b h e", h=IH)
                    kx = g.nat[0:B, TT:TT + 1, N_KI:N_KI + ID].to_broadcast([B, IH, ID])
                    step(nc.vector.tensor_tensor(own[:], qi, kx, ALU.mult))
                    step(nc.vector.tensor_reduce(owns[:, 0, :], own[:], AX.X, ALU.add))
                    step(nc.vector.tensor_scalar(owns[:, 1, :], owns[:, 0, :], ID ** -0.5, 0.0, ALU.mult, ALU.max))
                    step(nc.vector.tensor_scalar(owns[:, 2, :], g.nat[0:B, TT, N_WI:N_WI + IH], IH ** -0.5, None, ALU.mult))
                    step(nc.vector.tensor_tensor(owns[:, 3, :], owns[:, 1, :], owns[:, 2, :], ALU.mult))
                    step(nc.vector.tensor_reduce(owns[:, 0, 0:1], owns[:, 3, :], AX.X, ALU.add))
                    step(nc.vector.memset(score[:, PAST:KEYS], -BIG))
                    step(nc.vector.tensor_scalar(score[:, PAST:PAST + 1], owns[:, 0, 0:1], 0.0, None, ALU.add))

                @block.sync
                def _(sp):
                    sp.wait_ge(vec, 8)
                    for s in range(SEGS):
                        w = SEG + (KEYS - PAST if s == SEGS - 1 else 0)
                        sp.dma_start(seg[s * B:(s + 1) * B, 0:w], score[:, s * SEG:s * SEG + w]).then_inc(spread, 16)
                    sp.wait_ge(spread, 16 * SEGS)


def sample_lists(g, top, topi, merged):
    nc = g.nc
    with stage(g, "moved") as (block, moved):
        @block.sync
        def _(sp):
            for s in range(SEGS):
                sp.dma_start(merged[:, s * TOPK_S:(s + 1) * TOPK_S], top[s * B:(s + 1) * B, :]).then_inc(moved, 16)
                sp.dma_start(g.scratch_place.rearrange("(b s r) a -> b s (r a)", b=B, s=SEGS)[:, s, :],
                             topi[s * B:(s + 1) * B, :]).then_inc(moved, 16)
            sp.wait_ge(moved, 16 * 2 * SEGS)


def sparse_sample(g, l, d, oat, pos):
    nc = g.nc
    HALVES = TOPK_S // P
    places, all_rows = 16 * B * HALVES, 16 * 3 * B * HALVES
    with ExitStack() as ctx:
        def sb(name, *shape, dt=FP32):
            return ctx.enter_context(g.buffer(name, shape, dt))
        qb = sb("qb", P, B * (B + 1) * AH)
        rows = sb("addresses", P, HALVES, B, dt=I32)
        fresh = sb("fresh", P, HALVES, B)
        small = sb("small", P, 4)

        def q_nat(g4):
            return g.nat[0:B, TT, N_Q:N_Q + AH * HD].rearrange("p (k g e) -> p g k e", k=KV, e=HD)[:, g4]

        with ExitStack() as inner:
            def sbi(name, *shape, dt=FP32):
                return inner.enter_context(g.buffer(name, shape, dt))
            q4 = sbi("q4", B, 4, KV * HD)
            at = sbi("at", P, HALVES * B)
            ati = sbi("ati", P, 2, HALVES * B, dt=I32)
            place = sbi("place", P, HALVES * B)
            posT = sbi("posT", P, HALVES * B)
            posi = sbi("posi", P, 3, HALVES * B, dt=I32)
            posf = sbi("posf", P, 3, HALVES * B)
            hot = sbi("hot", P, HALVES, B, PAGES)
            pti = sbi("pti", P, B * PAGES, dt=I32)
            ptf = sbi("ptf", P, B * PAGES)
            with stage(g, "table_in", "kv_out", "turned", "addressed", "vec") as (
                    block, table_in, kv_out, turned, addressed, vec):
                @block.sync
                def _(sp):
                    sp.dma_start(pti[:], d["page_table"].rearrange("(a b) n -> a (b n)", a=1).to_broadcast([P, B * PAGES])
                                 ).then_inc(table_in, 16)
                    sp.dma_start(g.scratch_kv, g.nat[0:B, TT, N_K:N_K + 2 * KV * HD]).then_inc(kv_out, 16)
                    sp.wait_ge(kv_out, 16)

                @block.tensor
                def _(pe):
                    pe.wait_ge(vec, 5)
                    for x in range(4):
                        nc.tensor.transpose(g.ps[:, 1, x * B:(x + 1) * B], q4[:, x, :], g.ident[0:B, 0:B])
                    for x in range(HALVES):
                        last = nc.tensor.transpose(g.ps[:, 0, x * B:(x + 1) * B], pos[:, x * P:(x + 1) * P], g.ident[0:B, 0:B])
                    last.then_inc(turned, 1)

                @block.gpsimd
                def _(pool):
                    pool.wait_ge(addressed, 1)
                    for n in range(HALVES * B):
                        nc.gpsimd.indirect_dma_start(place[:, n:n + 1], None, g.scratch_place,
                                                     bass.IndirectOffsetOnAxis(ati[:, 1, n:n + 1], 0)
                                                     ).then_inc(g.gathered, 16)

                @block.vector
                def _(dve):
                    step = in_order(dve, vec)
                    step(nc.vector.memset(qb[:], 0.0))
                    for x in range(4):
                        step(nc.vector.tensor_copy(q4[:, x, :].rearrange("b (k e) -> b k e", k=KV), q_nat(x)))
                    dve.wait_ge(table_in, 16)
                    step(nc.vector.tensor_copy(ptf[:], pti[:]))
                    dve.wait_ge(turned, 1)
                    step(nc.vector.tensor_copy(at[:], g.ps[:, 0, 0:HALVES * B]))
                    step(nc.vector.tensor_tensor(
                        at[:].rearrange("p (x b) -> p x b", b=B), at[:].rearrange("p (x b) -> p x b", b=B),
                        g.lists.unsqueeze(1).to_broadcast([P, HALVES, B]), ALU.add))
                    step(nc.vector.tensor_copy(ati[:, 1, :], at[:]))
                    nc.vector.engine_nop().then_inc(addressed, 1)
                    step(nc.vector.tensor_copy(ati[:, 0, :], g.ps[:, 0, 0:HALVES * B]))
                    step(nc.vector.tensor_scalar(posi[:, 0, :], ati[:, 0, :], TOPK_S.bit_length() - 1,
                                                 None, ALU.logical_shift_right))
                    step(nc.vector.tensor_copy(posf[:, 0, :], posi[:, 0, :]))
                    for k in range(KV):
                        nc.vector.tensor_copy(
                            diag(qb, AH)[k * HD:(k + 1) * HD, :, 4 * k:4 * k + 4],
                            g.ps[k * HD:(k + 1) * HD, 1, 0:4 * B].rearrange("p (x b) -> p b x", b=B))
                    dve.wait_ge(g.gathered, l * all_rows + places)
                    step(nc.vector.scalar_tensor_tensor(posf[:, 1, :], posf[:, 0, :], float(SEG), place[:], ALU.mult, ALU.add))
                    step(nc.vector.tensor_copy(posi[:, 0, :], posf[:, 1, :]))
                    step(nc.vector.tensor_scalar(fresh[:].rearrange("p x b -> p (x b)"), posf[:, 1, :],
                                                 float(PAST), None, ALU.is_ge))
                    step(nc.vector.tensor_scalar(posi[:, 1, :], posi[:, 0, :], 7, None, ALU.logical_shift_right))
                    step(nc.vector.tensor_scalar(posi[:, 2, :], posi[:, 0, :], PAGE - 1, None, ALU.bitwise_and))
                    step(nc.vector.tensor_copy(posf[:, 0:2, :], posi[:, 1:3, :]))
                    for x in range(HALVES):
                        step(nc.vector.tensor_tensor(
                            hot[:, x], posf[:, 0, x * B:(x + 1) * B].unsqueeze(2).to_broadcast([P, B, PAGES]),
                            g.iota[:, 0:PAGES].unsqueeze(1).to_broadcast([P, B, PAGES]), ALU.is_equal))
                        step(nc.vector.tensor_tensor(hot[:, x], hot[:, x], ptf[:].rearrange("p (b n) -> p b n", b=B), ALU.mult))
                    step(nc.vector.tensor_reduce(posT[:], hot[:].rearrange("p x b n -> p (x b) n"), AX.X, ALU.add))
                    step(nc.vector.scalar_tensor_tensor(posT[:], posT[:], float(PAGE), posf[:, 1, :], ALU.mult, ALU.add))
                    step(nc.vector.tensor_scalar(posT[:], posT[:], float(DEPTH), g.layer[:], ALU.mult, ALU.add))
                    step(nc.vector.tensor_copy(rows[:].rearrange("p x b -> p (x b)"), posT[:]))
        with ExitStack() as inner:
            def sbi(name, *shape, dt=FP32):
                return inner.enter_context(g.buffer(name, shape, dt))
            ks = sbi("k_sel", P, B, HALVES, KV * HD)
            vs = sbi("v_sel", P, B, HALVES, KV * HD)
            idle = g.wb[:].rearrange("p a k n -> p (a k n)")
            new = idle[:, 0:2 * B * KV * HD].rearrange("p (b a n) -> p b a n", b=B, a=2)
            tmp = idle[:, 2 * B * KV * HD:3 * B * KV * HD].rearrange("p (b n) -> p b n", b=B)
            old = sbi("old", P, HALVES, B)
            ksT = sbi("k_selT", P, 2, 2 * TOPK_S)
            sc = sbi("sc", B * AH, TOPK_S)
            pT = sbi("pT_s", P, HALVES, B * AH)
            with stage(g, "new_in", "vec") as (block, new_in, vec):
                @block.gpsimd
                def _(pool):
                    for x in range(HALVES):
                        for b in range(B):
                            for dst, src in ((ks, d["cache_k"]), (vs, d["cache_v"])):
                                nc.gpsimd.indirect_dma_start(
                                    dst[:, b, x, :], None, src.rearrange("n s l k e -> (n s l) (k e)"),
                                    bass.IndirectOffsetOnAxis(rows[:, x, b:b + 1], 0)).then_inc(g.gathered, 16)

                @block.sync
                def _(sp):
                    sp.dma_start(new.rearrange("p b a e -> p (b a e)"),
                                 g.scratch_kv.rearrange("(a b) x -> a (b x)", a=1).to_broadcast([P, B * 2 * KV * HD])
                                 ).then_inc(new_in, 16)

                @block.vector
                def _(dve):
                    step = in_order(dve, vec)
                    step(nc.vector.tensor_scalar(old[:], fresh[:], -1.0, 1.0, ALU.mult, ALU.add))
                    dve.wait_ge(new_in, 16)
                    dve.wait_ge(g.gathered, l * all_rows + all_rows)
                    for a, buf in enumerate((ks, vs)):
                        for x in range(HALVES):
                            def over(y):
                                return y[:, x, :].unsqueeze(2).to_broadcast([P, B, KV * HD])
                            step(nc.vector.tensor_tensor(tmp, new[:, :, a, :], over(fresh), ALU.mult))
                            step(nc.vector.tensor_tensor(buf[:, :, x, :], buf[:, :, x, :], over(old), ALU.mult))
                            step(nc.vector.tensor_tensor(buf[:, :, x, :], buf[:, :, x, :], tmp, ALU.add))
            with stage(g, "turned", "back", "multiplied") as (block, turned, back, multiplied):
                @block.tensor
                def _(pe):
                    def dots(n):
                        pe.wait_ge(back, n + 1)
                        for b in (2 * n, 2 * n + 1):
                            last = nc.tensor.matmul(g.ps[0:B * AH, 2, 0:TOPK_S], qb[:, b * B * AH:(b + 1) * B * AH],
                                                    ksT[:, n % 2, (b % 2) * TOPK_S:(b % 2 + 1) * TOPK_S],
                                                    start=(b == 0), stop=(b == B - 1))
                        return last
                    for n in range(B // 2):
                        for i in range(2 * HALVES):
                            last = nc.tensor.transpose(g.ps[:, n % 2, i * P:(i + 1) * P],
                                                       ks[:, 2 * n + i // HALVES, i % HALVES, :], g.ident)
                        last.then_inc(turned, 1)
                        if n >= 1:
                            last = dots(n - 1)
                    dots(B // 2 - 1).then_inc(multiplied, 1)

                @block.scalar
                def _(act):
                    for n in range(B // 2):
                        act.wait_ge(turned, n + 1)
                        nc.scalar.copy(ksT[:, n % 2, :], g.ps[:, n % 2, :]).then_inc(back, 1)
                    act.wait_ge(multiplied, 1)
                    nc.scalar.mul(sc[:], g.ps[0:B * AH, 2, 0:TOPK_S], HD ** -0.5)
            softmax_rows(g, B * AH, TOPK_S, sc, small)
            with stage(g, "turned", "back", "out_ready") as (block, turned, back, out_ready):
                @block.tensor
                def _(pe):
                    for x in range(HALVES):
                        last = nc.tensor.transpose(g.ps[:, 0, x * B * AH:(x + 1) * B * AH], sc[:, x * P:(x + 1) * P],
                                                   g.ident[0:B * AH, 0:B * AH])
                    last.then_inc(turned, 1)
                    pe.wait_ge(back, 1)
                    for b in range(B):
                        for k in range(KV):
                            c = b * AH + k * 4
                            for half in range(2):
                                for x in range(HALVES):
                                    last = nc.tensor.matmul(g.ps[half * HD:(half + 1) * HD, 1, c:c + 4],
                                                            vs[:, b, x, k * HD:(k + 1) * HD], pT[:, x, c:c + 4],
                                                            start=(x == 0), stop=(x == HALVES - 1))
                    last.then_inc(out_ready, 1)

                @block.vector
                def _(dve):
                    dve.wait_ge(turned, 1)
                    nc.vector.tensor_copy(pT[:].rearrange("p x n -> p (x n)"), g.ps[:, 0, 0:HALVES * B * AH]).then_inc(back, 1)
                    dve.wait_ge(out_ready, 1)
                    for half in range(2):
                        nc.vector.tensor_copy(
                            oat[half * HD:(half + 1) * HD, :, T:TOK],
                            g.ps[half * HD:(half + 1) * HD, 1, 0:B * AH].rearrange("p (b k a) -> p a k b", k=4, a=2)[:, half])



def branch_gates(g, l, d, gate, beside):
    nc = g.nc

    def squash(kind, m, main, side):
        nc.scalar.activation(gate[:, ds(m, 1), 0:T].rearrange("p a n -> p (a n)"), main, ACT.Sigmoid)
        return nc.scalar.activation(gate[:, ds(m, 1), T:TOK].rearrange("p a n -> p (a n)"), side, ACT.Sigmoid)
    channel_major(g, "gates", weight_rows(d["w_in"], l, 0, KD, C_G, 512), g.ht, KD, 512, 4, squash,
                  only="scalar", beside=beside)


def merge(g, l, d, ot, oat, gate):
    nc = g.nc
    for w, src, first in ((d["w_dn_up"], ot, 0), (d["w_att_up"], oat, KD)):
        def scale(kind, m, main, side):
            v = gate[:, ds(m + first, 1), :].rearrange("p a n -> p (a n)")
            nc.vector.tensor_tensor(v[:, 0:T], v[:, 0:T], main, ALU.mult)
            return nc.vector.tensor_tensor(v[:, T:TOK], v[:, T:TOK], side, ALU.mult)
        channel_major(g, "up", weight_rows(w, l, 0, H, 0, 512), src, H, 512, 2, scale, only="vector")
    with stage(g, "added") as (block, added):
        @block.vector
        def _(dve):
            nc.vector.memset(g.ht[:, :, TOK:TOKP], 0.0)
            nc.vector.tensor_tensor(g.ht[:, :, 0:TOK], gate[:, 0:KD, :], gate[:, KD:2 * KD, :], ALU.add)
    token_major(g, "w_o", weight_rows(d["w_o"], l, 0, KD, 0, 512), g.ht, KD, 512, 2,
                lambda kind, t, j, ps: add_to_x(g, t, j, ps), only="vector")


def add_to_x(g, t, j, ps, w=512):
    x = g.x[:, t, ds(j * w, w)]
    return g.nc.vector.tensor_tensor(x, x, ps, ALU.add)



def memory(g, l, d):
    nc = g.nc
    N = B * MH
    with ExitStack() as ctx:
        def sb(name, *shape, dt=FP32):
            return ctx.enter_context(g.buffer(name, shape, dt))
        mk = sb("mk", P, MT_, MW)
        mv = sb("mv", P, MT_, MW)
        with ExitStack() as inner:
            mem = inner.enter_context(g.buffer("mem", [P, MT_, D], FP32))
            mt = inner.enter_context(g.buffer("memT", [P, KD, MEM], FP32))
            with stage(g, "mem_in") as (block, mem_in):
                @block.sync
                def _(sp):
                    sp.dma_start(mem[:], d["mem_prompt"][0].rearrange("(t p) n -> p t n", p=P)).then_inc(mem_in, 16)
                    sp.wait_ge(mem_in, 16)
            norm_transposed(g, mem, MT_, d["norm_mem_kv"].rearrange("l (k p) -> p l k", p=P)[:, ds(l, 1), :], mt)
            for w, dst in ((d["w_mk"], mk), (d["w_mv"], mv)):
                token_major(g, "mkv", weight_rows(w, l, 0, KD, 0, 256), mt, KD, 256, 2,
                            lambda kind, t, j, ps: copy(g, kind, dst[:, t, ds(j * 256, 256)], ps), tiles=MT_)
            with stage(g, "stored") as (block, stored):
                @block.sync
                def _(sp):
                    for out, src in ((d["p_mem_k"], mk), (d["p_mem_v"], mv)):
                        sp.dma_start(out.rearrange("l b (t p) h e -> p (l b) t (h e)", p=P)[:, ds(l, 1), :, :]
                                     .rearrange("p a t n -> p (a t) n"), src[:]).then_inc(stored, 16)
                    sp.wait_ge(stored, 32)
        norm_transposed(g, g.x, NT, d["norm_mem_q"].rearrange("l (k p) -> p l k", p=P)[:, ds(l, 1), :], g.ht)
        qT = sb("mqT", P, MH, TOK)
        om = sb("om", P, TT, MW)
        omT = sb("omT", P, MH, TOKP)
        mkT = sb("mkT", P, MH, MEM)

        def evac(kind, m, main, side):
            copy(g, kind, qT[:, ds(m, 1), 0:T].rearrange("p a n -> p (a n)"), main)
            return copy(g, kind, qT[:, ds(m, 1), T:TOK].rearrange("p a n -> p (a n)"), side)
        channel_major(g, "mq", weight_rows(d["w_mq"], l, 0, KD, 0, 256), g.ht, KD, 256, 2, evac)
        with stage(g, "turned", "copied") as (block, turned, copied):
            @block.tensor
            def _(pe):
                for h in range(MH):
                    for t in range(MT_):
                        last = nc.tensor.transpose(g.ps[:, h, t * P:(t + 1) * P], mk[:, t, h * MD:(h + 1) * MD], g.ident)
                last.then_inc(turned, 1)

            @block.scalar
            def _(act):
                act.wait_ge(turned, 1)
                nc.scalar.copy(mkT[:], g.ps[:, 0:MH, 0:MEM])
        with ExitStack() as inner:
            def sbi(name, *shape, dt=FP32):
                return inner.enter_context(g.buffer(name, shape, dt))
            pr = sbi("mpr", P, 2, MEM)
            nm = sbi("mnm", P, TT * MH)
            sums = sbi("msums", P, TT * MH)
            pT = sbi("mpT", P, 2, MT_, P)
            with stage(g, "multiplied", "maxed", "exped", "turned", "back", "ready", "rows_out", "inverted",
                       "scaled") as (block, multiplied, maxed, exped, turned, back, ready, rows_out, inverted, scaled):
                NI = TT * MH
                scale = MD ** -0.5

                @block.tensor
                def _(pe):
                    def scores(i):
                        t, h = i // MH, i % MH
                        nc.tensor.matmul(g.ps[:, i % 2, 0:MEM], qT[:, h, t * P:(t + 1) * P], mkT[:, h, :],
                                         start=True, stop=True).then_inc(multiplied, 1)
                    for i in range(2):
                        scores(i)
                    for i in range(NI):
                        pe.wait_ge(exped, i + 1)
                        if i + 2 < NI:
                            scores(i + 2)
                        if i >= 2:
                            pe.wait_ge(back, i - 1)
                        for k in range(MT_):
                            last = nc.tensor.transpose(g.ps[:, 2 + i % 2, k * P:(k + 1) * P], pr[:, i % 2, k * P:(k + 1) * P], g.ident)
                        last.then_inc(turned, 1)
                        pe.wait_ge(back, i + 1)
                        if i >= 2:
                            pe.wait_ge(rows_out, i - 1)
                        for k in range(MT_):
                            last = nc.tensor.matmul(g.ps[:, 4 + i % 2, 0:MD], pT[:, i % 2, k, :],
                                                    mv[:, k, (i % MH) * MD:(i % MH + 1) * MD],
                                                    start=(k == 0), stop=(k == MT_ - 1))
                        last.then_inc(ready, 1)

                @block.vector
                def _(dve):
                    def finish(i):
                        dve.wait_ge(exped, i + 1)
                        nc.vector.reciprocal(sums[:, i:i + 1], sums[:, i:i + 1]).then_inc(inverted, 1)
                        dve.wait_ge(ready, i + 1)
                        dve.wait_ge(inverted, i + 1)
                        nc.vector.tensor_scalar(om[:, i // MH, (i % MH) * MD:(i % MH + 1) * MD], g.ps[:, 4 + i % 2, 0:MD],
                                                sums[:, i:i + 1], None, ALU.mult).then_inc(rows_out, 1)
                    for i in range(NI):
                        dve.wait_ge(multiplied, i + 1)
                        nc.vector.tensor_reduce(nm[:, i:i + 1], g.ps[:, i % 2, 0:MEM], AX.X, ALU.max,
                                                negate=True).then_inc(maxed, 1)
                        if i >= 1:
                            finish(i - 1)
                    finish(NI - 1)

                @block.scalar
                def _(act):
                    for i in range(NI):
                        act.wait_ge(maxed, i + 1)
                        if i >= 2:
                            act.wait_ge(turned, i - 1)
                        nc.scalar.mul(nm[:, i:i + 1], nm[:, i:i + 1], scale).then_inc(scaled, 1)
                        act.wait_ge(scaled, i + 1)
                        nc.scalar.activation(pr[:, i % 2, :], g.ps[:, i % 2, 0:MEM], ACT.Exp, bias=nm[:, i:i + 1], scale=scale,
                                             accum_out=sums[:, i:i + 1]).then_inc(exped, 1)
                        act.wait_ge(turned, i + 1)
                        nc.scalar.copy(pT[:, i % 2, :, :].rearrange("p k n -> p (k n)"), g.ps[:, 2 + i % 2, 0:MEM]).then_inc(back, 1)
        turn_tokens(g, lambda t, k: om[:, t, k * P:(k + 1) * P], omT, TT)
        memory_sample(g, l, d, qT, omT)
        token_major(g, "w_mo", weight_rows(d["w_mo"], l, 0, MH, 0, 512), omT, MH, 512, 2,
                    lambda kind, t, j, ps: add_to_x(g, t, j, ps), only="vector")


def memory_sample(g, l, d, qT, omT):
    nc = g.nc
    N = B * MH
    with ExitStack() as ctx:
        def sb(name, *shape, dt=FP32):
            return ctx.enter_context(g.buffer(name, shape, dt))
        kin = sb("mem_k", P, 2, MT_, MW)
        kT = sb("mem_kT", P, 2, MH, MEM)
        qz = sb("qz", P, N * (N + 1))
        sc = sb("msc", N, MEM)
        small = sb("msmall", P, 4)
        pT = sb("mspT", P, MT_, N)
        tk = d["cache_mem_k"].rearrange("l b (t p) h e -> p (l b) t (h e)", p=P)
        tv = d["cache_mem_v"].rearrange("l b (t p) h e -> p (l b) t (h e)", p=P)
        with stage(g, "vec") as (block, vec):
            @block.vector
            def _(dve):
                step = in_order(dve, vec)
                step(nc.vector.memset(qz[:], 0.0))
                step(nc.vector.tensor_copy(
                    qz[:].rearrange("p (b h x) -> p b h x", b=B, h=MH)[:, :, :, 0],
                    qT[:, :, T:TOK].rearrange("p h b -> p b h")))
                nc.vector.memset(omT[:, :, TOK:TOKP], 0.0)
        with stage(g, "k_in0", "k_in1", "turned", "back", "multiplied") as (block, k_in0, k_in1, turned, back, multiplied):
            k_in = (k_in0, k_in1)

            @block.sync
            def _(sp):
                for b in range(B):
                    if b >= 2:
                        sp.wait_ge(turned, (b - 1) * MT_)
                    sp.dma_start(kin[:, b % 2], tk[:, ds(l * B + b, 1), :, :].rearrange("p a t n -> p (a t) n")
                                 ).then_inc(k_in[b % 2], 16)

            @block.tensor
            def _(pe):
                def dots(b):
                    pe.wait_ge(back, (b + 1) * MT_)
                    for h in range(MH):
                        n = b * MH + h
                        last = nc.tensor.matmul(g.ps[0:N, 4, 0:MEM], qz[:, n * N:(n + 1) * N], kT[:, b % 2, h, :],
                                                start=(n == 0), stop=(n == N - 1))
                    return last
                for b in range(B):
                    pe.wait_ge(k_in[b % 2], 16 * (b // 2 + 1))
                    for t in range(MT_):
                        for h in range(MH):
                            last = nc.tensor.transpose(g.ps[:, 2 * (b % 2) + t, h * P:(h + 1) * P],
                                                       kin[:, b % 2, t, h * MD:(h + 1) * MD], g.ident)
                        last.then_inc(turned, 1)
                    if b >= 1:
                        dots(b - 1)
                dots(B - 1).then_inc(multiplied, 1)

            @block.scalar
            def _(act):
                for b in range(B):
                    for t in range(MT_):
                        act.wait_ge(turned, b * MT_ + t + 1)
                        nc.scalar.copy(kT[:, b % 2, :, t * P:(t + 1) * P],
                                       g.ps[:, 2 * (b % 2) + t, :].rearrange("p (h m) -> p h m", h=MH)).then_inc(back, 1)
                act.wait_ge(multiplied, 1)
                nc.scalar.mul(sc[:], g.ps[0:N, 4, 0:MEM], MD ** -0.5)
        softmax_rows(g, N, MEM, sc, small)
        with stage(g, "k_in0", "k_in1", "turned", "back", "ready") as (block, k_in0, k_in1, turned, back, ready):
            k_in = (k_in0, k_in1)

            @block.sync
            def _(sp):
                for b in range(B):
                    if b >= 2:
                        sp.wait_ge(ready, b - 1)
                    sp.dma_start(kin[:, b % 2], tv[:, ds(l * B + b, 1), :, :].rearrange("p a t n -> p (a t) n")
                                 ).then_inc(k_in[b % 2], 16)

            @block.tensor
            def _(pe):
                for t in range(MT_):
                    last = nc.tensor.transpose(g.ps[:, 0, t * N:(t + 1) * N], sc[:, t * P:(t + 1) * P], g.ident[0:N, 0:N])
                last.then_inc(turned, 1)
                pe.wait_ge(back, 1)
                for b in range(B):
                    pe.wait_ge(k_in[b % 2], 16 * (b // 2 + 1))
                    for h in range(MH):
                        n = b * MH + h
                        for t in range(MT_):
                            last = nc.tensor.matmul(g.ps[:, 1, n:n + 1], kin[:, b % 2, t, h * MD:(h + 1) * MD], pT[:, t, n:n + 1],
                                                    start=(t == 0), stop=(t == MT_ - 1))
                    last.then_inc(ready, 1)

            @block.vector
            def _(dve):
                dve.wait_ge(turned, 1)
                nc.vector.tensor_copy(pT[:].rearrange("p t n -> p (t n)"), g.ps[:, 0, 0:MT_ * N]).then_inc(back, 1)
                dve.wait_ge(ready, B)
                nc.vector.tensor_copy(omT[:, :, T:TOK], g.ps[:, 1, 0:N].rearrange("p (b h) -> p h b", b=B))



def peer_route(g, l, d, rT):
    nc = g.nc
    HC = 2 * PH
    PAIRS = PTOP * PTOP
    with ExitStack() as ctx:
        def sb(name, *shape, dt=FP32):
            return ctx.enter_context(g.buffer(name, shape, dt))
        qT = sb("pqT", P, HC, TOKP)
        keysT = sb("keysT", P, HC, NK)

        def evac(kind, m, main, side):
            copy(g, kind, qT[:, ds(m, 1), 0:T].rearrange("p a n -> p (a n)"), main)
            return copy(g, kind, qT[:, ds(m, 1), T:TOK].rearrange("p a n -> p (a n)"), side)
        channel_major(g, "pq", weight_rows(d["peer_wq"], l, 0, KD, 0, 512), g.ht, KD, 512, 4, evac)
        q = sb("pq", P, HC, P)
        s = sb("ps", P, HC, NK)
        top = sb("top", P, HC, PTOP)
        topi = sb("topi", P, HC, PTOP, dt=U32)
        topf = sb("topf", P, HC, PTOP)
        cand = sb("cand", P, PH, PAIRS)
        best = sb("best", P, PH, PTOP)
        at = sb("at", P, 3, PJ, dt=U32)
        atf = sb("atf", P, 2, PJ)
        route = sb("route", P, 3, PJ)
        small = sb("gsmall", P, 2, PH)
        with stage(g, "keys_in", "turned", "back") as (block, keys_in, turned, back):
            @block.sync
            def _(sp):
                for x in range(0, HC, 8):
                    sp.dma_start(s[:, x:x + 8, :], d["peer_keys"].rearrange("l h c k e -> k (l h c) e")
                                 [:, ds(l * HC + x, 8), :]).then_inc(keys_in, 16)

            @block.tensor
            def _(pe):
                pe.wait_ge(keys_in, 16 * HC // 8)
                for x in range(HC):
                    last = nc.tensor.transpose(g.ps[:, x // 4, (x % 4) * P:(x % 4 + 1) * P], s[:, x, :], g.ident)
                    if x % 4 == 3:
                        last.then_inc(turned, 1)

            @block.scalar
            def _(act):
                for b in range(HC // 4):
                    act.wait_ge(turned, b + 1)
                    nc.scalar.copy(keysT[:, 4 * b:4 * b + 4, :].rearrange("p x k -> p (x k)"), g.ps[:, b, :])

            @block.vector
            def _(dve):
                nc.vector.memset(qT[:, :, TOK:TOKP], 0.0)
        with nc.Fori(0, NT) as t:
            with stage(g, "fetched", "scored", "back", "vec", "exped", "turned") as (
                    block, fetched, scored, back, vec, exped, turned):
                V = {}

                @block.vector
                def _(dve):
                    count = [0]

                    def step(ins, name=None):
                        count[0] += 1
                        ins.then_inc(vec, 1)
                        dve.wait_ge(vec, count[0])
                        if name:
                            V[name] = count[0]

                    def together(rows):
                        for ins in rows:
                            count[0] += 1
                            ins.then_inc(vec, 1)
                        dve.wait_ge(vec, count[0])

                    def best16(rows):
                        for r in range(2):
                            part = slice(8 * r, 8 * r + 8)
                            together(nc.vector.max(out[:, part], values) for values, out, index in rows)
                            together(nc.vector.max_index(index[:, part], out[:, part], values)
                                     for values, out, index in rows)
                            if r == 0:
                                together(nc.vector.match_replace(values, out[:, part], values, TAKEN)
                                         for values, out, index in rows)
                    for b in range(HC // 4):
                        dve.wait_ge(back, b + 1)
                        best16([(s[:, x, :], top[:, x, :], topi[:, x, :]) for x in range(4 * b, 4 * b + 4)])
                    step(nc.vector.tensor_copy(topf[:], topi[:]))
                    halves = top[:].rearrange("p (h c) k -> p h c k", c=2)
                    step(nc.vector.tensor_tensor(
                        cand[:].rearrange("p h (a b) -> p h a b", a=PTOP),
                        halves[:, :, 0, :].unsqueeze(3).to_broadcast([P, PH, PTOP, PTOP]),
                        halves[:, :, 1, :].unsqueeze(2).to_broadcast([P, PH, PTOP, PTOP]), ALU.add))
                    posi = at[:, 0, :].rearrange("p (h k) -> p h k", h=PH)
                    best16([(cand[:, h, :], best[:, h, :], posi[:, h, :]) for h in range(PH)])
                    step(nc.vector.tensor_copy(small[:, 0, :], best[:, :, 0]))
                    step(nc.vector.tensor_tensor(best[:], best[:], small[:, 0, :].unsqueeze(2).to_broadcast([P, PH, PTOP]),
                                                 ALU.subtract), "shifted")
                    step(nc.vector.tensor_scalar(at[:, 1, :], at[:, 0, :], 4, None, ALU.logical_shift_right))
                    step(nc.vector.tensor_scalar(at[:, 2, :], at[:, 0, :], PTOP - 1, None, ALU.bitwise_and))
                    step(nc.vector.tensor_copy(atf[:], at[:, 1:3, :]))
                    fhalves = topf[:].rearrange("p (h c) k -> p h c k", c=2)
                    c4 = cand[:].rearrange("p h (k a) -> p h k a", a=PTOP)
                    for c in range(2):
                        step(nc.vector.tensor_tensor(
                            cand[:].rearrange("p h (k a) -> p (h k) a", a=PTOP),
                            atf[:, c, :].unsqueeze(2).to_broadcast([P, PJ, PTOP]),
                            g.iota[:, 0:PTOP].unsqueeze(1).to_broadcast([P, PJ, PTOP]), ALU.is_equal))
                        step(nc.vector.tensor_tensor(c4, c4, fhalves[:, :, c, :].unsqueeze(2).to_broadcast([P, PH, PTOP, PTOP]),
                                                     ALU.mult))
                        step(nc.vector.tensor_reduce(route[:, c, :], cand[:].rearrange("p h (k a) -> p (h k) a", a=PTOP),
                                                     AX.X, ALU.add))
                    dve.wait_ge(exped, 1)
                    step(nc.vector.tensor_reduce(small[:, 0, :], best[:], AX.X, ALU.add))
                    step(nc.vector.reciprocal(small[:, 1, :], small[:, 0, :]))
                    step(nc.vector.tensor_tensor(route[:, 2, :].rearrange("p (h k) -> p h k", h=PH), best[:],
                                                 small[:, 1, :].unsqueeze(2).to_broadcast([P, PH, PTOP]), ALU.mult), "routed")

                @block.scalar
                def _(act):
                    nc.scalar.copy(q[:], qT[:, :, ds(t * P, P)]).then_inc(fetched, 1)
                    for b in range(HC // 4):
                        act.wait_ge(scored, b + 1)
                        nc.scalar.copy(s[:, 4 * b:4 * b + 4, :].rearrange("p x k -> p (x k)"), g.ps[:, b, :]).then_inc(back, 1)
                    act.wait_ge(vec, V["shifted"])
                    nc.scalar.activation(best[:], best[:], ACT.Exp).then_inc(exped, 1)
                    act.wait_ge(turned, 1)
                    nc.scalar.copy(rT[:, :, ds(t * P, P)], g.ps[:, 4, 0:3 * P].rearrange("p (a n) -> p a n", a=3))

                @block.tensor
                def _(pe):
                    pe.wait_ge(fetched, 1)
                    for x in range(HC):
                        last = nc.tensor.matmul(g.ps[:, x // 4, (x % 4) * P:(x % 4 + 1) * P], q[:, x, :], keysT[:, x, :],
                                                start=True, stop=True)
                        if x % 4 == 3:
                            last.then_inc(scored, 1)
                    pe.wait_ge(vec, V["routed"])
                    for a in range(3):
                        last = nc.tensor.transpose(g.ps[:, 4, a * P:(a + 1) * P], route[:, a, :], g.ident)
                    last.then_inc(turned, 1)


GB = 104
NB = TOK // GB
QUADS = GB // 4


def peer_gates(g, rT):
    nc = g.nc
    with ExitStack() as ctx:
        out = ctx.enter_context(g.buffer("gates", [P, 2, NK, GB], FP32))
        hot = ctx.enter_context(g.buffer("hot0", [P, 2, 4, NK], FP32))
        other = ctx.enter_context(g.buffer("hot1", [P, 2, 4, NK], FP32))
        square = g.wb[:].rearrange("p a k n -> p (a k n)")[:, 0:8 * NK].rearrange("p (u a x k) -> p u a x k", u=2, a=2, x=2)
        NQ = NB * QUADS
        with stage(g, "hot_ready", "apart", "squared", "other_ready", "multiplied", "emptied", "stored0", "stored1") as (
                block, hot_ready, apart, squared, other_ready, multiplied, emptied, stored0, stored1):
            stored = (stored0, stored1)

            @block.vector
            def _(dve):
                dve.sem_inc(multiplied, 2)
                for blk in range(NB):
                    with dve.Fori(0, QUADS // 2) as it:
                        for u in range(2):
                            dve.wait_ge(multiplied, it * 2 + (blk * QUADS + u + 1))
                            for x in range(4):
                                def at(a):
                                    return rT[:, a, ds(it * 8 + (blk * GB + 4 * u + x), 1)]
                                nc.vector.tensor_scalar(hot[:, u, x, :], g.iota, at(0), at(2), ALU.is_equal, ALU.mult)
                            nc.vector.tensor_tensor(
                                other[:, u, 2:4], g.iota.unsqueeze(1).to_broadcast([P, 2, NK]),
                                rT[:, 1, ds(it * 8 + (blk * GB + 4 * u + 2), 2)].unsqueeze(2).to_broadcast([P, 2, NK]),
                                ALU.is_equal).then_inc(hot_ready, 1)

            @block.gpsimd
            def _(pool):
                def squares(it, u):
                    nc.gpsimd.tensor_tensor(
                        square[:, u, 0], g.iota.unsqueeze(1).to_broadcast([P, 2, NK]),
                        rT[:, 1, ds(it * 8 + 4 * u, 2)].unsqueeze(2).to_broadcast([P, 2, NK]),
                        ALU.subtract).then_inc(apart, 1)
                    pool.wait_ge(apart, it * 2 + (u + 1))
                    nc.gpsimd.tensor_tensor(square[:, u, 1], square[:, u, 0], square[:, u, 0], ALU.mult).then_inc(squared, 1)
                for u in range(2):
                    squares(0, u)
                with pool.Fori(1, NQ // 2) as it:
                    for u in range(2):
                        pool.wait_ge(other_ready, it * 2 + (u - 1))
                        squares(it, u)

            @block.tensor
            def _(pe):
                pe.sem_inc(emptied, 2)
                for blk in range(NB):
                    with pe.Fori(0, QUADS // 2) as it:
                        for u in range(2):
                            pe.wait_ge(hot_ready, it * 2 + (blk * QUADS + u + 1))
                            pe.wait_ge(other_ready, it * 2 + (blk * QUADS + u + 1))
                            pe.wait_ge(emptied, it * 2 + (blk * QUADS + u + 1))
                            for x in range(4):
                                last = nc.tensor.matmul(g.ps[:, u, x * P:(x + 1) * P], other[:, u, x, :], hot[:, u, x, :],
                                                        start=True, stop=True)
                            last.then_inc(multiplied, 1)

            @block.scalar
            def _(act):
                def one_hot(u, n):
                    act.wait_ge(squared, n + 1)
                    act.wait_ge(multiplied, n + 1)
                    nc.scalar.activation(other[:, u, 0:2], square[:, u, 1], ACT.Relu, bias=g.ones[:, 0:1],
                                         scale=-1.0).then_inc(other_ready, 1)

                def empty(blk, it, u):
                    act.wait_ge(multiplied, it * 2 + (blk * QUADS + u + 3))
                    nc.scalar.copy(out[:, blk % 2, :, ds(it * 8 + 4 * u, 4)],
                                   g.ps[:, u, :].rearrange("p (x k) -> p k x", x=4)).then_inc(emptied, 1)
                for u in range(2):
                    one_hot(u, u)
                for blk in range(NB):
                    if blk >= 2:
                        act.wait_ge(stored[blk % 2], 16 * (blk // 2))
                    ends = blk == NB - 1
                    with act.Fori(0, QUADS // 2 - ends) as it:
                        for u in range(2):
                            empty(blk, it, u)
                            one_hot(u, it * 2 + (blk * QUADS + u + 2))
                    if ends:
                        for u in range(2):
                            empty(blk, QUADS // 2 - 1, u)

            @block.sync
            def _(sp):
                for blk in range(NB):
                    sp.wait_ge(emptied, (blk + 1) * QUADS + 2)
                    sp.dma_start(g.gates[:, :, blk * GB:(blk + 1) * GB], out[:, blk % 2]).then_inc(stored[blk % 2], 16)
                sp.wait_ge(stored0, 16 * ((NB + 1) // 2))
                sp.wait_ge(stored1, 16 * (NB // 2))


def peer_experts(g, l, d):
    nc = g.nc
    GT = 2
    NG = NK // GT
    HALF_TOK = TOK // 2
    PART = [range(0, KD // 2), range(KD // 2, KD)]
    uview = d["peer_u"].rearrange("l (i p) n -> p (l i) n", p=P)
    vview = d["peer_v"].rearrange("l (i p) n -> p (l i) n", p=P)
    with ExitStack() as ctx:
        def sb(name, *shape, dt=FP32):
            return ctx.enter_context(g.buffer(name, shape, dt))
        flat = g.wb[:].rearrange("p a k n -> p (a k n)")
        raw = flat.rearrange("p (w a i n) -> p w a i n", w=2, a=2, i=GT)
        ub, vb = raw[:, 0], raw[:, 1]
        ht = [sb(f"ht{x}", P, KD, TOK, dt=FP32R) for x in "hl"]
        v2 = [sb(f"v{x}", P, 2, GT, D, dt=FP32R) for x in "hl"]
        u2 = [sb(f"u{x}", P, KD, P, dt=FP32R) for x in "hl"]
        z2 = [sb(f"z{x}", P, 2, GT, TOK, dt=FP32R) for x in "hl"]
        yT = sb("yT", P, KD, TOK)
        gt = sb("gt", P, 2, GT, TOK)
        act_out = sb("act_out", P, 2, TOK)
        TERMS = ((0, 0), (0, 1), (1, 0))

        def value(x):
            return x.bitcast(FP32)

        with stage(g, "high", "vec") as (block, high, vec):
            @block.scalar
            def _(act):
                for k in range(KD):
                    nc.scalar.copy(ht[0][:, k, :], g.ht[:, k, 0:TOK]).then_inc(high, 1)

            @block.vector
            def _(dve):
                for k in range(KD):
                    dve.wait_ge(high, k + 1)
                    nc.vector.tensor_tensor(ht[1][:, k, :], g.ht[:, k, 0:TOK], value(ht[0][:, k, :]), ALU.subtract)
                nc.vector.memset(yT[:], 0.0)

        with stage(g, "u_in0", "u_in1", "v_in0", "v_in1", "g_in0", "g_in1", "turned", "a_full", "out_full",
                   "u_high", "v_high", "gelued", "z_high", "u_low", "v_low", "gated", "z_low", "out_free") as (
                       block, u_in0, u_in1, v_in0, v_in1, g_in0, g_in1, turned, a_full, out_full,
                       u_high, v_high, gelued, z_high, u_low, v_low, gated, z_low, out_free):
            u_in, v_in, g_in = (u_in0, u_in1), (v_in0, v_in1), (g_in0, g_in1)

            def pairs(eng, emit):
                emit(0, "first")
                with eng.Fori(1, NG // 2 - 1) as it:
                    emit(it, "")
                emit(NG // 2 - 1, "last")

            @block.sync
            def _(sp):
                def emit(it, place):
                    for u in range(2):
                        G = it * 2 + u
                        before = None if place == "first" else (it - 1) * (2 * GT) + (u + 1) * GT
                        if before is not None:
                            sp.wait_ge(turned, before)
                        sp.dma_start(ub[:, u], uview[:, ds(l * NK + G * GT, GT), :]).then_inc(u_in[u], 16)
                        if before is not None:
                            sp.wait_ge(gated, before)
                        sp.dma_start(gt[:, u], g.gates[:, ds(G * GT, GT), :]).then_inc(g_in[u], 16)
                        if before is not None:
                            sp.wait_ge(v_low, before)
                        sp.dma_start(vb[:, u], vview[:, ds(l * NK + G * GT, GT), :]).then_inc(v_in[u], 16)
                pairs(sp, emit)

            def out_banks(c):
                return g.ps[:, 4 + 2 * (c % 2):6 + 2 * (c % 2), 0:HALF_TOK]

            @block.tensor
            def _(pe):
                pe.sem_inc(out_free, 2)

                def outputs(it, w, part):
                    for c in part:
                        pe.wait_ge(out_free, it * (2 * KD) + (w * KD + c + 1))
                        for m, (i, (x, y)) in enumerate((i, xy) for i in range(GT) for xy in TERMS):
                            for hf in range(2):
                                last = nc.tensor.matmul(out_banks(c)[:, hf], v2[x][:, w, i, c * P:(c + 1) * P],
                                                        z2[y][:, w, i, hf * HALF_TOK:(hf + 1) * HALF_TOK],
                                                        start=(m == 0), stop=(m == 3 * GT - 1))
                        last.then_inc(out_full, 1)

                def turn(it, n):
                    u, i = n // GT, n % GT
                    if i == 0:
                        pe.wait_ge(u_in[u], it * 16 + 16)
                    for k in range(KD):
                        last = nc.tensor.transpose(g.ps[:, k // 4, (k % 4) * P:(k % 4 + 1) * P],
                                                   ub[:, u, i, k * P:(k + 1) * P], g.ident)
                    last.then_inc(turned, 1)

                def emit(it, place):
                    if place == "first":
                        turn(it, 0)
                    for n in range(2 * GT):
                        u, i = n // GT, n % GT
                        done = it * (2 * GT) + n
                        if not (place == "first" and n == 0):
                            pe.wait_ge(gelued, done)
                        pe.wait_ge(u_low, done + 1)
                        for m, (k, (x, y)) in enumerate((k, xy) for k in range(KD) for xy in TERMS):
                            for hf in range(2):
                                last = nc.tensor.matmul(g.ps[:, 2 + hf, 0:HALF_TOK], u2[x][:, k, :],
                                                        ht[y][:, k, hf * HALF_TOK:(hf + 1) * HALF_TOK],
                                                        start=(m == 0), stop=(m == 3 * KD - 1))
                        last.then_inc(a_full, 1)
                        if n + 1 < 2 * GT:
                            turn(it, n + 1)
                        elif place != "last":
                            turn(it + 1, 0)
                        if not (place == "first" and u == 0):
                            if i == 0:
                                pe.wait_ge(z_low, it * (2 * GT) + (u * GT + 2))
                                pe.wait_ge(v_low, it * (2 * GT) + u * GT)
                            outputs(it if u == 1 else it - 1, 1 - u, PART[i])
                pairs(pe, emit)
                pe.wait_ge(z_low, NG * GT + 2)
                pe.wait_ge(v_low, NG * GT)
                outputs(NG // 2 - 1, 1, range(KD))

            turned_tile = g.ps[:, 0:2, :].rearrange("p a n -> p (a n)")

            @block.scalar
            def _(act):
                def split(it, n):
                    act.wait_ge(turned, it * (2 * GT) + (n + 1))
                    nc.scalar.copy(u2[0][:].rearrange("p k e -> p (k e)"), turned_tile).then_inc(u_high, 1)

                def emit(it, place):
                    if place == "first":
                        split(it, 0)
                    for n in range(2 * GT):
                        this = it * (2 * GT) + (n + 1)
                        act.wait_ge(a_full, this)
                        act.wait_ge(z_low, this)
                        nc.scalar.activation(act_out[:, n % 2, :].rearrange("p (a t) -> p a t", a=2),
                                             g.ps[:, 2:4, 0:HALF_TOK], ACT.Gelu).then_inc(gelued, 1)
                        act.wait_ge(gated, this)
                        nc.scalar.copy(z2[0][:, n // GT, n % GT, 0:TOK], act_out[:, n % 2, :]).then_inc(z_high, 1)
                        if n + 1 < 2 * GT:
                            split(it, n + 1)
                        elif place != "last":
                            split(it + 1, 0)
                        u, i = n // GT, n % GT
                        if i == 0:
                            act.wait_ge(v_in[u], it * 16 + 16)
                        nc.scalar.copy(v2[0][:, u, i, :], vb[:, u, i, :]).then_inc(v_high, 1)
                pairs(act, emit)

            @block.vector
            def _(dve):
                dve.sem_inc(z_low, 2)

                def outputs(it, w, part):
                    for c in part:
                        dve.wait_ge(out_full, it * (2 * KD) + (w * KD + c + 1))
                        y = yT[:, c, :].rearrange("p (a t) -> p a t", a=2)
                        nc.vector.tensor_tensor(y, y, out_banks(c), ALU.add).then_inc(out_free, 1)

                def split(it, n):
                    dve.wait_ge(u_high, it * (2 * GT) + (n + 1))
                    nc.vector.tensor_tensor(u2[1][:].rearrange("p k e -> p (k e)"), turned_tile,
                                            value(u2[0][:].rearrange("p k e -> p (k e)")),
                                            ALU.subtract).then_inc(u_low, 1)

                def emit(it, place):
                    if place == "first":
                        split(it, 0)
                    for n in range(2 * GT):
                        u, i = n // GT, n % GT
                        this = it * (2 * GT) + (n + 1)
                        if i == 0:
                            dve.wait_ge(g_in[u], it * 16 + 16)
                        dve.wait_ge(gelued, this)
                        a = act_out[:, n % 2, :]
                        nc.vector.tensor_tensor(a, a, gt[:, u, i, :], ALU.mult).then_inc(gated, 1)
                        dve.wait_ge(z_high, this)
                        nc.vector.tensor_tensor(z2[1][:, u, i, 0:TOK], a, value(z2[0][:, u, i, 0:TOK]),
                                                ALU.subtract).then_inc(z_low, 1)
                        if not (place == "first" and u == 0):
                            outputs(it if u == 1 else it - 1, 1 - u, PART[i][0:1])
                        if n + 1 < 2 * GT:
                            split(it, n + 1)
                        elif place != "last":
                            split(it + 1, 0)
                        if not (place == "first" and u == 0):
                            outputs(it if u == 1 else it - 1, 1 - u, PART[i][1:3])
                        dve.wait_ge(v_high, this)
                        nc.vector.tensor_tensor(v2[1][:, u, i, :], vb[:, u, i, :], value(v2[0][:, u, i, :]),
                                                ALU.subtract).then_inc(v_low, 1)
                        if not (place == "first" and u == 0):
                            outputs(it if u == 1 else it - 1, 1 - u, PART[i][3:])
                pairs(dve, emit)
                outputs(NG // 2 - 1, 1, range(KD))

        with stage(g, "turned", "added") as (block, turned, added):
            @block.tensor
            def _(pe):
                for n in range(2 * NT):
                    t, w = n // 2, P if n // 2 < TT else B
                    if n >= 4:
                        pe.wait_ge(added, n - 3)
                    for k in range(4):
                        last = nc.tensor.transpose(g.ps[0:w, n % 4, k * P:(k + 1) * P],
                                                   yT[:, (n % 2) * 4 + k, t * P:t * P + w], g.ident)
                    last.then_inc(turned, 1)

            @block.vector
            def _(dve):
                for n in range(2 * NT):
                    t, w = n // 2, P if n // 2 < TT else B
                    dve.wait_ge(turned, n + 1)
                    x = g.x[0:w, t, (n % 2) * 512:(n % 2 + 1) * 512]
                    nc.vector.tensor_tensor(x, x, g.ps[0:w, n % 4, :], ALU.add).then_inc(added, 1)


def peer(g, l, d):
    norm_transposed(g, g.x, NT, d["norm_ffn"].rearrange("l (k p) -> p l k", p=P)[:, ds(l, 1), :], g.ht)
    with ExitStack() as ctx:
        rT = ctx.enter_context(g.buffer("routeT", [P, 3, TOKP], FP32))
        peer_route(g, l, d, rT)
        peer_gates(g, rT)
    peer_experts(g, l, d)


def layer(g, l, d):
    nc = g.nc
    mixer(g, l, d)
    memory(g, l, d)
    peer(g, l, d)
    with stage(g, "counted") as (block, counted):
        @block.vector
        def _(dve):
            nc.vector.tensor_scalar(g.layer[:], g.layer[:], 1.0, None, ALU.add)


def final(g, d):
    nc = g.nc
    with ExitStack() as ctx:
        gain = ctx.enter_context(g.buffer("fgain", [P, D], FP32))
        y = ctx.enter_context(g.buffer("y", [P, NT, D], FP32))
        ss = ctx.enter_context(g.buffer("fss", [P, 4, NT], FP32))
        with stage(g, "gain_in", "squared", "vec", "rooted", "stored") as (block, gain_in, squared, vec, rooted, stored):
            @block.sync
            def _(sp):
                sp.dma_start(gain[:], d["norm_final"].rearrange("(a n) -> a n", a=1).to_broadcast([P, D])).then_inc(gain_in, 16)
                sp.wait_ge(vec, 2 + 2 * NT)
                sp.dma_start(d["y_prompt"][0].rearrange("(t p) n -> p t n", p=P), y[:, 0:TT, :]).then_inc(stored, 16)
                sp.dma_start(d["y_sample"][:, 0, :], y[0:B, TT, :]).then_inc(stored, 16)
                sp.wait_ge(stored, 32)

            @block.scalar
            def _(act):
                for t in range(NT):
                    nc.scalar.activation(y[:, t, :], g.x[:, t, :], ACT.Square, accum_out=ss[:, 0, t:t + 1]).then_inc(squared, 1)
                act.wait_ge(vec, 1)
                nc.scalar.activation(ss[:, 2, :], ss[:, 1, :], ACT.Sqrt).then_inc(rooted, 1)

            @block.vector
            def _(dve):
                step = in_order(dve, vec)
                dve.wait_ge(squared, NT)
                step(nc.vector.tensor_scalar(ss[:, 1, :], ss[:, 0, :], 1.0 / D, EPS, ALU.mult, ALU.add))
                dve.wait_ge(rooted, 1)
                step(nc.vector.reciprocal(ss[:, 3, :], ss[:, 2, :]))
                dve.wait_ge(gain_in, 16)
                for t in range(NT):
                    step(nc.vector.tensor_scalar(y[:, t, :], g.x[:, t, :], ss[:, 3, t:t + 1], None, ALU.mult))
                    step(nc.vector.tensor_tensor(y[:, t, :], y[:, t, :], gain[:], ALU.mult))


def mixer(g, l, d):
    norm_transposed(g, g.x, NT, d["norm_mix"].rearrange("l (k p) -> p l k", p=P)[:, ds(l, 1), :], g.ht)
    with ExitStack() as ctx:
        def sb(name, shape, dt=FP32):
            return ctx.enter_context(g.buffer(name, shape, dt))
        g.nat = sb("nat", [P, NT, NAT_W])
        o_all = sb("o_all", [P, NT, H, DK])
        top = sb("seg_top", [SEGS * B, TOPK_S])
        topi = sb("seg_place", [SEGS * B, TOPK_S])
        wn = NAT_W // 4
        token_major(g, "nat", weight_rows(d["w_in"], l, 0, KD, C_Z, wn), g.ht, KD, wn, 4,
                    lambda kind, t, j, ps: copy(g, kind, g.nat[:, t, ds(j * wn, wn)], ps))
        rotary(g, l, d)
        with ExitStack() as inner:
            def sbi(name, shape, dt=FP32):
                return inner.enter_context(g.buffer(name, shape, dt))
            conv = sbi("conv", [P, CC, TOK])
            with ExitStack() as ranked:
                seg = ranked.enter_context(g.buffer("seg_scores", [SEGS * B, SEG + 8], FP32))
                best = ranked.enter_context(g.buffer("best32", [SEGS * B, 32], FP32))
                besti = ranked.enter_context(g.buffer("best32_at", [SEGS * B, 32], U32))
                sample_scores(g, l, d, seg)
                convolution(g, l, d, conv,
                            lambda dve, vec: best_in_order(g, dve, vec, seg[:], best[:], besti[:], top, topi))
            kn = sbi("kn", [P, TT, H, DK])
            vn = sbi("vn", [P, TT, H, DK])
            gb = sbi("gb", [P, NT, 2 * H])
            delta_features(g, l, d, conv, kn, vn, gb)
            delta_prompt(g, l, d, conv, kn, vn, gb, o_all)
            delta_sample(g, l, d, conv, gb, o_all)
        ot = sb("ot", [P, H, TOKP])
        delta_output(g, l, d, o_all, ot)
        oat = sb("oat", [P, 4, TOKP])
        sparse_prompt(g, l, d, oat)
        gate = sb("gate", [P, 2 * KD, TOK])
        pos = sb("pos", [B, TOPK_S])
        with ExitStack() as ranked:
            merged = ranked.enter_context(g.buffer("merged", [B, SEGS * TOPK_S], FP32))
            best = ranked.enter_context(g.buffer("best32", [B, 32], FP32))
            besti = ranked.enter_context(g.buffer("best32_at", [B, 32], U32))
            sample_lists(g, top, topi, merged)
            branch_gates(g, l, d, gate,
                         lambda dve, vec: best_in_order(g, dve, vec, merged[:], best[:], besti[:], None, pos))
        sparse_sample(g, l, d, oat, pos)
        merge(g, l, d, ot, oat, gate)
def program(nc, d, where):
    with ExitStack() as ctx:
        g = Core(nc)

        def sb(name, shape, dt=FP32):
            return ctx.enter_context(g.buffer(name, shape, dt))
        n_const = sum(w for _, w in where.values())
        consts = sb("tables", [P, n_const])

        def const(name):
            at, w = where[name]
            return consts[:, at:at + w]
        g.ident, g.ones, g.triu, g.strict = const("ident"), const("ones"), const("triu"), const("strict")
        g.iota, g.iota512, g.tpos, g.slot = const("iota"), const("iota512"), const("tpos"), const("slot")
        g.own, g.lists = const("own"), const("lists")
        g.lev = [const(f"lev{s}") for s in range(7)]
        g.cos = const("cos").rearrange("p (t h) -> p t h", h=HALF)
        g.sin = const("sin").rearrange("p (t h) -> p t h", h=HALF)
        g.layer = sb("layer", [P, 1])
        g.pages = sb("pages", [1, B * PAGES], I32)
        g.x = sb("x", [P, NT, D])
        g.ht = sb("ht", [P, KD, TOKP])
        g.wb = sb("wb", [P, 2, KD, 512])
        g.scratch_ab = nc.dram_tensor("scratch_ab", [B, 2 * H], FP32, kind="Internal").ap()
        g.scratch_w = nc.dram_tensor("scratch_w", [B, IH], FP32, kind="Internal").ap()
        g.scratch_kv = nc.dram_tensor("scratch_kv", [B, 2 * KV * HD], FP32, kind="Internal").ap()
        g.scratch_place = nc.dram_tensor("scratch_place", [B * SEGS * TOPK_S, 1], FP32, kind="Internal").ap()
        g.gates = nc.dram_tensor("gates", [P, NK, TOK], FP32, kind="Internal").ap()
        g.gathered = ctx.enter_context(nc.semaphore("gathered"))
        g.ps = ctx.enter_context(nc.psum_tensor("ps", [P, 8, 512], FP32))
        with stage(g, "loaded", "cleared") as (block, loaded, cleared):
            @block.sync
            def _(sp):
                sp.dma_start(consts[:], d["consts"]).then_inc(loaded, 16)
                sp.dma_start(g.pages[:], d["page_table"].rearrange("(a b) n -> a (b n)", a=1)).then_inc(loaded, 16)
                sp.dma_start(g.x[:, 0:TT, :], d["x_prompt"][0].rearrange("(t p) n -> p t n", p=P)).then_inc(loaded, 16)
                sp.wait_ge(cleared, 1)
                sp.dma_start(g.x[0:B, TT, :], d["x_sample"][:, 0, :]).then_inc(loaded, 16)
                sp.wait_ge(loaded, 64)

            @block.vector
            def _(dve):
                nc.vector.memset(g.layer[:], 0.0)
                nc.vector.memset(g.x[:, TT, :], 0.0).then_inc(cleared, 1)
        with nc.Fori(0, DEPTH) as l:
            layer(g, l, d)
        final(g, d)



_INS = ['x_prompt', 'x_sample', 'cache_k', 'cache_v', 'cache_kidx', 'state_conv', 'state_delta', 'cache_mem_k',
        'cache_mem_v', 'page_table', 'mem_prompt', 'norm_mix', 'w_in', 'dn_conv_w', 'dn_a_log', 'dn_dt_bias', 'dn_norm',
        'w_dn_up', 'w_att_up', 'w_o', 'norm_mem_q', 'norm_mem_kv', 'w_mq', 'w_mk', 'w_mv', 'w_mo', 'norm_ffn',
        'peer_wq', 'peer_keys', 'peer_u', 'peer_v', 'norm_final']
_OUTS = [('y_prompt', (1, T, D)), ('y_sample', (B, 1, D)),
         ('p_k', (1, T, DEPTH, KV, HD)), ('p_v', (1, T, DEPTH, KV, HD)), ('p_kidx', (1, T, DEPTH, ID)),
         ('p_conv', (DEPTH, 1, CW - 1, CONV)), ('p_delta', (DEPTH, 1, H, DK, DK)),
         ('p_mem_k', (DEPTH, 1, MEM, MH, MD)), ('p_mem_v', (DEPTH, 1, MEM, MH, MD)),
         ('s_k', (B, 1, DEPTH, KV, HD)), ('s_v', (B, 1, DEPTH, KV, HD)), ('s_kidx', (B, 1, DEPTH, ID)),
         ('s_conv', (DEPTH, B, CW - 1, CONV)), ('s_delta', (DEPTH, B, H, DK, DK))]


def kernel(**inputs):
    import concourse.bacc as _bacc
    from concourse.bass_utils import run_bass_kernel_spmd as _run

    nc = _bacc.Bacc("TRN2", target_bir_lowering=False, num_devices=1)
    arrays = {name: np.ascontiguousarray(inputs[name]) for name in _INS}
    arrays["consts"], where = host_constants()
    aps = {}
    for name, a in arrays.items():
        aps[name] = nc.dram_tensor(name, a.shape, mybir.dt.from_np(a.dtype), kind="ExternalInput").ap()
    for name, shape in _OUTS:
        aps[name] = nc.dram_tensor(name, shape, FP32, kind="ExternalOutput").ap()
    program(nc, aps, where)
    r = _run(nc, [arrays], core_ids=[0])
    return tuple(r.results[0][name] for name, _ in _OUTS)
```
